# Optimizing a Trainium2 kernel written in Bass

```python
import math
import jax
import jax.numpy as jnp
from jax import lax
import numpy as np

D_MODEL = 1024
BATCH = 1
SEQ = 256
DEPTH = 2
DEC_BATCH = 8
DEC_SEQ = 8
PAST_LEN = 2048
PAGE_SIZE = 128

RW_HEADS = 6
RW_HD = 64
RW_W = RW_HEADS * RW_HD
RW_DECAY_LORA = 64
RW_AAA_LORA = 64
RW_GATE_LORA = 128
RW_PROJ = 3 * RW_W + RW_DECAY_LORA + RW_AAA_LORA + RW_GATE_LORA
RW_GN_EPS = 64e-5
GLA_HEADS = 4
GLA_DK = 48
GLA_DV = 96
GLA_QK = GLA_HEADS * GLA_DK
GLA_W = GLA_HEADS * GLA_DV
GLA_GATE_LORA = 16
GLA_TAU = 16.0
GLA_CHUNK = 64
GLA_PROJ = 2 * GLA_QK + 2 * GLA_W + GLA_GATE_LORA
ML_HEADS = 4
ML_HD = 64
ML_W = ML_HEADS * ML_HD
ML_CONV = 4
ML_CHUNK = 64
ML_PROJ = 4 * ML_W + 2 * ML_HEADS
D_MIX = RW_W + GLA_W + ML_W
D_IN = RW_PROJ + GLA_PROJ + ML_PROJ
D_FF = 2752
ALPHA = (2 * DEPTH) ** 0.25
BETA = (8 * DEPTH) ** -0.25
LN_EPS = 1e-5
NORM_EPS = 1e-6

kernel_name = 'hybrid_rwkv7_gla_mlstm_decode_step'

def _f32(t):
    return t.astype(jnp.float32)

def _split(t, sizes):
    return jnp.split(t, np.cumsum(sizes)[:-1].tolist(), axis=-1)

def _standardize(t, eps):
    t = _f32(t)
    mu = jnp.mean(t, -1, keepdims=True)
    var = jnp.mean(jnp.square(t - mu), -1, keepdims=True)
    return (t - mu) * lax.rsqrt(var + eps)

def _layer_norm(t, g, b):
    return (_standardize(t, LN_EPS) * g + b).astype(t.dtype)

def _swiglu(h, wg, wu, wd):
    return (jax.nn.silu(h @ wg) * (h @ wu)) @ wd

def _rwkv7_mix(p, shift0, S0, mu, w0, w2, a0, a2, g2, k_k, k_a, r_k, gn_g, gn_b):
    B, T, _ = p.shape
    prev = jnp.concatenate([shift0[:, None].astype(p.dtype), p[:, :-1]], axis=1)
    xs = p + (prev - p) * mu
    r, k, v, wd, ad, gd = _split(xs, [RW_W, RW_W, RW_W, RW_DECAY_LORA, RW_AAA_LORA, RW_GATE_LORA])
    log_w = -jax.nn.softplus(-_f32(w0 + jnp.tanh(wd) @ w2)) - 0.5
    heads = lambda t: _f32(t).reshape(B, T, RW_HEADS, RW_HD)
    decay = heads(jnp.exp(-jnp.exp(log_w)))
    a = heads(jax.nn.sigmoid(_f32(a0 + ad @ a2)))
    g = _f32(jax.nn.sigmoid(gd) @ g2)
    r, k, v = heads(r), heads(k), heads(v)
    kk = k * k_k.reshape(RW_HEADS, RW_HD)
    kk = kk * lax.rsqrt(jnp.maximum(jnp.sum(kk * kk, -1, keepdims=True), 1e-24))
    k = k * (1.0 + (a - 1.0) * k_a.reshape(RW_HEADS, RW_HD))

    def step(S, inp):
        r_t, w_t, k_t, v_t, kk_t, a_t = inp
        sa = jnp.einsum('bhvk,bhk->bhv', S, -kk_t)
        S = (S * w_t[:, :, None, :] + sa[..., None] * (kk_t * a_t)[:, :, None, :]
             + v_t[..., None] * k_t[:, :, None, :])
        return S, jnp.einsum('bhvk,bhk->bhv', S, r_t)

    time_major = lambda t: jnp.moveaxis(t, 1, 0)
    S_T, y = lax.scan(step, _f32(S0), tuple(time_major(t) for t in (r, decay, k, v, kk, a)))
    y = jnp.moveaxis(y, 0, 1)
    y = _standardize(y, RW_GN_EPS) * gn_g.reshape(RW_HEADS, RW_HD) + gn_b.reshape(RW_HEADS, RW_HD)
    bonus = jnp.sum(r * k * r_k, -1, keepdims=True) * v
    out = (y + bonus).reshape(B, T, RW_W) * g
    return out.astype(p.dtype), p[:, -1], S_T

def _gla_mix(p, S0, a2, a_b, gn_g):
    B, T, _ = p.shape
    q, k, v, gdown, gr = _split(p, [GLA_QK, GLA_QK, GLA_W, GLA_GATE_LORA, GLA_W])
    log_a = jax.nn.log_sigmoid(_f32(gdown @ a2 + a_b)) / GLA_TAU
    qk_heads = lambda t: _f32(t).reshape(B, T, GLA_HEADS, GLA_DK)
    q = qk_heads(q) * GLA_DK ** -0.5
    k, log_a = qk_heads(k), qk_heads(log_a)
    v = _f32(v).reshape(B, T, GLA_HEADS, GLA_DV)
    L_ch = math.gcd(T, GLA_CHUNK)
    n_ch = T // L_ch
    causal = jnp.tril(jnp.ones((L_ch, L_ch), bool))
    chunks = lambda t: jnp.moveaxis(t.reshape(B, n_ch, L_ch, *t.shape[2:]), 1, 0)

    def body(S, inp):
        qc, kc, vc, lac = inp
        b = jnp.cumsum(lac, axis=1)
        q_dec = qc * jnp.exp(b)
        A = jnp.einsum('bihd,bjhd->bhij', q_dec, kc * jnp.exp(-b))
        A = jnp.where(causal, A, 0.0)
        o = jnp.einsum('bhij,bjhv->bihv', A, vc) + jnp.einsum('bihd,bhdv->bihv', q_dec, S)
        b_last = b[:, -1]
        S = S * jnp.exp(b_last)[..., None] + jnp.einsum(
            'bjhd,bjhv->bhdv', kc * jnp.exp(b_last[:, None] - b), vc)
        return S, o

    S_T, o = lax.scan(body, _f32(S0), tuple(chunks(t) for t in (q, k, v, log_a)))
    o = jnp.moveaxis(o, 0, 1).reshape(B, T, GLA_HEADS, GLA_DV)
    o = o * lax.rsqrt(jnp.mean(o * o, -1, keepdims=True) + NORM_EPS) * gn_g.reshape(GLA_HEADS, GLA_DV)
    out = o.reshape(B, T, GLA_W) * jax.nn.silu(_f32(gr))
    return out.astype(p.dtype), S_T

def _mlstm_mix(p, conv0, C0, n0, m0, conv_w, conv_b, i_b, f_b, gn_g):
    B, T, _ = p.shape
    qk_raw, v, o_raw, i_raw, f_raw = _split(p, [2 * ML_W, ML_W, ML_W, ML_HEADS, ML_HEADS])
    xpad = jnp.concatenate([conv0.astype(p.dtype), qk_raw], axis=1)
    conv = conv_b
    for j in range(ML_CONV):
        conv = conv + xpad[:, j:j + T] * conv_w[j]
    q, k = _split(jax.nn.silu(_f32(conv)), [ML_W, ML_W])
    heads = lambda t: _f32(t).reshape(B, T, ML_HEADS, ML_HD)
    q, k, v = heads(q), heads(k) * ML_HD ** -0.5, heads(v)
    i_pre = _f32(i_raw + i_b)
    log_f = jax.nn.log_sigmoid(_f32(f_raw + f_b))
    L_ch = math.gcd(T, ML_CHUNK)
    n_ch = T // L_ch
    causal = jnp.tril(jnp.ones((L_ch, L_ch), bool))
    chunks = lambda t: jnp.moveaxis(t.reshape(B, n_ch, L_ch, *t.shape[2:]), 1, 0)

    def body(carry, inp):
        Cs, ns, ms = carry
        qc, kc, vc, ic, fc = inp
        b = jnp.moveaxis(jnp.cumsum(fc, axis=1), 1, 2)
        ig = jnp.moveaxis(ic, 1, 2)
        D = jnp.where(causal, b[..., :, None] - b[..., None, :] + ig[..., None, :], -jnp.inf)
        inter = b + ms[..., None]
        m_t = jnp.maximum(inter, jnp.max(D, -1))
        Dw = jnp.exp(D - m_t[..., None])
        w_inter = jnp.exp(inter - m_t)
        s = jnp.einsum('bihd,bjhd->bhij', qc, kc) * Dw
        num = jnp.einsum('bhij,bjhv->bhiv', s, vc) + w_inter[..., None] * jnp.einsum('bhvd,bihd->bhiv', Cs, qc)
        den = jnp.sum(s, -1) + w_inter * jnp.einsum('bhd,bihd->bhi', ns, qc)
        hc = num / jnp.maximum(jnp.abs(den), jnp.exp(-m_t))[..., None]
        m_last = m_t[..., -1]
        w_state = jnp.exp(b[..., -1] + ms - m_last)
        w_j = jnp.exp(b[..., -1:] - b + ig - m_last[..., None])
        Cs = Cs * w_state[..., None, None] + jnp.einsum('bhj,bjhv,bjhd->bhvd', w_j, vc, kc)
        ns = ns * w_state[..., None] + jnp.einsum('bhj,bjhd->bhd', w_j, kc)
        return (Cs, ns, m_last), jnp.moveaxis(hc, 1, 2)

    (C_T, n_T, m_T), h = lax.scan(body, (_f32(C0), _f32(n0), _f32(m0)),
                                  tuple(chunks(t) for t in (q, k, v, i_pre, log_f)))
    h = jnp.moveaxis(h, 0, 1).reshape(B, T, ML_HEADS, ML_HD)
    h = _standardize(h, NORM_EPS) * gn_g.reshape(ML_HEADS, ML_HD)
    out = h.reshape(B, T, ML_W) * jax.nn.sigmoid(_f32(o_raw))
    return out.astype(p.dtype), xpad[:, T:], C_T, n_T, m_T

def _layer(x, c, st, prm):
    (ada_w, ada_b, ln_g, ln_b, ffn_wg, ffn_wu, ffn_wd, w_in, w_out,
     rw_mu, rw_w0, rw_w2, rw_a0, rw_a2, rw_g2, rw_k_k, rw_k_a, rw_r_k, rw_gn_g, rw_gn_b,
     gla_a2, gla_a_b, gla_gn_g, ml_conv_w, ml_conv_b, ml_i_b, ml_f_b, ml_gn_g) = prm
    st_rw, st_shift, st_gla, st_c, st_n, st_m, st_conv = st
    B = x.shape[0]
    mods = (jax.nn.silu(c) @ ada_w + ada_b).reshape(B, 3, 3, 1, D_MODEL)

    def modulate(t, i):
        return t * (1.0 + mods[:, i, 1]) + mods[:, i, 0]

    def residual(t, i, out, w):
        return _layer_norm(ALPHA * t + w * (1.0 + mods[:, i, 2]) * out, ln_g[i], ln_b[i])

    x = residual(x, 0, _swiglu(modulate(x, 0), ffn_wg[0], ffn_wu[0], ffn_wd[0]), 0.5)
    proj = modulate(x, 1) @ w_in
    p_rw, p_gla, p_ml = _split(proj, [RW_PROJ, GLA_PROJ, ML_PROJ])
    o_rw, new_shift, new_rw = _rwkv7_mix(p_rw, st_shift, st_rw, rw_mu, rw_w0, rw_w2, rw_a0, rw_a2, rw_g2,
                                         rw_k_k, rw_k_a, rw_r_k, rw_gn_g, rw_gn_b)
    o_gla, new_gla = _gla_mix(p_gla, st_gla, gla_a2, gla_a_b, gla_gn_g)
    o_ml, new_conv, new_c, new_n, new_m = _mlstm_mix(p_ml, st_conv, st_c, st_n, st_m, ml_conv_w, ml_conv_b,
                                                     ml_i_b, ml_f_b, ml_gn_g)
    mix = jnp.concatenate([o_rw, o_gla, o_ml], axis=-1) @ w_out
    x = residual(x, 1, mix, 1.0)
    x = residual(x, 2, _swiglu(modulate(x, 2), ffn_wg[1], ffn_wu[1], ffn_wd[1]), 0.5)
    return x, (new_rw, new_shift, new_gla, new_c, new_n, new_m, new_conv)

def _run_trunk(x, c, states, params):
    collected = [[] for _ in states]
    for l in range(DEPTH):
        x, new = _layer(x, c, tuple(s[l] for s in states), tuple(w[l] for w in params))
        for lst, s in zip(collected, new):
            lst.append(s)
    return x, tuple(jnp.stack(lst) for lst in collected)

def setup_inputs(seed: int = 0) -> dict:
    key = jax.random.key(seed)
    ks = iter(jax.random.split(key, 64))
    nrm = lambda shape, scale: scale * jax.random.normal(next(ks), shape, jnp.float32)
    uni = lambda shape, lo, hi: jax.random.uniform(next(ks), shape, jnp.float32, lo, hi)
    L = DEPTH
    return {
        'x_prompt': nrm((BATCH, SEQ, D_MODEL), 1.0),
        'x_sample': nrm((DEC_BATCH, DEC_SEQ, D_MODEL), 1.0),
        'c_prompt': nrm((BATCH, D_MODEL), 1.0),
        'c_sample': nrm((DEC_BATCH, D_MODEL), 1.0),
        'state_rwkv': nrm((L, DEC_BATCH, RW_HEADS, RW_HD, RW_HD), 0.1),
        'state_rwkv_shift': nrm((L, DEC_BATCH, RW_PROJ), 1.0),
        'state_gla': nrm((L, DEC_BATCH, GLA_HEADS, GLA_DK, GLA_DV), 0.1),
        'state_mlstm_c': nrm((L, DEC_BATCH, ML_HEADS, ML_HD, ML_HD), 0.1),
        'state_mlstm_n': nrm((L, DEC_BATCH, ML_HEADS, ML_HD), 0.5),
        'state_mlstm_m': nrm((L, DEC_BATCH, ML_HEADS), 1.0),
        'state_mlstm_conv': nrm((L, DEC_BATCH, ML_CONV - 1, 2 * ML_W), 1.0),
        'ada_w': nrm((L, D_MODEL, 9 * D_MODEL), 0.2 * D_MODEL ** -0.5),
        'ada_b': nrm((L, 9 * D_MODEL), 0.02),
        'ln_g': 1.0 + nrm((L, 3, D_MODEL), 0.02),
        'ln_b': nrm((L, 3, D_MODEL), 0.02),
        'ffn_wg': nrm((L, 2, D_MODEL, D_FF), D_MODEL ** -0.5),
        'ffn_wu': nrm((L, 2, D_MODEL, D_FF), D_MODEL ** -0.5),
        'ffn_wd': nrm((L, 2, D_FF, D_MODEL), BETA * D_FF ** -0.5),
        'w_in': nrm((L, D_MODEL, D_IN), D_MODEL ** -0.5),
        'w_out': nrm((L, D_MIX, D_MODEL), BETA * D_MIX ** -0.5),
        'rw_mu': uni((L, RW_PROJ), 0.0, 1.0),
        'rw_w0': uni((L, RW_W), -5.0, 1.0),
        'rw_w2': nrm((L, RW_DECAY_LORA, RW_W), 0.5 * RW_DECAY_LORA ** -0.5),
        'rw_a0': nrm((L, RW_W), 0.1),
        'rw_a2': nrm((L, RW_AAA_LORA, RW_W), RW_AAA_LORA ** -0.5),
        'rw_g2': nrm((L, RW_GATE_LORA, RW_W), RW_GATE_LORA ** -0.5),
        'rw_k_k': 0.85 + nrm((L, RW_W), 0.05),
        'rw_k_a': 1.0 + nrm((L, RW_W), 0.05),
        'rw_r_k': nrm((L, RW_HEADS, RW_HD), 0.1),
        'rw_gn_g': 1.0 + nrm((L, RW_W), 0.02),
        'rw_gn_b': nrm((L, RW_W), 0.02),
        'gla_a2': nrm((L, GLA_GATE_LORA, GLA_QK), GLA_GATE_LORA ** -0.5),
        'gla_a_b': 1.0 + nrm((L, GLA_QK), 0.5),
        'gla_gn_g': 1.0 + nrm((L, GLA_W), 0.02),
        'ml_conv_w': nrm((L, ML_CONV, 2 * ML_W), 0.5),
        'ml_conv_b': nrm((L, 2 * ML_W), 0.02),
        'ml_i_b': nrm((L, ML_HEADS), 0.1),
        'ml_f_b': uni((L, ML_HEADS), 3.0, 6.0),
        'ml_gn_g': 1.0 + nrm((L, ML_W), 0.02),
    }

def reference(x_prompt, x_sample, c_prompt, c_sample, state_rwkv, state_rwkv_shift, state_gla,
              state_mlstm_c, state_mlstm_n, state_mlstm_m, state_mlstm_conv,
              ada_w, ada_b, ln_g, ln_b, ffn_wg, ffn_wu, ffn_wd, w_in, w_out,
              rw_mu, rw_w0, rw_w2, rw_a0, rw_a2, rw_g2, rw_k_k, rw_k_a, rw_r_k, rw_gn_g, rw_gn_b,
              gla_a2, gla_a_b, gla_gn_g, ml_conv_w, ml_conv_b, ml_i_b, ml_f_b, ml_gn_g):
    params = (ada_w, ada_b, ln_g, ln_b, ffn_wg, ffn_wu, ffn_wd, w_in, w_out,
              rw_mu, rw_w0, rw_w2, rw_a0, rw_a2, rw_g2, rw_k_k, rw_k_a, rw_r_k, rw_gn_g, rw_gn_b,
              gla_a2, gla_a_b, gla_gn_g, ml_conv_w, ml_conv_b, ml_i_b, ml_f_b, ml_gn_g)
    Bp = x_prompt.shape[0]
    dt = x_prompt.dtype
    zero_states = (
        jnp.zeros((DEPTH, Bp, RW_HEADS, RW_HD, RW_HD), dt),
        jnp.zeros((DEPTH, Bp, RW_PROJ), dt),
        jnp.zeros((DEPTH, Bp, GLA_HEADS, GLA_DK, GLA_DV), dt),
        jnp.zeros((DEPTH, Bp, ML_HEADS, ML_HD, ML_HD), dt),
        jnp.zeros((DEPTH, Bp, ML_HEADS, ML_HD), dt),
        jnp.zeros((DEPTH, Bp, ML_HEADS), dt),
        jnp.zeros((DEPTH, Bp, ML_CONV - 1, 2 * ML_W), dt),
    )
    y_prompt, p_states = _run_trunk(x_prompt, c_prompt, zero_states, params)
    p_rwkv, p_rwkv_shift, p_gla, p_mlstm_c, p_mlstm_n, p_mlstm_m, p_mlstm_conv = p_states
    sample_states = (state_rwkv, state_rwkv_shift, state_gla, state_mlstm_c, state_mlstm_n,
                     state_mlstm_m, state_mlstm_conv)
    y_sample, s_states = _run_trunk(x_sample, c_sample, sample_states, params)
    s_rwkv, s_rwkv_shift, s_gla, s_mlstm_c, s_mlstm_n, s_mlstm_m, s_mlstm_conv = s_states
    return (y_prompt, y_sample, p_rwkv, p_rwkv_shift, p_gla, p_mlstm_c, p_mlstm_n, p_mlstm_m, p_mlstm_conv,
            s_rwkv, s_rwkv_shift, s_gla, s_mlstm_c, s_mlstm_n, s_mlstm_m, s_mlstm_conv)


_drawn_inputs = setup_inputs


def setup_inputs(seed=0):
    import zlib

    import numpy as np

    out = dict(_drawn_inputs(seed))
    spreads = {}
    factors = {'rw_gn_g': 8.0, 'rw_gn_b': 8.0, 'gla_gn_g': 8.0, 'ml_gn_g': 8.0}
    for name, (base, spread) in spreads.items():
        noise = np.random.default_rng([zlib.crc32(name.encode()), seed]).standard_normal(out[name].shape)
        drawn = base * np.exp(spread * noise) if base else spread * noise
        out[name] = jnp.asarray(drawn.astype(out[name].dtype))
    for name, factor in factors.items():
        out[name] = (out[name] * factor).astype(out[name].dtype)
    return out
```

```python
from contextlib import ExitStack

import numpy as np

import concourse.bass as bass
from concourse import mybir

F32 = mybir.dt.float32
F32R = mybir.dt.float32r
ALU = mybir.AluOpType
ACT = mybir.ActivationFunctionType

P = 128
D = 1024
DT = D // P
SEQ, DB, DS = 256, 8, 8
NS = DB * DS
TOK = SEQ + NS
DEPTH = 2
FF = 2752
FT = -(-FF // P)
ALPHA = (2 * DEPTH) ** 0.25
LN_EPS, GN_EPS, NORM_EPS = 1e-5, 64e-5, 1e-6
CH = 64
NCH = SEQ // CH

RW_H, HD = 6, 64
RW_W = RW_H * HD
RP = RW_H // 2
RW_PROJ = 3 * RW_W + 64 + 64 + 128
GH, DK, DV = 4, 48, 96
GP = GH // 2
GQK, GW = GH * DK, GH * DV
GLA_PROJ = 2 * GQK + 2 * GW + 16
MH = 4
MP = MH // 2
MW = MH * HD
CONV = 4
CW = SEQ + CONV - 1
CS = DS + CONV - 1
CN = CW + DB * CS

T_R, T_K, T_V, T_WA, T_G = 0, 3, 6, 9, 10
T_GQ, T_GK, T_GV, T_LOW, T_GR = 11, 13, 15, 18, 19
T_MQK, T_MV, T_MO = 23, 27, 29
NPROJ = 31
NRW = 11
MIXT = RP + GH + MP

_cols, _n = {}, 0
for _name, _k in (("ln_g", 24), ("ln_b", 24), ("ada_b", 72), ("mu", 11), ("w0", 3), ("a0", 3), ("k_k", 3),
                  ("k_a", 3), ("r_k", 3), ("gn_g", 3), ("gn_b", 3), ("gla_b", 2), ("gla_g", 4),
                  ("conv_w", 16), ("conv_b", 4), ("ml_g", 2), ("i_b", 1), ("f_b", 1)):
    _cols[_name] = _n
    _n += _k
PARC = _cols
NPAR = _n

_cols, _n = {}, 0
for _name, _k in (("ident", 128), ("ones64", 128), ("mean1024", 128), ("ones96", 128),
                  ("mask_p", 256), ("mask_s", 128), ("level", 6 * 128), ("level0t", 128), ("neg_p", 128),
                  ("neg_s", 64), ("seqmask", 8), ("reset", TOK), ("pairsel", 256), ("headsel", 512),
                  ("fold", 9), ("negreset", TOK)):
    _cols[_name] = _n
    _n += _k
CC = _cols
NCONST = _n

def layer_items():
    items = [("ada", 0, g) for g in range(6)]
    more = [("ada", i, g) for i in (1, 2) for g in range(6)]
    for f in range(FT):
        items.append(("up", 0, f))
        if f >= 1 and more:
            items.append(more.pop(0))
    items += [("down", 0, 0)]
    items += [("proj", t) for t in range(NPROJ)]
    items += [("mix",)]
    items += [("out",)]
    items += [("up", 1, f) for f in range(FT)]
    items += [("down", 1, 0)]
    return items


CHUNKS_OF = {"ada": 4, "up": 2, "down": DT * FT // 8, "proj": 1, "mix": 0, "out": DT * MIXT // 8}
ITEMS = layer_items()
NCHUNK = sum(CHUNKS_OF[i[0]] for i in ITEMS)

def chunk_starts():
    at, out = 0, []
    for item in ITEMS:
        out.append(at)
        at += CHUNKS_OF[item[0]]
    return out


RAW, SPL = 6, 3


class Arena:

    def __init__(self, nc, at):
        self.nc, self.at = nc, at

    def take(self, name, shape, dt=F32):
        size = 4 * int(np.prod(shape[1:]))
        t = self.nc.alloc_sbuf_tensor_at(name, shape, dt, offset=self.at)
        self.at += -(-size // 32) * 32
        assert self.at <= 229344, (name, self.at)
        return t


class Lane:

    def __init__(self, eng, steps):
        self.eng, self.steps, self.count, self.last = eng, steps, {}, None

    def do(self, ins, signal=None):
        s = self.steps if signal is None else signal
        self.count[s.num] = self.count.get(s.num, 0) + 1
        self.last = (s, self.count[s.num])
        ins.then_inc(s, 1)

    def settle(self):
        if self.last:
            self.eng.wait_ge(*self.last)
            self.last = None

    def mark(self, signal):
        self.settle()
        self.eng.sem_inc(signal, 1)
        self.count[signal.num] = self.count.get(signal.num, 0) + 1


class Banks:

    def __init__(self, pe, banks, full, free):
        self.pe, self.banks, self.full, self.free = pe, banks, full, free
        self.n, self.frees, self.freed = 0, 0, [None] * 4

    def open(self):
        if self.freed[self.n % 4]:
            self.pe.wait_ge(*self.freed[self.n % 4])
        return self.banks[self.n % 4]

    def close(self, ins=None, freed=None):
        if ins is not None:
            ins.then_inc(self.full, 1)
        if freed is None:
            self.frees += 1
            freed = (self.free, self.frees)
        self.freed[self.n % 4] = freed
        self.n += 1
        return freed


class RowTiles:

    def __init__(self, pe, order):
        self.pe, self.order, self.n = pe, order, 0

    def after(self, ins):
        ins.then_inc(self.order, 1)
        self.n += 1
        self.pe.wait_ge(self.order, self.n)


class Filled:

    def __init__(self, eng, banks, full):
        self.eng, self.banks, self.full, self.n, self.fulls = eng, banks, full, 0, 0

    def take(self, at=None):
        if at is None:
            self.fulls += 1
            at = (self.full, self.fulls)
        self.eng.wait_ge(*at)
        self.n += 1
        return self.banks[(self.n - 1) % 4]


def hybrid_trunk(nc, xT, cT, weights, par, consts, w2, g2, a2g, st_shift, st_rw, st_gla, st_c, st_n, st_m, st_conv,
                 yT, o_rwp, o_rws, o_shift, o_glap, o_glas, o_cp, o_cs, o_np, o_m, o_conv):
    with ExitStack() as ctx:
        sems = {}

        def sem(name):
            if name not in sems:
                sems[name] = ctx.enter_context(nc.semaphore(name))
            return sems[name]

        keep = Arena(nc, 16512)
        XT = keep.take("XT", [P, DT, TOK])
        raw = keep.take("raw", [P, RAW, 8, P])
        whi = keep.take("whi", [P, SPL, 8, P], F32R)
        wlo = keep.take("wlo", [P, SPL, 8, P], F32R)
        CON = keep.take("CON", [P, NCONST])
        PAR = keep.take("PAR", [P, NPAR])
        MODS = keep.take("MODS", [P, 72, 1 + DB])
        CS_T = keep.take("CS_T", [P, 8, P], F32R)
        crow = keep.take("crow", [P, 8, 1 + DB])
        W2 = keep.take("W2", [P, RW_W])
        G2 = keep.take("G2", [P, RW_W])
        OMK = keep.take("OMK", [P, RP])
        A2G = keep.take("A2G", [16, GP, P])
        MR = keep.take("MR", [64, 2, 512])
        XH = keep.take("XH", [P, 9, TOK], F32R)
        XL = keep.take("XL", [P, 9, TOK], F32R)
        base = keep.at
        ffn = Arena(nc, base)
        ZT = ffn.take("ZT", [P, DT, TOK])
        HH = ffn.take("HH", [P, FT, TOK], F32R)
        HL = ffn.take("HL", [P, FT, TOK], F32R)
        SG = ffn.take("SG", [P, 2, TOK])
        HF = ffn.take("HF", [P, 2, TOK])
        SQ = ffn.take("SQ", [P, DT, TOK])
        XM = SQ
        ZSUM = ffn.take("ZSUM", [P, TOK])
        QSUM = ffn.take("QSUM", [P, TOK])
        MN = ffn.take("MN", [P, TOK])
        VR = ffn.take("VR", [P, TOK])
        RS = ffn.take("RS", [P, TOK])
        gtmp = ffn.take("gtmp", [P, 2, NS])

        mix = Arena(nc, base)
        PJ = mix.take("PJ", [P, NPROJ, TOK])
        hold = mix.at
        rw = Arena(nc, hold)
        DF = rw.take("DF", [P, NRW, TOK])
        rw = Arena(nc, hold)
        AR = rw.take("AR", [P, 2, RP, TOK])
        BH = rw.take("BH", [P, RP, TOK])
        KH = rw.take("KH", [P, RP, TOK])
        BT = rw.take("BT", [P, RP, TOK])
        KT = rw.take("KT", [P, RP, TOK])
        SH = rw.take("SH", [P, NRW, DB])
        SHO = rw.take("SHO", [P, NRW, 1 + DB])
        tau0 = rw.at
        TK = rw.take("TK", [P, 4, RW_W])
        AM = rw.take("AM", [P, RW_H, 4, P])
        Tn = rw.take("Tn", [P, RW_H, P])
        Tt = rw.take("Tt", [P, RW_H, P])
        Yb = rw.take("Yb", [P, RW_H, P])
        RB = nc.alloc_sbuf_tensor_at("RB", [P, RW_W], F32, offset=rw.at - 4 * RW_H * P)
        UX = nc.alloc_sbuf_tensor_at("UX", [64, 2, 2, DB, HD], F32, offset=rw.at - 12 * RW_H * P)
        U0 = rw.take("U0", [P, RW_W])
        U = rw.take("U", [P, RW_W])
        WT = rw.take("WT", [P, RP, P])
        Z = rw.take("Z", [P, 2, RP, HD])
        ZP = rw.take("ZP", [P, RP, HD])
        PC = rw.take("PC", [P, RP, NCH + DB])
        GT = rw.take("GT", [P, RP, NS])
        pre = Arena(nc, tau0)
        TH = pre.take("TH", [64, TOK])
        SGD = pre.take("SGD", [P, TOK])
        SW = pre.take("SW", [P, RP, TOK])
        BB = pre.take("BB", [P, RP, TOK])
        BP = pre.take("BP", [P, RP, TOK])
        KKS = pre.take("KKS", [P, RP, TOK])
        EX = pre.take("EX", [P, 4, RP, TOK])
        post = Arena(nc, tau0)
        N2 = post.take("N2", [P, RP, TOK])
        N3 = post.take("N3", [P, RP, TOK])
        N4 = post.take("N4", [P, RP, TOK])
        BON, YT = PJ[:, T_R:T_R + RP], PJ[:, T_K:T_K + RP]
        xh_at, xl_at = base - 2 * 9 * TOK * 4, base - 9 * TOK * 4
        ZS = nc.alloc_sbuf_tensor_at("ZS", [P, RP, DB, HD], F32, offset=xh_at + 3 * TOK * 4)
        over = Arena(nc, xl_at)
        AA = over.take("AA", [P, RP, TOK])
        KK = over.take("KK", [P, RP, TOK])
        GG = over.take("GG", [P, RP, TOK])
        gl = Arena(nc, hold)
        GZ = gl.take("GZ", [P, GP, TOK])
        GA = gl.take("GA", [P, GP, TOK])
        GE = gl.take("GE", [P, GP, TOK])
        GB = gl.take("GB", [P, GP, TOK])
        QD = gl.take("QD", [P, GP, TOK])
        KI = gl.take("KI", [P, GP, TOK])
        KE = gl.take("KE", [P, GP, TOK])
        GX = gl.take("GX", [P, 3, GP, TOK])
        GN = nc.alloc_sbuf_tensor_at("GN", [P, GH, TOK], F32, offset=gl.at - 12 * GP * TOK)
        VG = gl.take("VG", [P, 3, GW])
        KET = gl.take("KET", [P, 3, GP * P])
        ATG = gl.take("ATG", [P, 3, GH, P])
        SP = gl.take("SP", [P, NCH + 1, GP, DV])
        S0 = gl.take("S0", [P, GP, DB, DV])
        GPC = gl.take("GPC", [P, GP, NCH + DB])
        OT = gl.take("OT", [P, GH, TOK])
        KX = nc.alloc_sbuf_tensor_at("KX", [64, DB, GP * P], F32, offset=base)
        ml = Arena(nc, hold)
        XP = ml.take("XP", [P, 4, CN])
        QW = nc.alloc_sbuf_tensor_at("QW", [P, MP, TOK], F32, offset=hold)
        EMB = nc.alloc_sbuf_tensor_at("EMB", [P, MP, TOK], F32, offset=hold + 4 * MP * TOK)
        at = ml.at
        CV = ml.take("CV", [P, 4, CN])
        HT = nc.alloc_sbuf_tensor_at("HT", [P, MP, TOK], F32, offset=at)
        DD = nc.alloc_sbuf_tensor_at("DD", [P, MP, TOK], F32, offset=at + 4 * MP * TOK)
        QK = ml.take("QK", [P, 4, TOK])
        IG, FZ, LF, BM, MM, ER, CR, D0, D1, E2, WJ = (
            ml.take(f"row{i}", [MH, TOK]) for i in range(11))
        M0 = ml.take("M0", [MH, DB])
        MO = ml.take("MO", [MH, 1 + DB])
        N0 = ml.take("N0", [P, MP, DB])
        NO = ml.take("NO", [P, MP, 1 + DB])
        SCV = ml.take("SCV", [P, 4, DB, CONV - 1])
        COV = ml.take("COV", [P, 4, 1 + DB, CONV - 1])
        COLS = ml.take("COLS", [P, 3, 8])
        MPC = ml.take("MPC", [P, MP, NCH + DB])
        DW = ml.take("DW", [P, MH, P])
        ST = ml.take("ST", [P, 3, MH, P])
        KW = ml.take("KW", [P, 3, MW])
        CP = ml.take("CP", [P, NCH + 1, MP, P])
        C0 = ml.take("C0", [P, MP, DB, P])
        VM = nc.alloc_sbuf_tensor_at("VM", [P, 3, MH, P], F32, offset=base)
        VX = nc.alloc_sbuf_tensor_at("VX", [64, MH, DB, HD], F32, offset=base + 4 * 3 * MH * P)
        assert 4 * (3 * MH * P + MH * DB * HD) <= 4 * 14 * TOK

        psV = [ctx.enter_context(nc.psum_tensor(f"psV{i}", [P, 512], F32)) for i in range(4)]
        psA = [ctx.enter_context(nc.psum_tensor(f"psA{i}", [P, 512], F32)) for i in range(4)]

        def con(name, k, rows=P, at=0):
            return CON[0:rows, CC[name] + at:CC[name] + at + k]

        def pcol(name, i=0, lo=0, hi=P):
            return PAR[lo:hi, PARC[name] + i:PARC[name] + i + 1]

        def s8(ap):
            return ap.rearrange("p (s t) -> p s t", t=DS)

        def t88(ap):
            return ap.rearrange("p a (s t) -> p a s t", t=DS)

        def whole(t):
            return t.rearrange("p a b -> p (a b)")

        loaded0 = sem("loaded0")
        with nc.Block() as block:
            @block.sync
            def _(sp):
                sp.dma_start(CON[:], consts).then_inc(loaded0, 16)
                sp.dma_start(crow[:], cT).then_inc(loaded0, 16)
                sp.dma_start(XT[:], xT).then_inc(loaded0, 16)
                sp.wait_ge(loaded0, 48)

            @block.gpsimd
            def _(pool):
                nc.gpsimd.memset(raw[:, 0], 0.0).then_inc(sem("zeroed"), 1)
                nc.gpsimd.memset(A2G[:], 0.0).then_inc(sem("zeroed"), 1)

            @block.scalar
            def _(act):
                act.wait_ge(loaded0, 48)
                nc.scalar.activation(crow[:], crow[:], ACT.Silu).then_inc(sem("c_silu"), 1)

            @block.vector
            def _(vec):
                vec.wait_ge(sem("c_silu"), 1)
                vec.wait_ge(sem("zeroed"), 2)
                nc.vector.tensor_copy(CS_T[:], raw[:, 0]).then_inc(sem("c_split"), 1)
                vec.wait_ge(sem("c_split"), 1)
                nc.vector.tensor_copy(CS_T[:, :, 0:9], crow[:]).then_inc(sem("c_split"), 1)
                vec.wait_ge(sem("c_split"), 2)
                nc.vector.tensor_tensor(CS_T[:, :, 32:41], crow[:], CS_T[:, :, 0:9].bitcast(F32),
                                        ALU.subtract).then_inc(sem("c_split"), 1)
                vec.wait_ge(sem("c_split"), 3)

        names = ["chunk_used", "row_tiles", "hi_done", "lo_done", "bankV_full", "bankV_free", "bankA_full", "bankA_free",
                 "steps_vec", "steps_act", "steps_pool", "x_split", "xm_sample", "gate_done", "hidden_done", "h_ready",
                 "z_ready", "sq_ready", "zsum_ready", "zn_ready", "x_ready", "mods_ready", "mrow_done",
                 "var_ready", "sd_ready", "proj_ready", "params", "stored"]
        for n in names:
            sem(n)
        loaded = [sem(f"loaded_{i}") for i in range(RAW)]
        chunk_used, hi_done, lo_done = sem("chunk_used"), sem("hi_done"), sem("lo_done")

        STARTS = chunk_starts()

        def product_end(d, kts):
            q = (d + 1) * kts
            return q % 8 == 0, q // 8

        def scol(i, j, dt, g=0, n=1):
            return MODS[:, i * 24 + j * 8 + dt, g:g + n]

        nc.all_engine_barrier()
        with nc.Fori(0, DEPTH) as layer:
            with nc.Block() as block:
                at_layer = bass.ds(layer, 1)

                def of_layer(ap):
                    return ap[at_layer].rearrange("l p a -> p (l a)")

                TAUS = ((0, 0, P), (1, P, P), (2, 2 * P, NS))

                def hp(h):
                    return h // 2, slice(64 * (h % 2), 64 * (h % 2) + 64)

                def EVEN_ODD(n):
                    return [*range(0, n, 2), *range(1, n, 2)]

                def rw_pe(pe, bV, bA, rt):
                    mm, tr = nc.tensor.matmul, nc.tensor.transpose

                    pe.wait_ge(sem("rw_tanh"), 1)
                    for j in range(RP):
                        bank = bA.open()
                        bA.close(mm(bank[:, 0:TOK], W2[0:64, j * P:(j + 1) * P], TH[:], start=True, stop=True),
                                 (sem("rw_low"), 3 * 0 + j + 1))
                    for j in range(RP):
                        bank = bA.open()
                        bA.close(mm(bank[:, 0:TOK], W2[64:128, j * P:(j + 1) * P], PJ[64:128, T_WA], start=True, stop=True),
                                 (sem("rw_low"), 3 + j + 1))
                    pe.wait_ge(sem("rw_gd"), 1)
                    for j in range(RP):
                        bank = bA.open()
                        bA.close(mm(bank[:, 0:TOK], G2[:, j * P:(j + 1) * P], SGD[:], start=True, stop=True),
                                 (sem("rw_low"), 6 + j + 1))
                    pe.wait_ge(sem("rw_sq"), 1)
                    for j in range(RP):
                        bank = bV.open()
                        bV.close(mm(bank[:, 0:TOK], con("ones64", P), KKS[:, j], start=True, stop=True))
                    pe.wait_ge(sem("rw_rkk"), 1)
                    for j in range(RP):
                        bank = bV.open()
                        bV.close(mm(bank[:, 0:TOK], con("ones64", P), BP[:, j], start=True, stop=True))
                    for tau, t0, w in TAUS:
                        if tau == 0:
                            pe.wait_ge(sem("rw_hats"), 1)
                        for q, src in enumerate((PJ[:, T_V:T_V + RP], BT[:], KT[:], AR[:, 0])):
                            bank = bA.open()
                            for j in range(RP):
                                ins = tr(bank[0:w, j * P:(j + 1) * P], src[:, j, t0:t0 + w], con("ident", P))
                            tok_freed = bA.close(ins)
                        for h in range(RW_H):
                            j, p = hp(h)
                            bank = bV.open()
                            for q, lhs in enumerate((BH, KH)):
                                ins = mm(bank[0:w, 0:4 * P].rearrange("p (q x t) -> p q x t", q=2, x=2)[:, q, :, 0:w],
                                         lhs[p, j, t0:t0 + w], AR[p, :, j, t0:t0 + w], start=True, stop=True)
                            am_freed = bV.close(ins)
                        pe.wait_ge(*am_freed)
                        def six(f, last=None):
                            for heads in (range(0, 4), range(4, 6)):
                                bank = bV.open()
                                for i, h in enumerate(heads):
                                    lhs, rhs = f(h)
                                    ins = mm(bank[0:w, i * P:i * P + w], lhs, rhs, start=True, stop=True)
                                freed = bV.close(ins, last if heads[0] == 4 else None)
                            return freed

                        f = six(lambda h: (AM[0:w, h, 0, 0:w], con("ident", w, rows=w)), (sem("rw_t0"), tau + 1))
                        pe.wait_ge(*f)
                        pe.wait_ge(sem("rw_tt"), tau + 1)
                        levels = 3 if tau == 2 else 6
                        for lev in range(1, levels):
                            f = six(lambda h: (AM[0:w, h, 0, 0:w], Tn[0:w, h, 0:w]))
                            pe.wait_ge(*f)
                            if lev < levels - 1:
                                six(lambda h: (Tt[0:w, h, 0:w], Yb[0:w, h, 0:w]))
                            f = six(lambda h: (Yb[0:w, h, 0:w], Tt[0:w, h, 0:w]))
                            pe.wait_ge(*f)
                        pe.wait_ge(*tok_freed)
                        bank = bA.open()
                        for h in range(RW_H):
                            ins = mm(bank[0:w, h * HD:(h + 1) * HD], AM[0:w, h, 2, 0:w], TK[0:w, 0, h * HD:(h + 1) * HD],
                                     start=True, stop=True)
                        f = bA.close(ins)
                        bank = bA.open()
                        for h in range(RW_H):
                            j, p = hp(h)
                            ins = mm(bank[p, j * P:j * P + w], TK[0:w, 3, h * HD:(h + 1) * HD], Tt[0:w, h, 0:w],
                                     start=True, stop=True)
                        bA.close(ins)
                        pe.wait_ge(*f)
                        bank = bA.open()
                        for h in range(RW_H):
                            ins = mm(bank[0:w, h * HD:(h + 1) * HD], Tt[0:w, h, 0:w], RB[0:w, h * HD:(h + 1) * HD],
                                     start=True, stop=True)
                        f = bA.close(ins)
                        pe.wait_ge(*f)
                        if tau < 2:
                            ybank = bA.open()
                            for half in range(2):
                                c, s = 2 * tau + half, slice(64 * half, 64 * half + 64)
                                bank = bV.open()
                                pe.wait_ge(sem("rw_z"), c + 1)
                                for h in EVEN_ODD(RW_H):
                                    j, p = hp(h)
                                    ins = mm(bank[s, h * HD:(h + 1) * HD], WT[p, j, s], Z[p, c % 2, j], start=True, stop=True)
                                    if h == RW_H - 2:
                                        rt.after(ins)
                                f = bV.close(ins)
                                for h in range(RW_H):
                                    j, p = hp(h)
                                    mm(ybank[p, j * P + 64 * half:j * P + 64 * half + 64], Z[p, c % 2, j],
                                       AR[p, 1, j, t0 + 64 * half:t0 + 64 * half + 64],
                                       start=(half == 0 and j == 0), stop=False, skip_group_check=True)
                                pe.wait_ge(*f)
                                bank = bV.open()
                                for h in range(RW_H):
                                    j, p = hp(h)
                                    mm(bank[p, j * HD:(j + 1) * HD], TK[s, 1, h * HD:(h + 1) * HD],
                                       U[s, h * HD:(h + 1) * HD], start=(j == 0), stop=False, skip_group_check=True)
                                for h in range(RW_H):
                                    j, p = hp(h)
                                    ins = mm(bank[p, j * HD:(j + 1) * HD], TK[s, 2, h * HD:(h + 1) * HD],
                                             TK[s, 0, h * HD:(h + 1) * HD], start=False, stop=True, skip_group_check=True)
                                bV.close(ins, (sem("rw_z"), c + 2))
                        else:
                            pe.wait_ge(sem("rw_state"), 16)
                            bank = bA.open()
                            for h in range(RW_H):
                                j, p = hp(h)
                                for s in range(DB):
                                    ins = mm(bank[p, j * NS + 8 * s:j * NS + 8 * s + 8], ZS[p, j, s],
                                             WT[p, j, 8 * s:8 * s + 8], start=True, stop=True)
                            f = bA.close(ins)
                            ybank = bA.open()
                            for h in range(RW_H):
                                j, p = hp(h)
                                for s in range(DB):
                                    ins = mm(ybank[p, j * P + 8 * s:j * P + 8 * s + 8], ZS[p, j, s],
                                             AR[p, 1, j, t0 + 8 * s:t0 + 8 * s + 8],
                                             start=(s == 0 and j == 0), stop=False, skip_group_check=True)
                            rt.after(ins)
                            pe.wait_ge(*f)
                            bank = bV.open()
                            for j in range(RP):
                                ins = tr(bank[0:NS, j * P:(j + 1) * P], GT[:, j], con("ident", P))
                            f = bV.close(ins)
                            pe.wait_ge(*f)
                        for h in range(RW_H):
                            j, p = hp(h)
                            mm(ybank[p, j * P:j * P + w], U[0:w, h * HD:(h + 1) * HD], AM[0:w, h, 1, 0:w],
                               start=False, stop=False, skip_group_check=True)
                            ins = mm(ybank[p, j * P:j * P + w], TK[0:w, 0, h * HD:(h + 1) * HD], AM[0:w, h, 3, 0:w],
                                     start=False, stop=True, skip_group_check=True)
                        f = bA.close(ins)
                        if tau == 2:
                            for j in range(RP):
                                bank = bV.open()
                                pe.wait_ge(sem("rw_spread_u"), j + 1)
                                pe.wait_ge(sem("rw_spread_v"), j + 1)
                                for h in (2 * j, 2 * j + 1):
                                    _, p = hp(h)
                                    mm(bank[p, :], TK[0:NS, 1, h * HD:(h + 1) * HD], UX[0:NS, 0, h % 2].rearrange("p s v -> p (s v)"),
                                       start=True, stop=False, skip_group_check=True)
                                    ins = mm(bank[p, :], TK[0:NS, 2, h * HD:(h + 1) * HD], UX[0:NS, 1, h % 2].rearrange("p s v -> p (s v)"),
                                             start=False, stop=True, skip_group_check=True)
                                bV.close(ins)
                    pe.wait_ge(*f)
                    for j in range(RP):
                        bank = bV.open()
                        bV.close(mm(bank[:, 0:TOK], con("ones64", P), YT[:, j], start=True, stop=True))
                    pe.wait_ge(sem("rw_gsq"), 1)
                    for j in range(RP):
                        bank = bV.open()
                        bV.close(mm(bank[:, 0:TOK], con("ones64", P), N3[:, j], start=True, stop=True))

                def rw_act(act, A, fA):
                    activation = nc.scalar.activation

                    act.wait_ge(sem("rw_xs"), 1)
                    A.do(activation(TH[:], PJ[0:64, T_WA], ACT.Tanh), sem("rw_tanh"))
                    act.wait_ge(sem("rw_xs"), 2)
                    A.do(activation(SGD[:], PJ[:, T_G], ACT.Sigmoid), sem("rw_gd"))
                    for j in range(RP):
                        bank = fA.take()
                        A.do(activation(SW[:, j], bank[:, 0:TOK], ACT.Sigmoid, bias=pcol("w0", j)), sem("rw_low"))
                    for j in range(RP):
                        bank = fA.take()
                        A.do(activation(AA[:, j], bank[:, 0:TOK], ACT.Sigmoid, bias=pcol("a0", j)), sem("rw_low"))
                    for j in range(RP):
                        bank = fA.take()
                        A.do(activation(GG[:, j], bank[:, 0:TOK], ACT.Copy), sem("rw_low"))
                    act.wait_ge(sem("rw_kk0"), 1)
                    A.do(activation(KKS[:], KK[:], ACT.Square), sem("rw_sq"))
                    act.wait_ge(sem("rw_n2"), 1)
                    A.do(activation(KKS[:], KKS[:], ACT.Sqrt), sem("rw_root"))
                    act.wait_ge(sem("rw_b"), 1)
                    A.do(activation(EX[:, 0], BB[:], ACT.Exp), sem("rw_exp"))
                    A.do(activation(EX[:, 1], BB[:], ACT.Exp, scale=-1.0), sem("rw_exp"))
                    act.wait_ge(sem("rw_b"), 2)
                    A.do(activation(EX[:, 2], BP[:], ACT.Exp), sem("rw_exp"))
                    act.wait_ge(sem("rw_be"), 1)
                    A.do(activation(EX[:, 3], SW[:], ACT.Exp), sem("rw_exp"))
                    for tau, t0, w in TAUS:
                        for q in range(4):
                            bank = fA.take()
                            if q == 0:
                                act.wait_ge(sem("rw_hats"), 1)
                            A.do(activation(TK[0:w, q], bank[0:w, 0:RW_W], ACT.Copy), sem("bankA_free"))
                        bank = fA.take()
                        A.do(activation(RB[0:w], bank[0:w, 0:RW_W], ACT.Copy), sem("bankA_free"))
                        bank = fA.take()
                        A.do(activation(WT[:, :, 0:w], bank[:, 0:RW_W].rearrange("p (j t) -> p j t", t=P)[:, :, 0:w], ACT.Copy),
                             sem("bankA_free"))
                        bank = fA.take()
                        A.do(activation(U0[0:w], bank[0:w, 0:RW_W], ACT.Copy), sem("bankA_free"))
                        if tau == 2:
                            bank = fA.take()
                            A.do(activation(GT[:], bank[:, 0:RP * NS].rearrange("p (j t) -> p j t", t=NS), ACT.Copy), sem("bankA_free"))
                        bank = fA.take()
                        A.do(activation(YT[:, :, t0:t0 + w], bank[:, 0:RW_W].rearrange("p (j t) -> p j t", t=P)[:, :, 0:w], ACT.Copy),
                             sem("bankA_free"))
                    act.wait_ge(sem("rw_yc"), 1)
                    A.do(activation(N3[:], N2[:], ACT.Square), sem("rw_gsq"))
                    act.wait_ge(sem("rw_gvar"), 1)
                    A.do(activation(N4[:], N4[:], ACT.Sqrt), sem("rw_gsd"))
                    act.wait_ge(sem("rw_m"), 1)
                    A.do(activation(XH[:, 0:RP], N2[:], ACT.Copy), sem("rw_mh"))

                def rw_vec(vec, V, fV):
                    tt, ts, stt = nc.vector.tensor_tensor, nc.vector.tensor_scalar, nc.vector.scalar_tensor_tensor
                    copy = nc.vector.tensor_copy
                    pj = PJ[:, 0:NRW]

                    vec.wait_ge(sem("proj_ready"), NPROJ)
                    vec.wait_ge(sem("rw_shift"), 16)
                    V.do(tt(DF[:, :, 1:SEQ], pj[:, :, 0:SEQ - 1], pj[:, :, 1:SEQ], ALU.subtract))
                    V.do(ts(DF[:, :, 0:1], pj[:, :, 0:1], -1.0, None, ALU.mult))
                    df, pp = t88(DF[:, :, SEQ:TOK]), t88(pj[:, :, SEQ:TOK])
                    V.do(tt(df[:, :, :, 1:DS], pp[:, :, :, 0:DS - 1], pp[:, :, :, 1:DS], ALU.subtract))
                    V.do(tt(df[:, :, :, 0], SH[:], pp[:, :, :, 0], ALU.subtract))
                    vec.wait_ge(sem("rw_shift_kept"), 2)
                    V.settle()
                    for i in (T_WA, T_G, 0, 1, 2, 3, 4, 5, 6, 7, 8):
                        V.do(stt(PJ[:, i], DF[:, i], pcol("mu", i), PJ[:, i], ALU.mult, ALU.add), sem("rw_xs"))
                    V.settle()
                    r, k, v = PJ[:, T_R:T_R + RP], PJ[:, T_K:T_K + RP], PJ[:, T_V:T_V + RP]
                    for j in range(RP):
                        V.do(ts(KK[:, j], k[:, j], pcol("k_k", j), None, ALU.mult))
                    V.mark(sem("rw_kk0"))
                    vec.wait_ge(sem("rw_low"), 3)
                    V.do(ts(SW[:], SW[:], -float(np.exp(-0.5)), None, ALU.mult))
                    V.settle()
                    for j in range(RP):
                        V.do(nc.vector.tensor_tensor_scan(BB[:, j], con("reset", TOK), SW[:, j], 0.0, ALU.mult, ALU.add))
                    V.mark(sem("rw_b"))
                    V.do(tt(BP[:], BB[:], SW[:], ALU.subtract), sem("rw_b"))
                    V.settle()
                    ends = BB[:, :, CH - 1:SEQ:CH]
                    V.do(tt(SW[:, :, 0:SEQ].rearrange("p a (c t) -> p a c t", t=CH), ends.unsqueeze(3).to_broadcast([P, RP, NCH, CH]),
                            BB[:, :, 0:SEQ].rearrange("p a (c t) -> p a c t", t=CH), ALU.subtract))
                    ends8 = BB[:, :, SEQ + DS - 1:TOK:DS]
                    V.do(tt(t88(SW[:, :, SEQ:TOK]), ends8.unsqueeze(3).to_broadcast([P, RP, DB, DS]), t88(BB[:, :, SEQ:TOK]), ALU.subtract))
                    V.mark(sem("rw_be"))
                    vec.wait_ge(sem("rw_low"), 6)
                    for j in range(RP):
                        V.do(ts(OMK[:, j:j + 1], pcol("k_a", j), -1.0, 1.0, ALU.mult, ALU.add))
                    V.settle()
                    for j in range(RP):
                        V.do(ts(BT[:, j], AA[:, j], pcol("k_a", j), OMK[:, j:j + 1], ALU.mult, ALU.add))
                    V.settle()
                    V.do(tt(k, k, BT[:], ALU.mult))
                    V.settle()
                    for j in range(RP):
                        bank = fV.take()
                        if j == 0:
                            vec.wait_ge(sem("rw_sq"), 1)
                        V.do(ts(KKS[:, j], bank[:, 0:TOK], 64.0, 1e-24, ALU.mult, ALU.max), sem("bankV_free"))
                    V.mark(sem("rw_n2"))
                    vec.wait_ge(sem("rw_root"), 1)
                    V.do(nc.vector.reciprocal(KKS[:], KKS[:]))
                    V.settle()
                    V.do(tt(KK[:], KK[:], KKS[:], ALU.mult))
                    V.settle()
                    V.do(tt(BT[:], KK[:], AA[:], ALU.mult))
                    vec.wait_ge(sem("rw_exp"), 4)
                    V.do(stt(AR[:, 0], KK[:], -1.0, EX[:, 2], ALU.mult, ALU.mult))
                    V.settle()
                    V.do(tt(BH[:], BT[:], EX[:, 1], ALU.mult))
                    V.settle()
                    V.do(tt(BT[:], BT[:], EX[:, 3], ALU.mult))
                    V.do(tt(KH[:], k, EX[:, 1], ALU.mult))
                    V.do(tt(AR[:, 1], r, EX[:, 0], ALU.mult))
                    V.do(tt(KT[:], k, EX[:, 3], ALU.mult))
                    V.do(copy(PC[:, :, 0:NCH], EX[:, 0, :, CH - 1:SEQ:CH]))
                    V.do(copy(PC[:, :, NCH:NCH + DB], EX[:, 0, :, SEQ + DS - 1:TOK:DS]))
                    for j in range(RP):
                        V.do(stt(BP[:, j], r[:, j], pcol("r_k", j), k[:, j], ALU.mult, ALU.mult))
                    V.mark(sem("rw_rkk"))
                    V.do(nc.vector.memset(Z[:, 0], 0.0), sem("rw_z"))
                    for j in range(RP):
                        bank = fV.take()
                        V.do(stt(BON[:, j], bank[:, 0:TOK], 64.0, v[:, j], ALU.mult, ALU.mult), sem("bankV_free"))
                    V.mark(sem("rw_hats"))
                    for tau, t0, w in TAUS:
                        mask = (con("mask_p", 2 * P) if tau < 2 else con("mask_s", P, rows=w)).rearrange("p (x t) -> p x t", x=2)
                        for h in range(RW_H):
                            bank = fV.take()
                            for q in range(2):
                                V.do(tt(AM[0:w, h, 2 * q:2 * q + 2, 0:w],
                                        bank[0:w, 2 * q * P:2 * (q + 1) * P].rearrange("p (x t) -> p x t", t=P)[:, :, 0:w],
                                        mask, ALU.mult), sem("bankV_free") if q else None)
                        V.mark(sem("rw_am"))

                        def six():
                            for heads in (slice(0, 4), slice(4, 6)):
                                bank = fV.take()
                                n = heads.stop - heads.start
                                yield heads, bank[0:w, 0:n * P].rearrange("p (h t) -> p h t", t=P)[:, :, 0:w], n

                        def level(i, n):
                            return CON[0:w, CC["level"] + i * P:CC["level"] + i * P + w].unsqueeze(1).to_broadcast([w, n, w])

                        for heads, bank, n in six():
                            V.do(tt(Tn[0:w, heads, 0:w], bank, level(0, n), ALU.mult), sem("bankV_free") if n == 4 else None)
                        V.settle()
                        V.do(tt(Tn[0:w, :, 0:w], Tn[0:w, :, 0:w],
                                con("ident", w, rows=w).unsqueeze(1).to_broadcast([w, RW_H, w]), ALU.add), sem("rw_t0"))
                        levels = 3 if tau == 2 else 6
                        for lev in range(1, levels):
                            for heads, bank, n in six():
                                V.do(tt(Yb[0:w, heads, 0:w], bank, level(lev, n), ALU.mult), sem("bankV_free"))
                            V.settle()
                            for T in ((Tn, Tt) if lev < levels - 1 else (Tt,)):
                                if T is Tt and lev == 1:
                                    vec.wait_ge(sem("rw_tt"), tau + 1)
                                for heads, bank, n in six():
                                    V.do(tt(T[0:w, heads, 0:w], bank, T[0:w, heads, 0:w], ALU.add), sem("bankV_free"))
                            V.settle()
                        if tau < 2:
                            for half in range(2):
                                c, s = 2 * tau + half, slice(64 * half, 64 * half + 64)
                                V.do(tt(ZP[:], Z[:, c % 2], PC[:, :, c:c + 1].to_broadcast([P, RP, HD]), ALU.mult))
                                bank = fV.take()
                                V.do(tt(U[s], bank[s, 0:RW_W], U0[s], ALU.add), sem("bankV_free"))
                                bank = fV.take()
                                V.settle()
                                V.do(tt(Z[:, (c + 1) % 2], bank[:, 0:RP * HD].rearrange("p (j v) -> p j v", v=HD), ZP[:], ALU.add),
                                     sem("rw_z"))
                                V.settle()
                        else:
                            bank = fV.take()
                            V.do(tt(U[0:NS], bank[0:NS, 0:RW_W], U0[0:NS], ALU.add), sem("bankV_free"))
                            V.mark(sem("rw_u8"))
                            seqmask = con("seqmask", DB, rows=NS).unsqueeze(2).to_broadcast([NS, DB, HD])
                            for j in range(RP):
                                for h in (2 * j, 2 * j + 1):
                                    V.do(tt(UX[0:NS, 0, h % 2], U[0:NS, h * HD:(h + 1) * HD].unsqueeze(1).to_broadcast([NS, DB, HD]),
                                            seqmask, ALU.mult), sem("rw_spread_u") if h % 2 else None)
                                V.do(tt(ZS[:, j], ZS[:, j], PC[:, j, NCH:NCH + DB].unsqueeze(2).to_broadcast([P, DB, HD]), ALU.mult))
                                bank = fV.take()
                                V.settle()
                                V.do(tt(ZS[:, j], bank[:].rearrange("p (s v) -> p s v", v=HD), ZS[:, j], ALU.add), sem("bankV_free"))
                                V.mark(sem("rw_zs"))
                    for j in range(RP):
                        bank = fV.take()
                        V.do(tt(N2[:, j], YT[:, j], bank[:, 0:TOK], ALU.subtract), sem("bankV_free"))
                    V.mark(sem("rw_yc"))
                    for j in range(RP):
                        bank = fV.take()
                        V.do(ts(N4[:, j], bank[:, 0:TOK], GN_EPS, None, ALU.add), sem("bankV_free"))
                    V.mark(sem("rw_gvar"))
                    vec.wait_ge(sem("rw_gsd"), 1)
                    V.do(nc.vector.reciprocal(N4[:], N4[:]))
                    V.settle()
                    V.do(tt(N2[:], N2[:], N4[:], ALU.mult))
                    V.settle()
                    for j in range(RP):
                        V.do(ts(N2[:, j], N2[:, j], pcol("gn_g", j), pcol("gn_b", j), ALU.mult, ALU.add))
                    V.settle()
                    V.do(tt(N2[:], N2[:], BON, ALU.add))
                    V.settle()
                    V.do(tt(N2[:], N2[:], GG[:], ALU.mult))
                    V.mark(sem("rw_m"))
                    vec.wait_ge(sem("rw_mh"), 1)
                    V.do(tt(XL[:, 0:RP], N2[:], XH[:, 0:RP].bitcast(F32), ALU.subtract))
                    for j in range(RP):
                        V.mark(sem("mixed"))

                def rw_pool(pool, G):
                    pool.wait_ge(sem("proj_ready"), NPROJ)
                    G.do(nc.gpsimd.tensor_copy(SHO[:, :, 0:1], PJ[:, 0:NRW, SEQ - 1:SEQ]), sem("rw_shift_kept"))
                    G.do(nc.gpsimd.tensor_copy(SHO[:, :, 1:1 + DB], PJ[:, 0:NRW, SEQ + DS - 1:TOK:DS]), sem("rw_shift_kept"))
                    for tau, t0, w in TAUS:
                        pool.wait_ge(sem("rw_am"), tau + 1)
                        lev = CON[0:w, CC["level0t"]:CC["level0t"] + w].unsqueeze(1).to_broadcast([w, RW_H, w])
                        G.do(nc.gpsimd.tensor_tensor(Tt[0:w, :, 0:w], AM[0:w, :, 0, 0:w], lev, ALU.mult))
                        G.settle()
                        G.do(nc.gpsimd.tensor_tensor(Tt[0:w, :, 0:w], Tt[0:w, :, 0:w],
                                                     con("ident", w, rows=w).unsqueeze(1).to_broadcast([w, RW_H, w]), ALU.add),
                             sem("rw_tt"))
                    seqmask = con("seqmask", DB, rows=NS).unsqueeze(2).to_broadcast([NS, DB, HD])
                    for j in range(RP):
                        pool.wait_ge(*((sem("rw_u8"), 1) if j == 0 else (sem("rw_zs"), j)))
                        for h in (2 * j, 2 * j + 1):
                            G.do(nc.gpsimd.tensor_tensor(UX[0:NS, 1, h % 2],
                                                         TK[0:NS, 0, h * HD:(h + 1) * HD].unsqueeze(1).to_broadcast([NS, DB, HD]),
                                                         seqmask, ALU.mult), sem("rw_spread_v") if h % 2 else None)

                def rw_sp(sp):
                    sp.wait_ge(sem("proj_ready"), NPROJ)
                    sp.dma_start(ZS[:].rearrange("p j s v -> p (j s v)"), of_layer(st_rw)).then_inc(sem("rw_state"), 16)
                    sp.wait_ge(sem("rw_shift_kept"), 2)
                    sp.dma_start(of_layer(o_shift), whole(SHO[:])).then_inc(sem("stored"), 16)
                    sp.wait_ge(sem("rw_z"), NCH + 1)
                    sp.dma_start(of_layer(o_rwp), Z[:, 0].rearrange("p j v -> p (j v)")).then_inc(sem("stored"), 16)
                    sp.wait_ge(sem("rw_zs"), RP)
                    sp.dma_start(of_layer(o_rws), ZS[:].rearrange("p j s v -> p (j s v)")).then_inc(sem("stored"), 16)

                def gl_pe(pe, bV, bA, rt):
                    mm, tr = nc.tensor.matmul, nc.tensor.transpose
                    pe.wait_ge(sem("gl_start"), 1)
                    for j in range(GP):
                        bank = bV.open()
                        bV.close(mm(bank[:, 0:TOK], A2G[:, j], PJ[0:16, T_LOW], start=True, stop=True))
                    for tau, t0, w in TAUS:
                        bank = bA.open()
                        for j in range(3):
                            ins = tr(bank[0:w, j * P:(j + 1) * P], PJ[:, T_GV + j, t0:t0 + w], con("ident", P))
                        bA.close(ins)
                    pe.wait_ge(sem("gl_hats"), 1)
                    for tau, t0, w in TAUS:
                        bank = bA.open()
                        for j in range(GP):
                            ins = tr(bank[0:w, j * P:(j + 1) * P], KE[:, j, t0:t0 + w], con("ident", P))
                        tok_freed = bA.close(ins)
                        bank = bV.open()
                        for h in EVEN_ODD(GH):
                            j, p = hp(h)
                            ins = mm(bank[0:w, h * P:h * P + w], KI[p, j, t0:t0 + w], QD[p, j, t0:t0 + w], start=True, stop=True)
                            if h == GH - 2:
                                rt.after(ins)
                        att_freed = bV.close(ins)
                    pe.wait_ge(*tok_freed)
                    for c in range(NCH):
                        s = slice(64 * (c % 2), 64 * (c % 2) + 64)
                        bank = bV.open()
                        for h in range(GH):
                            j, p = hp(h)
                            ins = mm(bank[p, j * DV:(j + 1) * DV], KET[s, c // 2, h * 64:(h + 1) * 64],
                                     VG[s, c // 2, h * DV:(h + 1) * DV], start=True, stop=True)
                        bV.close(ins, (sem("gl_state"), c + 2))
                    pe.wait_ge(sem("gl_state"), NCH + 1)
                    pe.wait_ge(*att_freed)
                    pe.wait_ge(sem("gl_state0"), 16)
                    for h in range(GH):
                        j, p = hp(h)
                        bank = bA.open()
                        for tau, t0, w in TAUS:
                            ins = mm(bank[0:DV, t0:t0 + w], VG[0:w, tau, h * DV:(h + 1) * DV], ATG[0:w, tau, h, 0:w],
                                     start=(tau == 0), stop=False, skip_group_check=True)
                        if h % 2:
                            rt.after(ins)
                        for c in range(1, NCH):
                            mm(bank[0:DV, c * CH:(c + 1) * CH], SP[p, c, j], QD[p, j, c * CH:(c + 1) * CH],
                               start=False, stop=False, skip_group_check=True)
                        for s in range(DB):
                            ins = mm(bank[0:DV, SEQ + DS * s:SEQ + DS * (s + 1)], S0[p, j, s],
                                     QD[p, j, SEQ + DS * s:SEQ + DS * (s + 1)], start=False, stop=True, skip_group_check=True)
                        bA.close(ins)
                    pe.wait_ge(sem("gl_kx"), 1)
                    for b in range(DB // 2):
                        bank = bV.open()
                        for s in (2 * b, 2 * b + 1):
                            for h in range(GH):
                                j, p = hp(h)
                                o = (s % 2) * GP * DV + j * DV
                                ins = mm(bank[p, o:o + DV], KX[:, s, h * 64:(h + 1) * 64], VG[0:NS, 2, h * DV:(h + 1) * DV],
                                         start=True, stop=True)
                        bV.close(ins)
                    pe.wait_ge(sem("gl_sq"), 1)
                    for h in range(GH):
                        bank = bV.open()
                        bV.close(mm(bank[0:DV, 0:TOK], CON[0:DV, CC["ones96"]:CC["ones96"] + DV], GN[0:DV, h], start=True, stop=True))

                def gl_act(act, A, fA):
                    activation = nc.scalar.activation
                    act.wait_ge(sem("gl_start"), 1)
                    for tau, t0, w in TAUS:
                        bank = fA.take()
                        A.do(activation(VG[0:w, tau], bank[0:w, 0:GW], ACT.Copy), sem("bankA_free"))
                    act.wait_ge(sem("gl_abs"), 1)
                    A.do(activation(GE[:], GA[:], ACT.Exp, scale=-1.0))
                    A.settle()
                    A.do(activation(GE[:], GE[:], ACT.Ln, bias=1.0), sem("gl_log"))
                    act.wait_ge(sem("gl_b"), 1)
                    A.do(activation(GX[:, 0], GB[:], ACT.Exp, scale=1.0 / 16), sem("gl_exp"))
                    A.do(activation(GX[:, 1], GB[:], ACT.Exp, scale=-1.0 / 16), sem("gl_exp"))
                    act.wait_ge(sem("gl_b"), 2)
                    A.do(activation(GX[:, 2], GE[:], ACT.Exp, scale=1.0 / 16), sem("gl_exp"))
                    for tau, t0, w in TAUS:
                        bank = fA.take()
                        A.do(activation(KET[0:w, tau], bank[0:w, 0:GP * P], ACT.Copy), sem("bankA_free"))
                    for h in range(GH):
                        bank = fA.take()
                        A.do(activation(OT[0:DV, h], bank[0:DV, 0:TOK], ACT.Copy), sem("bankA_free"))
                    A.mark(sem("gl_ot"))
                    A.do(activation(GN[0:DV], OT[0:DV], ACT.Square), sem("gl_sq"))
                    A.do(activation(PJ[0:DV, T_GR:T_GR + GH], PJ[0:DV, T_GR:T_GR + GH], ACT.Silu), sem("gl_gate"))
                    act.wait_ge(sem("gl_var"), 1)
                    A.do(activation(GN[0:DV], GN[0:DV], ACT.Sqrt), sem("gl_sd"))
                    act.wait_ge(sem("gl_m"), 1)
                    act.wait_ge(sem("gl_zero"), 1)
                    A.do(activation(XH[0:DV, RP:RP + GH], OT[0:DV], ACT.Copy), sem("gl_mh"))

                def gl_vec(vec, V, fV):
                    tt, ts, stt = nc.vector.tensor_tensor, nc.vector.tensor_scalar, nc.vector.scalar_tensor_tensor
                    copy = nc.vector.tensor_copy
                    vec.wait_ge(sem("stored"), 48)
                    V.mark(sem("gl_start"))
                    for j in range(GP):
                        bank = fV.take()
                        V.do(ts(GZ[:, j], bank[:, 0:TOK], pcol("gla_b", j), None, ALU.add), sem("bankV_free"))
                    V.settle()
                    V.do(stt(GA[:], GZ[:], -1.0, GZ[:], ALU.mult, ALU.max), sem("gl_abs"))
                    vec.wait_ge(sem("gl_log"), 1)
                    V.do(stt(GZ[:], GZ[:], 0.0, GE[:], ALU.min, ALU.subtract))
                    V.settle()
                    for j in range(GP):
                        V.do(nc.vector.tensor_tensor_scan(GB[:, j], con("reset", TOK), GZ[:, j], 0.0, ALU.mult, ALU.add))
                    V.mark(sem("gl_b"))
                    ends, ends8 = GB[:, :, CH - 1:SEQ:CH], GB[:, :, SEQ + DS - 1:TOK:DS]
                    V.do(tt(GE[:, :, 0:SEQ].rearrange("p a (c t) -> p a c t", t=CH), ends.unsqueeze(3).to_broadcast([P, GP, NCH, CH]),
                            GB[:, :, 0:SEQ].rearrange("p a (c t) -> p a c t", t=CH), ALU.subtract))
                    V.do(tt(t88(GE[:, :, SEQ:TOK]), ends8.unsqueeze(3).to_broadcast([P, GP, DB, DS]), t88(GB[:, :, SEQ:TOK]), ALU.subtract))
                    V.mark(sem("gl_b"))
                    vec.wait_ge(sem("gl_exp"), 3)
                    V.do(stt(QD[:], PJ[:, T_GQ:T_GQ + GP], DK ** -0.5, GX[:, 0], ALU.mult, ALU.mult))
                    V.do(tt(KI[:], PJ[:, T_GK:T_GK + GP], GX[:, 1], ALU.mult))
                    V.do(tt(KE[:], PJ[:, T_GK:T_GK + GP], GX[:, 2], ALU.mult))
                    V.do(copy(GPC[:, :, 0:NCH], GX[:, 0, :, CH - 1:SEQ:CH]))
                    V.do(copy(GPC[:, :, NCH:NCH + DB], GX[:, 0, :, SEQ + DS - 1:TOK:DS]))
                    V.do(nc.vector.memset(SP[:, 0], 0.0))
                    V.mark(sem("gl_hats"))
                    for tau, t0, w in TAUS:
                        bank = fV.take()
                        m = (con("mask_p", P, at=P) if tau < 2 else con("mask_s", NS, rows=w, at=NS))
                        V.do(tt(ATG[0:w, tau, :, 0:w], bank[0:w].rearrange("p (h t) -> p h t", t=P)[:, :, 0:w],
                                m.unsqueeze(1).to_broadcast([w, GH, w]), ALU.mult), sem("bankV_free"))
                    V.mark(sem("gl_state"))
                    for c in range(NCH):
                        bank = fV.take()
                        V.settle()
                        V.do(stt(SP[:, c + 1, 0], SP[:, c, 0], GPC[:, 0, c:c + 1], bank[:, 0:DV], ALU.mult, ALU.add))
                        V.do(stt(SP[:, c + 1, 1], SP[:, c, 1], GPC[:, 1, c:c + 1], bank[:, DV:2 * DV], ALU.mult, ALU.add),
                             sem("gl_state"))
                    vec.wait_ge(sem("gl_ot"), 1)
                    V.do(tt(S0[:], S0[:], GPC[:, :, NCH:NCH + DB].unsqueeze(3).to_broadcast([P, GP, DB, DV]), ALU.mult))
                    V.settle()
                    for b in range(DB // 2):
                        bank = fV.take()
                        V.do(tt(S0[:, :, 2 * b:2 * b + 2], bank[:, 0:4 * DV].rearrange("p (s j v) -> p j s v", s=2, j=2),
                                S0[:, :, 2 * b:2 * b + 2], ALU.add), sem("bankV_free"))
                    V.mark(sem("gl_out"))
                    for h in range(GH):
                        bank = fV.take()
                        V.do(ts(GN[0:DV, h], bank[0:DV, 0:TOK], NORM_EPS, None, ALU.add), sem("bankV_free"))
                    V.mark(sem("gl_var"))
                    vec.wait_ge(sem("gl_sd"), 1)
                    V.do(nc.vector.reciprocal(GN[0:DV], GN[0:DV]))
                    V.settle()
                    V.do(tt(OT[0:DV], OT[0:DV], GN[0:DV], ALU.mult))
                    V.settle()
                    for h in range(GH):
                        V.do(stt(OT[0:DV, h], OT[0:DV, h], pcol("gla_g", h, 0, DV), PJ[0:DV, T_GR + h], ALU.mult, ALU.mult))
                    V.mark(sem("gl_m"))
                    vec.wait_ge(sem("gl_mh"), 1)
                    V.do(tt(XL[0:DV, RP:RP + GH], OT[0:DV], XH[0:DV, RP:RP + GH].bitcast(F32), ALU.subtract))
                    for h in range(GH):
                        V.mark(sem("mixed"))

                def gl_pool(pool, G):
                    pool.wait_ge(sem("gl_start"), 1)
                    pool.wait_ge(sem("stored"), 48)
                    for x in (XH, XL):
                        G.do(nc.gpsimd.tensor_scalar(x[64:P, RP:RP + GH], CON[64:P, 0:GH * TOK].rearrange("p (h t) -> p h t", t=TOK),
                                                     0.0, None, ALU.mult))
                    G.mark(sem("gl_zero"))
                    pool.wait_ge(sem("gl_state"), NCH + 1)
                    G.do(nc.gpsimd.tensor_tensor(KX[:], KET[0:NS, 2].unsqueeze(1).to_broadcast([NS, DB, GP * P]),
                                                 con("seqmask", DB, rows=NS).unsqueeze(2).to_broadcast([NS, DB, GP * P]), ALU.mult),
                         sem("gl_kx"))

                def gl_sp(sp):
                    sp.wait_ge(sem("gl_start"), 1)
                    sp.dma_start(S0[:].rearrange("p j s v -> p (j s v)"), of_layer(st_gla)).then_inc(sem("gl_state0"), 16)
                    sp.wait_ge(sem("gl_state"), NCH + 1)
                    sp.dma_start(of_layer(o_glap), SP[:, NCH].rearrange("p j v -> p (j v)")).then_inc(sem("stored"), 16)
                    sp.wait_ge(sem("gl_out"), 1)
                    sp.dma_start(of_layer(o_glas), S0[:].rearrange("p j s v -> p (j s v)")).then_inc(sem("stored"), 16)

                def ml_pe(pe, bV, bA, rt):
                    mm, tr = nc.tensor.matmul, nc.tensor.transpose
                    pe.wait_ge(sem("ml_start"), 1)
                    for tau, t0, w in TAUS:
                        bank = bA.open()
                        for j in range(MP):
                            ins = tr(bank[0:w, j * P:(j + 1) * P], PJ[:, T_MV + j, t0:t0 + w], con("ident", P))
                        vm_freed = bA.close(ins)
                    pe.wait_ge(sem("ml_rows"), 1)
                    bank = bV.open()
                    for tau, t0, w in TAUS:
                        for q, row in enumerate((CR, WJ)):
                            o = tau * 8 + 4 * q
                            ins = tr(bank[0:w, o:o + 4], row[:, t0:t0 + w], con("ident", 4, rows=4))
                    bV.close(ins)
                    for j in range(MP):
                        bank = bV.open()
                        bV.close(mm(bank[:, 0:TOK], con("pairsel", P, rows=4, at=j * P), E2[:], start=True, stop=True))
                    for j in range(MP):
                        bank = bA.open()
                        bA.close(mm(bank[:, 0:TOK], con("pairsel", P, rows=4, at=j * P), D1[:], start=True, stop=True))
                    for tau, t0, w in TAUS:
                        bank = bV.open()
                        for h in range(MH):
                            ins = mm(bank[0:w, h * P:h * P + w], con("headsel", w, rows=4, at=h * P), ER[:, t0:t0 + w],
                                     start=True, stop=True)
                        bV.close(ins)
                        bank = bV.open()
                        for h in EVEN_ODD(MH):
                            j, p = hp(h)
                            ins = mm(bank[0:w, h * P:h * P + w], QK[p, 2 + j, t0:t0 + w], QK[p, j, t0:t0 + w], start=True, stop=True)
                            if h == MH - 2:
                                rt.after(ins)
                        bV.close(ins)
                        bank = bV.open()
                        for j in range(MP):
                            ins = tr(bank[0:w, j * P:(j + 1) * P], QK[:, 2 + j, t0:t0 + w], con("ident", P))
                        kw_freed = bV.close(ins)
                    pe.wait_ge(*vm_freed)
                    pe.wait_ge(*kw_freed)
                    pe.wait_ge(sem("ml_ones"), 1)
                    for c in range(NCH):
                        s = slice(64 * (c % 2), 64 * (c % 2) + 64)
                        bank = bV.open()
                        for h in range(MH):
                            j, p = hp(h)
                            ins = mm(bank[p, j * P:(j + 1) * P], KW[s, c // 2, h * HD:(h + 1) * HD], VM[s, c // 2, h],
                                     start=True, stop=True)
                        bV.close(ins, (sem("ml_state"), c + 2))
                    pe.wait_ge(sem("ml_state"), NCH + 1)
                    pe.wait_ge(sem("ml_c0"), 1)
                    for j in range(MP):
                        for part in (slice(64, 128), slice(0, 64)):
                            bank = bV.open()
                            for h in (2 * j, 2 * j + 1):
                                _, p = hp(h)
                                for tau, t0, w in TAUS:
                                    ins = mm(bank[p, t0:t0 + w], VM[0:w, tau, h, part], ST[0:w, tau, h, 0:w],
                                             start=(tau == 0), stop=False, skip_group_check=True)
                                if h % 2:
                                    rt.after(ins)
                                for c in range(1, NCH):
                                    mm(bank[p, c * CH:(c + 1) * CH], CP[p, c, j, part], QW[p, j, c * CH:(c + 1) * CH],
                                       start=False, stop=False, skip_group_check=True)
                                for s in range(DB):
                                    ins = mm(bank[p, SEQ + DS * s:SEQ + DS * (s + 1)], C0[p, j, s, part],
                                             QW[p, j, SEQ + DS * s:SEQ + DS * (s + 1)], start=False, stop=True, skip_group_check=True)
                            bV.close(ins)
                    pe.wait_ge(sem("ml_vx"), 1)
                    for j in range(MP):
                        bank = bV.open()
                        for h in (2 * j, 2 * j + 1):
                            _, p = hp(h)
                            ins = mm(bank[p, :], KW[0:NS, 2, h * HD:(h + 1) * HD], VX[:, h].rearrange("p s v -> p (s v)"),
                                     start=True, stop=True)
                        bV.close(ins)
                        bank = bV.open()
                        for h in (2 * j, 2 * j + 1):
                            _, p = hp(h)
                            ins = mm(bank[p, 0:DB], KW[0:NS, 2, h * HD:(h + 1) * HD], con("seqmask", DB, rows=NS), start=True, stop=True)
                        bV.close(ins)
                    pe.wait_ge(sem("ml_h"), 1)
                    for j in range(MP):
                        bank = bV.open()
                        bV.close(mm(bank[:, 0:TOK], con("ones64", P), HT[:, j], start=True, stop=True))
                    pe.wait_ge(sem("ml_sq"), 1)
                    for j in range(MP):
                        bank = bV.open()
                        bV.close(mm(bank[:, 0:TOK], con("ones64", P), DD[:, j], start=True, stop=True))

                def ml_act(act, A, fA):
                    activation = nc.scalar.activation
                    act.wait_ge(sem("ml_start"), 1)
                    qk = PJ[:, T_MQK:T_MQK + 4]
                    A.do(activation(XP[:, :, CONV - 1:CW], qk[:, :, 0:SEQ], ACT.Copy))
                    xs = XP[:, :, CW:CN].rearrange("p a (s t) -> p a s t", t=CS)
                    for i in range(4):
                        A.do(activation(xs[:, i, :, CONV - 1:CS], s8(qk[:, i, SEQ:TOK]), ACT.Copy))
                    act.wait_ge(sem("ml_conv0"), 16)
                    for i in range(4):
                        A.do(activation(xs[:, i, :, 0:CONV - 1], SCV[:, i], ACT.Copy))
                    A.mark(sem("ml_xp"))
                    for tau, t0, w in TAUS:
                        bank = fA.take()
                        A.do(activation(VM[0:w, tau, :, 0:HD], bank[0:w, 0:MW].rearrange("p (h v) -> p h v", v=HD), ACT.Copy),
                             sem("bankA_free"))
                    act.wait_ge(sem("ml_f"), 1)
                    A.do(activation(D0[:], D0[:], ACT.Exp, scale=-1.0))
                    A.settle()
                    A.do(activation(D0[:], D0[:], ACT.Ln, bias=1.0), sem("ml_log"))
                    act.wait_ge(sem("ml_m"), 1)
                    A.do(activation(E2[:], E2[:], ACT.Exp))
                    A.do(activation(WJ[:], WJ[:], ACT.Exp))
                    A.do(activation(D1[:], MM[:], ACT.Exp, scale=-1.0))
                    act.wait_ge(sem("ml_conv"), 1)
                    A.do(activation(QK[:, :, 0:SEQ], CV[:, :, 0:SEQ], ACT.Silu))
                    for i in range(4):
                        A.do(activation(s8(QK[:, i, SEQ:TOK]),
                                        CV[:, i, CW:CN].rearrange("p (s t) -> p s t", t=CS)[:, :, 0:DS], ACT.Silu))
                    A.mark(sem("ml_qk"))
                    for j in range(MP):
                        bank = fA.take()
                        A.do(activation(EMB[:, j], bank[:, 0:TOK], ACT.Copy), sem("bankA_free"))
                    A.mark(sem("ml_emb"))
                    for tau, t0, w in TAUS:
                        act.wait_ge(sem("ml_arg"), tau + 1)
                        A.do(activation(DW[0:w, :, 0:w], DW[0:w, :, 0:w], ACT.Exp), sem("ml_dw"))
                    A.do(activation(PJ[:, T_MO:T_MO + MP], PJ[:, T_MO:T_MO + MP], ACT.Sigmoid), sem("ml_gate"))
                    act.wait_ge(sem("ml_hc"), 1)
                    A.do(activation(DD[:], HT[:], ACT.Square), sem("ml_sq"))
                    act.wait_ge(sem("ml_var"), 1)
                    A.do(activation(DD[:], DD[:], ACT.Sqrt), sem("ml_sd"))
                    act.wait_ge(sem("ml_mix"), 1)
                    A.do(activation(XH[:, RP + GH:MIXT], HT[:], ACT.Copy), sem("ml_mh"))

                def ml_vec(vec, V, fV):
                    tt, ts, stt = nc.vector.tensor_tensor, nc.vector.tensor_scalar, nc.vector.scalar_tensor_tensor
                    copy = nc.vector.tensor_copy
                    vec.wait_ge(sem("stored"), 80)
                    V.do(nc.vector.memset(XP[:, :, 0:CONV - 1], 0.0))
                    V.do(nc.vector.memset(CP[:, 0], 0.0))
                    V.mark(sem("ml_start"))
                    V.do(ts(IG[:], PJ[32:36, T_LOW], pcol("i_b", 0, 32, 36), None, ALU.add))
                    V.do(ts(FZ[:], PJ[64:68, T_LOW], pcol("f_b", 0, 64, 68), None, ALU.add))
                    V.settle()
                    V.do(stt(D0[:], FZ[:], -1.0, FZ[:], ALU.mult, ALU.max), sem("ml_f"))
                    vec.wait_ge(sem("ml_log"), 1)
                    V.do(stt(LF[:], FZ[:], 0.0, D0[:], ALU.min, ALU.subtract))
                    V.do(copy(D1[:], IG[:]))
                    V.settle()
                    first = slice(SEQ, TOK, DS)
                    vec.wait_ge(sem("ml_m0"), 16)
                    V.do(tt(MO[:, 1:1 + DB], M0[:], LF[:, first], ALU.add))
                    V.do(tt(D0[:], LF[:], con("negreset", TOK, rows=4), ALU.add))
                    V.do(nc.vector.tensor_tensor_scan(BM[:], con("reset", TOK, rows=4), LF[:], 0.0, ALU.mult, ALU.add))
                    V.settle()
                    V.do(tt(D1[:, first], MO[:, 1:1 + DB], IG[:, first], ALU.max))
                    V.settle()
                    V.do(nc.vector.tensor_tensor_scan(MM[:], D0[:], D1[:], 0.0, ALU.add, ALU.max))
                    V.do(tt(CR[:], IG[:], BM[:], ALU.subtract))
                    V.settle()
                    V.do(tt(ER[:], BM[:], MM[:], ALU.subtract))
                    V.do(copy(MO[:, 0:1], MM[:, SEQ - 1:SEQ]))
                    V.do(copy(MO[:, 1:1 + DB], MM[:, SEQ + DS - 1:TOK:DS]))
                    V.settle()
                    def c64(ap, n):
                        return ap.rearrange("p (c t) -> p c t", t=CH if n != DB else DS)
                    V.do(copy(E2[:, 0:CH], ER[:, 0:CH]))
                    V.do(tt(c64(E2[:, CH:SEQ], 3), c64(ER[:, CH:SEQ], 3),
                            MM[:, CH - 1:SEQ - 1:CH].unsqueeze(2).to_broadcast([MH, NCH - 1, CH]), ALU.add))
                    V.do(tt(s8(E2[:, SEQ:TOK]), s8(ER[:, SEQ:TOK]), M0[:].unsqueeze(2).to_broadcast([MH, DB, DS]), ALU.add))
                    V.do(tt(c64(WJ[:, 0:SEQ], 4), c64(CR[:, 0:SEQ], 4),
                            ER[:, CH - 1:SEQ:CH].unsqueeze(2).to_broadcast([MH, NCH, CH]), ALU.add))
                    V.do(tt(s8(WJ[:, SEQ:TOK]), s8(CR[:, SEQ:TOK]), ER[:, SEQ + DS - 1:TOK:DS].unsqueeze(2).to_broadcast([MH, DB, DS]), ALU.add))
                    V.mark(sem("ml_m"))
                    vec.wait_ge(sem("ml_xp"), 1)
                    n = CN - CONV + 1
                    for i in range(4):
                        V.do(ts(CV[:, i, 0:n], XP[:, i, 3:3 + n], pcol("conv_w", 12 + i), pcol("conv_b", i), ALU.mult, ALU.add))
                    for tap in (2, 1, 0):
                        V.settle()
                        for i in range(4):
                            V.do(stt(CV[:, i, 0:n], XP[:, i, tap:tap + n], pcol("conv_w", 4 * tap + i), CV[:, i, 0:n],
                                     ALU.mult, ALU.add))
                    V.do(copy(COV[:, :, 0], XP[:, :, SEQ:CW]))
                    for i in range(4):
                        V.do(copy(COV[:, i, 1:1 + DB], XP[:, i, CW:CN].rearrange("p (s t) -> p s t", t=CS)[:, :, DS:CS]))
                    V.mark(sem("ml_conv"))
                    vec.wait_ge(sem("ml_qk"), 1)
                    V.do(ts(QK[:, 2:4], QK[:, 2:4], HD ** -0.5, None, ALU.mult))
                    V.mark(sem("ml_rows"))
                    bank = fV.take()
                    V.do(copy(COLS[:, 0:2], bank[:, 0:16].rearrange("p (a b) -> p a b", b=8)))
                    V.do(copy(COLS[0:NS, 2], bank[0:NS, 16:24]), sem("bankV_free"))
                    for j in range(MP):
                        bank = fV.take()
                        V.do(copy(MPC[:, j, 0:NCH], bank[:, CH - 1:SEQ:CH]))
                        V.do(copy(MPC[:, j, NCH:NCH + DB], bank[:, SEQ + DS - 1:TOK:DS]))
                        V.do(tt(QW[:, j], bank[:, 0:TOK], QK[:, j], ALU.mult), sem("bankV_free"))
                    V.settle()
                    for tau, t0, w in TAUS:
                        bank = fV.take()
                        neg = con("neg_p", P) if tau < 2 else con("neg_s", NS, rows=w)
                        for h in range(MH):
                            V.do(stt(DW[0:w, h, 0:w], bank[0:w, h * P:h * P + w], COLS[0:w, tau, h:h + 1], neg, ALU.add, ALU.add),
                                 sem("bankV_free") if h == 3 else None)
                        V.mark(sem("ml_arg"))
                        bank = fV.take()
                        vec.wait_ge(sem("ml_dw"), tau + 1)
                        V.do(tt(ST[0:w, tau, :, 0:w], bank[0:w].rearrange("p (h t) -> p h t", t=P)[:, :, 0:w], DW[0:w, :, 0:w], ALU.mult),
                             sem("bankV_free"))
                        bank = fV.take()
                        V.settle()
                        V.do(tt(KW[0:w, tau].rearrange("p (h d) -> p h d", d=HD), bank[0:w, 0:MW].rearrange("p (h d) -> p h d", d=HD),
                                COLS[0:w, tau, 4:8].unsqueeze(2).to_broadcast([w, MH, HD]), ALU.mult), sem("bankV_free"))
                    vec.wait_ge(sem("ml_c00"), 32)
                    V.do(copy(C0[:, :, :, HD:P].rearrange("p j s v -> p (j s) v"),
                              N0[:].rearrange("p j s -> p (j s)").unsqueeze(2).to_broadcast([P, MP * DB, HD])))
                    V.mark(sem("ml_c0"))
                    V.mark(sem("ml_state"))
                    for c in range(NCH):
                        bank = fV.take()
                        V.settle()
                        for j in range(MP):
                            V.do(stt(CP[:, c + 1, j], CP[:, c, j], MPC[:, j, c:c + 1], bank[:, j * P:(j + 1) * P], ALU.mult, ALU.add),
                                 sem("ml_state") if j == 1 else None)
                    V.settle()
                    V.do(copy(NO[:, :, 0:1], CP[:, NCH, :, HD:HD + 1]))
                    V.mark(sem("ml_prompt"))
                    vec.wait_ge(sem("ml_emb"), 1)
                    for j in range(MP):
                        bank = fV.take()
                        V.do(stt(DD[:, j], bank[:, 0:TOK], -1.0, EMB[:, j], ALU.mult, ALU.max))
                        V.settle()
                        V.do(tt(DD[:, j], bank[:, 0:TOK], DD[:, j], ALU.max), sem("bankV_free"))
                        V.settle()
                        V.do(nc.vector.reciprocal(DD[:, j], DD[:, j]))
                        bank = fV.take()
                        V.settle()
                        V.do(tt(HT[:, j], bank[:, 0:TOK], DD[:, j], ALU.mult), sem("bankV_free"))
                    V.mark(sem("ml_h"))
                    for j in range(MP):
                        V.do(tt(C0[:, j, :, 0:HD + 1], C0[:, j, :, 0:HD + 1],
                                MPC[:, j, NCH:NCH + DB].unsqueeze(2).to_broadcast([P, DB, HD + 1]), ALU.mult))
                    V.settle()
                    for j in range(MP):
                        bank = fV.take()
                        V.do(tt(C0[:, j, :, 0:HD], bank[:].rearrange("p (s v) -> p s v", v=HD), C0[:, j, :, 0:HD], ALU.add), sem("bankV_free"))
                        bank = fV.take()
                        V.do(tt(NO[:, j, 1:1 + DB], bank[:, 0:DB], C0[:, j, :, HD], ALU.add), sem("bankV_free"))
                    V.mark(sem("ml_out"))
                    for j in range(MP):
                        bank = fV.take()
                        V.do(tt(HT[:, j], HT[:, j], bank[:, 0:TOK], ALU.subtract), sem("bankV_free"))
                    V.mark(sem("ml_hc"))
                    for j in range(MP):
                        bank = fV.take()
                        V.do(ts(DD[:, j], bank[:, 0:TOK], NORM_EPS, None, ALU.add), sem("bankV_free"))
                    V.mark(sem("ml_var"))
                    vec.wait_ge(sem("ml_sd"), 1)
                    V.do(nc.vector.reciprocal(DD[:], DD[:]))
                    V.settle()
                    V.do(tt(HT[:], HT[:], DD[:], ALU.mult))
                    vec.wait_ge(sem("ml_gate"), 1)
                    V.settle()
                    for j in range(MP):
                        V.do(stt(HT[:, j], HT[:, j], pcol("ml_g", j), PJ[:, T_MO + j], ALU.mult, ALU.mult))
                    V.mark(sem("ml_mix"))
                    vec.wait_ge(sem("ml_mh"), 1)
                    V.do(tt(XL[:, RP + GH:MIXT], HT[:], XH[:, RP + GH:MIXT].bitcast(F32), ALU.subtract))
                    for j in range(MP):
                        V.mark(sem("mixed"))

                def ml_pool(pool, G):
                    pool.wait_ge(sem("ml_start"), 1)
                    G.do(nc.gpsimd.memset(VM[:, :, :, HD:P], 1.0), sem("ml_ones"))
                    pool.wait_ge(sem("ml_state"), 2)
                    for h in range(MH):
                        G.do(nc.gpsimd.tensor_tensor(VX[:, h], VM[0:NS, 2, h, 0:HD].unsqueeze(1).to_broadcast([NS, DB, HD]),
                                                     con("seqmask", DB, rows=NS).unsqueeze(2).to_broadcast([NS, DB, HD]), ALU.mult))
                    G.mark(sem("ml_vx"))

                def ml_sp(sp):
                    sp.wait_ge(sem("ml_start"), 1)
                    sp.dma_start(SCV[:].rearrange("p a s t -> p (a s t)"), of_layer(st_conv)).then_inc(sem("ml_conv0"), 16)
                    sp.dma_start(M0[:], of_layer(st_m)).then_inc(sem("ml_m0"), 16)
                    sp.dma_start(C0[:, :, :, 0:HD].rearrange("p j s v -> p (j s) v"),
                                 st_c[at_layer].rearrange("l p (a v) -> p (l a) v", v=HD)).then_inc(sem("ml_c00"), 16)
                    sp.dma_start(N0[:].rearrange("p j s -> p (j s)"), of_layer(st_n)).then_inc(sem("ml_c00"), 16)
                    sp.wait_ge(sem("ml_m"), 1)
                    sp.dma_start(of_layer(o_m), MO[:]).then_inc(sem("stored"), 16)
                    sp.wait_ge(sem("ml_conv"), 1)
                    sp.dma_start(of_layer(o_conv), COV[:].rearrange("p a s t -> p (a s t)")).then_inc(sem("stored"), 16)
                    sp.wait_ge(sem("ml_prompt"), 1)
                    sp.dma_start(of_layer(o_cp).rearrange("p (j v) -> p j v", v=HD), CP[:, NCH, :, 0:HD]).then_inc(sem("stored"), 16)
                    sp.wait_ge(sem("ml_out"), 1)
                    sp.dma_start(of_layer(o_cs).rearrange("p (a v) -> p a v", v=HD),
                                 C0[:, :, :, 0:HD].rearrange("p j s v -> p (j s) v")).then_inc(sem("stored"), 16)
                    sp.dma_start(of_layer(o_np), NO[:].rearrange("p j s -> p (j s)")).then_inc(sem("stored"), 16)

                def mix_pe(pe, bV, bA, rt):
                    rw_pe(pe, bV, bA, rt)
                    gl_pe(pe, bV, bA, rt)
                    ml_pe(pe, bV, bA, rt)

                def mix_act(act, A, fA):
                    rw_act(act, A, fA)
                    gl_act(act, A, fA)
                    ml_act(act, A, fA)

                def mix_vec(vec, V, fV):
                    rw_vec(vec, V, fV)
                    gl_vec(vec, V, fV)
                    ml_vec(vec, V, fV)

                def mix_sp(sp):
                    rw_sp(sp)
                    gl_sp(sp)
                    ml_sp(sp)

                def mix_pool(pool, G):
                    rw_pool(pool, G)
                    gl_pool(pool, G)
                    ml_pool(pool, G)

                @block.sync
                def _(sp):
                    sp.dma_start(PAR[:], of_layer(par)).then_inc(sem("params"), 16)
                    sp.dma_start(W2[:], of_layer(w2)).then_inc(sem("params"), 16)
                    sp.dma_start(G2[:], of_layer(g2)).then_inc(sem("params"), 16)
                    sp.dma_start(whole(A2G[:]), of_layer(a2g)).then_inc(sem("params"), 16)
                    for n in range(NCHUNK):
                        if n == STARTS[ITEMS.index(("proj", NRW))]:
                            sp.wait_ge(sem("proj_ready"), 1)
                            sp.dma_start(whole(SH[:]), of_layer(st_shift)).then_inc(sem("rw_shift"), 16)
                        if n == STARTS[ITEMS.index(("out",))] + SPL + RAW:
                            mix_sp(sp)
                        if n >= RAW:
                            sp.wait_ge(lo_done, n - RAW + 1)
                        sp.dma_start(whole(raw[:, n % RAW]),
                                     weights[at_layer, n].rearrange("l p a -> p (l a)")).then_inc(loaded[n % RAW], 16)

                @block.tensor
                def _(pe):
                    bV = Banks(pe, psV, sem("bankV_full"), sem("bankV_free"))
                    bA = Banks(pe, psA, sem("bankA_full"), sem("bankA_free"))
                    rt = RowTiles(pe, sem("row_tiles"))
                    mm = nc.tensor.matmul

                    def three(out, n, k, kt, first, last, hi, lo):
                        mm(out, whi[:, n % SPL, k], hi[:, kt], start=first, stop=False)
                        mm(out, whi[:, n % SPL, k], lo[:, kt], start=False, stop=False)
                        return mm(out, wlo[:, n % SPL, k], hi[:, kt], start=False, stop=last)

                    def ada(n0, i, g):
                        bank = bA.open()
                        for q in range(4):
                            n = n0 + q
                            pe.wait_ge(lo_done, n + 1)
                            h = whi[:, n % SPL].rearrange("p (k c) n -> p k (c n)", k=2)
                            l = wlo[:, n % SPL].rearrange("p (k c) n -> p k (c n)", k=2)
                            for k in range(2):
                                kt = 2 * q + k
                                mm(bank[:], CS_T[:, kt], h[:, k], start=(kt == 0), stop=False)
                                ins = mm(bank[:], CS_T[:, kt], l[:, k], start=False, stop=(kt == 7))
                            ins.then_inc(chunk_used, 1)
                        freed = bA.close(None, freed=(sem("mrow_done"), i * 6 + g + 1))
                        return (g, freed)

                    def fold(pending):
                        g, freed = pending
                        pe.wait_ge(*freed)
                        bank = bV.open()
                        for j in range(4):
                            ins = mm(bank[:, 9 * j:9 * j + 9], MR[:, g % 2, j * P:(j + 1) * P],
                                     con("fold", 9, rows=64), start=True, stop=True)
                        bV.close(ins)

                    def up(n0, s, f):
                        for q, ring, freed in ((0, bA, (sem("gate_done"), s * FT + f + 1)),
                                               (1, bV, (sem("hidden_done"), s * FT + f + 1))):
                            n = n0 + q
                            bank = ring.open()
                            pe.wait_ge(lo_done, n + 1)
                            for kt in range(DT):
                                if f == 0 and q == 0:
                                    pe.wait_ge(sem("x_split"), 2 * s * DT + kt + 1)
                                ins = three(bank[:, 0:TOK], n, kt, kt, kt == 0, kt == DT - 1, XH, XL)
                            ins.then_inc(chunk_used, 1)
                            ring.close(None, freed=freed)

                    def product(n0, kts, hi, lo, wait_for, z0):
                        for d in range(DT):
                            bank = bV.open()
                            for k in range(kts):
                                q = d * kts + k
                                if q % 8 == 0:
                                    pe.wait_ge(lo_done, n0 + q // 8 + 1)
                                if d == 0:
                                    wait_for(k)
                                ins = three(bank[:, 0:TOK], n0 + q // 8, q % 8, k, k == 0, k == kts - 1, hi, lo)
                                if q % 8 == 7:
                                    ins.then_inc(chunk_used, 1)
                            bV.close(None if product_end(d, kts)[0] else ins, freed=(sem("z_ready"), z0 + d + 1))

                    def norm(s):
                        bank = bV.open()
                        pe.wait_ge(sem("zsum_ready"), s + 1)
                        mm(bank[:, 0:TOK], con("mean1024", P), ZSUM[:], start=True, stop=False)
                        pe.wait_ge(sem("z_ready"), (s + 1) * DT)
                        ins = mm(bank[:, 0:TOK], con("mean1024", P), ZT[:, DT - 1], start=False, stop=True)
                        bV.close(ins)
                        bank = bV.open()
                        mm(bank[:, 0:TOK], con("mean1024", P), QSUM[:], start=True, stop=False)
                        pe.wait_ge(sem("sq_ready"), (s + 1) * DT)
                        ins = mm(bank[:, 0:TOK], con("mean1024", P), SQ[:, DT - 1], start=False, stop=True)
                        bV.close(ins)

                    pe.wait_ge(sem("params"), 64)
                    pending = None
                    for item, n0 in zip(ITEMS, STARTS):
                        kind = item[0]
                        if kind == "ada":
                            now = ada(n0, item[1], item[2])
                            if pending:
                                fold(pending)
                            pending = now
                            if item[1:] == (0, 5):
                                fold(pending)
                                pending = None
                            continue
                        if pending:
                            fold(pending)
                            pending = None
                        if kind == "up":
                            up(n0, item[1], item[2])
                        elif kind == "down":
                            s = 2 * item[1]
                            product(n0, FT, HH, HL, lambda k, s=s: pe.wait_ge(sem("h_ready"), (s // 2) * FT + k + 1), s * DT)
                            norm(s)
                        elif kind == "proj":
                            t = item[1]
                            bank = bA.open()
                            pe.wait_ge(lo_done, n0 + 1)
                            for kt in range(DT):
                                if t == 0:
                                    pe.wait_ge(sem("x_split"), DT + kt + 1)
                                ins = three(bank[:, 0:TOK], n0, kt, kt, kt == 0, kt == DT - 1, XH, XL)
                            ins.then_inc(chunk_used, 1)
                            bA.close(None, freed=(sem("proj_ready"), t + 1))
                        elif kind == "mix":
                            mix_pe(pe, bV, bA, rt)
                        elif kind == "out":
                            product(n0, MIXT, XH, XL, lambda k: pe.wait_ge(sem("mixed"), k + 1), DT)
                            norm(1)

                @block.scalar
                def _(act):
                    A = Lane(act, sem("steps_act"))
                    fA = Filled(act, psA, sem("bankA_full"))
                    nsplit = [0]
                    activation = nc.scalar.activation

                    def split_to(m):
                        while nsplit[0] < min(m + 1, NCHUNK):
                            n = nsplit[0]
                            act.wait_ge(loaded[n % RAW], 16 * (n // RAW + 1))
                            if n >= SPL:
                                act.wait_ge(chunk_used, n - SPL + 1)
                            activation(whi[:, n % SPL], raw[:, n % RAW], ACT.Copy).then_inc(hi_done, 1)
                            nsplit[0] += 1

                    def modulate(s, after):
                        if s is not None:
                            act.wait_ge(sem("mods_ready"), s + 1)
                        for t in range(DT + 1):
                            if t < DT:
                                if after is not None:
                                    act.wait_ge(sem("zn_ready"), after * DT + t + 1)
                                    A.do(activation(XT[:, t], ZT[:, t], ACT.Identity,
                                                    scale=pcol("ln_g", after * DT + t),
                                                    bias=pcol("ln_b", after * DT + t)), sem("x_ready"))
                                    A.settle()
                                if s is not None:
                                    A.do(activation(XM[:, t, 0:SEQ], XT[:, t, 0:SEQ], ACT.Identity,
                                                    scale=scol(s, 1, t), bias=scol(s, 0, t)), sem("xm_prompt"))
                            if s is not None and t >= 1:
                                act.wait_ge(sem("xm_prompt"), s * DT + t)
                                act.wait_ge(sem("xm_sample"), s * DT + t)
                                A.do(activation(XH[:, t - 1], XM[:, t - 1], ACT.Copy), sem("xh_ready"))

                    def norm(n0, kts, s):
                        for d in range(DT):
                            split_to(n0 + ((d + 1) * kts - 1) // 8 + 2)
                            act.wait_ge(sem("z_ready"), s * DT + d + 1)
                            A.do(activation(SQ[:, d], ZT[:, d], ACT.Square), sem("sq_ready"))
                        act.wait_ge(sem("var_ready"), s + 1)
                        A.do(activation(RS[:], VR[:], ACT.Sqrt), sem("sd_ready"))
                        modulate(s + 1 if s < 2 else None, s)

                    act.wait_ge(sem("params"), 64)
                    for item, n0 in zip(ITEMS, STARTS):
                        kind = item[0]
                        if kind == "ada":
                            for q in range(4):
                                split_to(n0 + q + 2)
                            g = item[2]
                            bank = fA.take((chunk_used, n0 + 4))
                            A.do(activation(MR[:, g % 2], bank[0:64, :], ACT.Copy), sem("mrow_done"))
                            if item[1:] == (0, 5):
                                modulate(0, None)
                        elif kind == "up":
                            u = item[1] * FT + item[2]
                            split_to(n0 + 2)
                            bank = fA.take((chunk_used, n0 + 1))
                            if u >= 2:
                                act.wait_ge(sem("hidden_done"), u - 1)
                            A.do(activation(SG[:, u % 2], bank[:, 0:TOK], ACT.Silu), sem("gate_done"))
                            split_to(n0 + 3)
                        elif kind == "down":
                            norm(n0, FT, 2 * item[1])
                        elif kind == "proj":
                            split_to(n0 + 2)
                            bank = fA.take((chunk_used, n0 + 1))
                            A.do(activation(PJ[:, item[1]], bank[:, 0:TOK], ACT.Copy), sem("proj_ready"))
                        elif kind == "mix":
                            split_to(n0 + 2)
                            mix_act(act, A, fA)
                        elif kind == "out":
                            norm(n0, MIXT, 1)

                @block.vector
                def _(vec):
                    V = Lane(vec, sem("steps_vec"))
                    fV = Filled(vec, psV, sem("bankV_full"))
                    nsplit = [0]
                    tt, ts, stt = nc.vector.tensor_tensor, nc.vector.tensor_scalar, nc.vector.scalar_tensor_tensor

                    def split_to(m):
                        while nsplit[0] < min(m + 1, NCHUNK):
                            n = nsplit[0]
                            vec.wait_ge(hi_done, n + 1)
                            tt(wlo[:, n % SPL], raw[:, n % RAW], whi[:, n % SPL].bitcast(F32),
                               ALU.subtract).then_inc(lo_done, 1)
                            nsplit[0] += 1

                    def unfold(i, g):
                        bank = fV.take()
                        m = i * 24 + 4 * g
                        V.do(tt(MODS[:, m:m + 4], bank[:, 0:36].rearrange("p (a b) -> p a b", b=9),
                                PAR[:, PARC["ada_b"] + m:PARC["ada_b"] + m + 4].unsqueeze(2).to_broadcast([P, 4, 9]),
                                ALU.add), sem("bankV_free"))
                        if g == 5:
                            V.settle()
                            V.do(ts(MODS[:, i * 24 + 8:i * 24 + 16], MODS[:, i * 24 + 8:i * 24 + 16], 1.0, None, ALU.add))
                            V.do(ts(MODS[:, i * 24 + 16:i * 24 + 24], MODS[:, i * 24 + 16:i * 24 + 24], 1.0,
                                    (1.0 if i == 1 else 0.5) / ALPHA, ALU.add, ALU.mult))
                            V.mark(sem("mods_ready"))

                    def by_sample(ap):
                        return ap.unsqueeze(2).to_broadcast([P, DB, DS])

                    def modulate(s, after):
                        for t in range(DT + 2):
                            if t < DT and after is not None:
                                V.do(tt(ZT[:, t], ZT[:, t], MN[:], ALU.subtract))
                                V.settle()
                                V.do(tt(ZT[:, t], ZT[:, t], RS[:], ALU.mult), sem("zn_ready"))
                            if s is not None and 1 <= t <= DT:
                                u = t - 1
                                if after is not None:
                                    vec.wait_ge(sem("x_ready"), after * DT + u + 1)
                                V.do(tt(s8(gtmp[:, u % 2]), s8(XT[:, u, SEQ:TOK]), by_sample(scol(s, 1, u, 1, DB)), ALU.mult))
                                V.settle()
                                V.do(tt(s8(XM[:, u, SEQ:TOK]), s8(gtmp[:, u % 2]), by_sample(scol(s, 0, u, 1, DB)), ALU.add),
                                     sem("xm_sample"))
                            if s is not None and t >= 2:
                                u = t - 2
                                vec.wait_ge(sem("xh_ready"), s * DT + u + 1)
                                V.do(tt(XL[:, u], XM[:, u], XH[:, u].bitcast(F32), ALU.subtract), sem("x_split"))

                    def norm(n0, kts, s):
                        for d in range(DT):
                            m = n0 + ((d + 1) * kts - 1) // 8
                            split_to(m + 2)
                            at_end, c = product_end(d, kts)
                            bank = fV.take((chunk_used, n0 + c) if at_end else None)
                            V.do(tt(s8(gtmp[:, d % 2]), s8(bank[:, SEQ:TOK]), by_sample(scol(s, 2, d, 1, DB)), ALU.mult))
                            V.do(stt(ZT[:, d, 0:SEQ], bank[:, 0:SEQ], scol(s, 2, d), XT[:, d, 0:SEQ], ALU.mult, ALU.add))
                            V.settle()
                            V.do(tt(ZT[:, d, SEQ:TOK], gtmp[:, d % 2], XT[:, d, SEQ:TOK], ALU.add), sem("z_ready"))
                        bank = fV.take()
                        V.do(nc.vector.tensor_copy(MN[:], bank[:, 0:TOK]), sem("bankV_free"))
                        V.settle()
                        V.do(tt(VR[:], MN[:], MN[:], ALU.mult))
                        V.settle()
                        bank = fV.take()
                        V.do(tt(VR[:], bank[:, 0:TOK], VR[:], ALU.subtract), sem("bankV_free"))
                        V.settle()
                        V.do(ts(VR[:], VR[:], 0.0, LN_EPS / ALPHA ** 2, ALU.max, ALU.add), sem("var_ready"))
                        vec.wait_ge(sem("sd_ready"), s + 1)
                        V.do(nc.vector.reciprocal(RS[:], RS[:]))
                        V.settle()
                        modulate(s + 1 if s < 2 else None, s)

                    vec.wait_ge(sem("params"), 64)
                    pending = None
                    for item, n0 in zip(ITEMS, STARTS):
                        kind = item[0]
                        if kind == "ada":
                            for q in range(4):
                                split_to(n0 + q + 2)
                            if pending:
                                unfold(*pending)
                            pending = item[1:]
                            if item[1:] == (0, 5):
                                unfold(*pending)
                                pending = None
                                modulate(0, None)
                            continue
                        if pending:
                            unfold(*pending)
                            pending = None
                        if kind == "up":
                            u = item[1] * FT + item[2]
                            split_to(n0 + 3)
                            bank = fV.take((chunk_used, n0 + 2))
                            vec.wait_ge(sem("gate_done"), u + 1)
                            V.do(tt(HF[:, u % 2], SG[:, u % 2], bank[:, 0:TOK], ALU.mult), sem("hidden_done"))
                            V.settle()
                            V.do(nc.vector.tensor_copy(HH[:, item[2]], HF[:, u % 2]))
                            V.settle()
                            V.do(tt(HL[:, item[2]], HF[:, u % 2], HH[:, item[2]].bitcast(F32), ALU.subtract), sem("h_ready"))
                        elif kind == "down":
                            norm(n0, FT, 2 * item[1])
                        elif kind == "proj":
                            split_to(n0 + 2)
                        elif kind == "mix":
                            split_to(n0 + 2)
                            mix_vec(vec, V, fV)
                        elif kind == "out":
                            vec.wait_ge(sem("stored"), 160)
                            norm(n0, MIXT, 1)

                @block.gpsimd
                def _(pool):
                    G = Lane(pool, sem("steps_pool"))

                    def sums(s):
                        add = nc.gpsimd.tensor_tensor
                        for d in range(1, DT - 1):
                            pool.wait_ge(sem("z_ready"), s * DT + d + 1)
                            G.settle()
                            G.do(add(ZSUM[:], ZT[:, 0] if d == 1 else ZSUM[:], ZT[:, d], ALU.add))
                            pool.wait_ge(sem("sq_ready"), s * DT + d + 1)
                            G.do(add(QSUM[:], SQ[:, 0] if d == 1 else QSUM[:], SQ[:, d], ALU.add))
                        G.mark(sem("zsum_ready"))

                    sums(0)
                    mix_pool(pool, G)
                    sums(1)
                    sums(2)
            numbers = [s.num for s in sems.values()]
            nc.all_engine_barrier(sems_to_clear=range(min(numbers), max(numbers) + 1))

        with nc.Block() as block:
            @block.sync
            def _(sp):
                sp.dma_start(yT, whole(XT[:])).then_inc(sem("stored"), 16)
                sp.wait_ge(sem("stored"), 16)


def _columns(v, rows=P):
    return np.ascontiguousarray(v.reshape(-1, rows).T)


def _spaced(v, heads, width, pitch):
    out = np.zeros(v.shape[:-1] + (heads, pitch), v.dtype)
    out[..., :width] = v.reshape(v.shape[:-1] + (heads, width))
    return out.reshape(v.shape[:-1] + (heads * pitch,))


def _weight_stream(a):
    out = np.zeros((DEPTH, NCHUNK, P, 8, P), np.float32)
    for l in range(DEPTH):
        ada = a["ada_w"][l].reshape(8, P, 18, 512)
        w_in = a["w_in"][l]
        g0, m0 = RW_PROJ, RW_PROJ + GLA_PROJ
        win = np.zeros((D, NPROJ * P), np.float32)

        def put(tile, part):
            win[:, tile * P:tile * P + part.shape[1]] = part

        put(0, w_in[:, 0:RW_PROJ])
        put(T_GQ, _spaced(w_in[:, g0:g0 + GQK], GH, DK, 64))
        put(T_GK, _spaced(w_in[:, g0 + GQK:g0 + 2 * GQK], GH, DK, 64))
        put(T_GV, w_in[:, g0 + 2 * GQK:g0 + 2 * GQK + GW])
        low = g0 + 2 * GQK + GW
        put(T_LOW, w_in[:, low:low + 16])
        win[:, T_LOW * P + 32:T_LOW * P + 36] = w_in[:, m0 + 4 * MW:m0 + 4 * MW + 4]
        win[:, T_LOW * P + 64:T_LOW * P + 68] = w_in[:, m0 + 4 * MW + 4:m0 + 4 * MW + 8]
        put(T_GR, _spaced(w_in[:, low + 16:low + 16 + GW], GH, DV, P))
        put(T_MQK, w_in[:, m0:m0 + 4 * MW])
        w_out = a["w_out"][l]
        wout = np.zeros((MIXT * P, D), np.float32)
        wout[0:RW_W] = w_out[0:RW_W]
        wout[RW_W:RW_W + GH * P] = _spaced(w_out[RW_W:RW_W + GW].T, GH, DV, P).T
        wout[RW_W + GH * P:] = w_out[RW_W + GW:]
        ff = {}
        for s in range(2):
            for name in ("ffn_wg", "ffn_wu"):
                t = np.zeros((D, FT * P), np.float32)
                t[:, :FF] = a[name][l, s]
                ff[name, s] = t
            t = np.zeros((FT * P, D), np.float32)
            t[:FF] = a["ffn_wd"][l, s]
            ff["ffn_wd", s] = t

        def columns(w, tile):
            return w[:, tile * P:(tile + 1) * P].reshape(8, P, P).transpose(1, 0, 2)

        def by_output(w):
            k = w.shape[0] // P
            t = w.reshape(k, P, DT, P).transpose(2, 0, 1, 3).reshape(DT * k // 8, 8, P, P)
            return t.transpose(0, 2, 1, 3)

        for item, n in zip(ITEMS, chunk_starts()):
            if item[0] == "ada":
                t = ada[:, :, item[1] * 6 + item[2]].reshape(4, 2, P, 512).transpose(0, 2, 1, 3)
                out[l, n:n + 4] = t.reshape(4, P, 8, P)
            elif item[0] == "up":
                out[l, n] = columns(ff["ffn_wg", item[1]], item[2])
                out[l, n + 1] = columns(ff["ffn_wu", item[1]], item[2])
            elif item[0] == "down":
                out[l, n:n + DT * FT // 8] = by_output(ff["ffn_wd", item[1]])
            elif item[0] == "proj":
                out[l, n] = columns(win, item[1])
            elif item[0] == "out":
                out[l, n:n + DT * MIXT // 8] = by_output(wout)
    return out.reshape(DEPTH, NCHUNK, P, 8 * P)


def _parameters(a):
    out = np.zeros((DEPTH, P, NPAR), np.float32)
    for l in range(DEPTH):
        def put(name, cols, row=0):
            out[l, row:row + cols.shape[0], PARC[name]:PARC[name] + cols.shape[1]] = cols

        for name, src in (("ln_g", "ln_g"), ("ln_b", "ln_b"), ("ada_b", "ada_b"), ("mu", "rw_mu"), ("w0", "rw_w0"),
                          ("a0", "rw_a0"), ("k_k", "rw_k_k"), ("k_a", "rw_k_a"), ("r_k", "rw_r_k"),
                          ("gn_g", "rw_gn_g"), ("gn_b", "rw_gn_b"), ("conv_w", "ml_conv_w"), ("conv_b", "ml_conv_b"),
                          ("ml_g", "ml_gn_g")):
            put(name, _columns(a[src][l]))
        put("gla_b", _columns(_spaced(a["gla_a_b"][l], GH, DK, 64)))
        put("gla_g", _columns(a["gla_gn_g"][l], DV))
        put("i_b", a["ml_i_b"][l][:, None], 32)
        put("f_b", a["ml_f_b"][l][:, None], 64)
    return out


def _constants():
    c = np.zeros((P, NCONST), np.float32)

    def put(name, m, at=0):
        c[:m.shape[0], CC[name] + at:CC[name] + at + m.shape[1]] = m

    i = np.arange(P)
    a, b = i[:, None], i[None, :]
    put("ident", np.eye(P, dtype=np.float32))
    put("ones64", (a // 64 == b // 64) / 64.0)
    put("mean1024", np.full((P, P), 1.0 / D))
    put("ones96", np.full((DV, P), 1.0 / DV))
    put("mask_p", (a // CH == b // CH) * (a < b))
    put("mask_p", (a // CH == b // CH) * (a <= b), P)
    u, v = a[:NS], b[:, :NS]
    put("mask_s", (u // DS == v // DS) * (u < v))
    put("mask_s", (u // DS == v // DS) * (u <= v), NS)
    for n in range(6):
        m = (a >> (n + 1) == b >> (n + 1)) * ((a >> n) % 2 == 1) * ((b >> n) % 2 == 0)
        put("level", m, n * P)
        if n == 0:
            put("level0t", m.T)
    put("neg_p", np.where((a // CH == b // CH) & (a <= b), 0.0, -1e30))
    put("neg_s", np.where((u // DS == v // DS) & (u <= v), 0.0, -1e30))
    put("seqmask", np.arange(NS)[:, None] // DS == np.arange(DB)[None])
    t = np.arange(TOK)
    first = np.where(t < SEQ, t % CH == 0, t % DS == 0)
    put("reset", np.tile(1.0 - first, (P, 1)))
    put("negreset", np.tile(np.where((t >= SEQ) & (t % DS == 0), -3e38, 0.0), (MH, 1)))
    f = np.arange(2 * P)
    put("pairsel", np.arange(MH)[:, None] == f[None] // 64)
    f = np.arange(4 * P)
    put("headsel", np.arange(MH)[:, None] == f[None] // P)
    fold = np.zeros((64, 9))
    fold[np.arange(9), np.arange(9)] = 1
    fold[32 + np.arange(9), np.arange(9)] = 1
    put("fold", fold)
    return c


def kernel(**inputs):
    import concourse.bacc as bacc
    from concourse.bass_utils import run_bass_kernel_spmd

    a = {k: np.asarray(v) for k, v in inputs.items()}
    L = DEPTH

    def flat(v):
        return np.ascontiguousarray(v).reshape(v.shape[0], v.shape[1], -1)

    tokens = np.concatenate([a["x_prompt"].reshape(SEQ, D), a["x_sample"].reshape(NS, D)])
    cond = np.concatenate([a["c_prompt"], a["c_sample"]])
    xT = np.ascontiguousarray(tokens.T.reshape(DT, P, TOK).transpose(1, 0, 2))
    cT = np.ascontiguousarray(cond.T.reshape(DT, P, 1 + DB).transpose(1, 0, 2))
    w2 = np.concatenate([a["rw_w2"], a["rw_a2"]], axis=1)
    a2g = _spaced(a["gla_a2"], GH, DK, 64)
    st_shift = flat(a["state_rwkv_shift"].reshape(L, DB, NRW, P).transpose(0, 3, 2, 1))
    st_rw = flat(a["state_rwkv"].reshape(L, DB, RP, 2, HD, HD).transpose(0, 3, 5, 2, 1, 4).reshape(L, P, -1))
    st_gla = np.zeros((L, 2, 64, GP, DB, DV), np.float32)
    st_gla[:, :, :DK] = a["state_gla"].reshape(L, DB, GP, 2, DK, DV).transpose(0, 3, 4, 2, 1, 5)
    st_gla = st_gla.reshape(L, P, -1)
    st_c = flat(a["state_mlstm_c"].reshape(L, DB, MP, 2, HD, HD).transpose(0, 3, 5, 2, 1, 4).reshape(L, P, -1))
    st_n = flat(a["state_mlstm_n"].reshape(L, DB, MP, 2, HD).transpose(0, 3, 4, 2, 1).reshape(L, P, -1))
    st_m = np.ascontiguousarray(a["state_mlstm_m"].transpose(0, 2, 1))
    st_conv = flat(a["state_mlstm_conv"].reshape(L, DB, CONV - 1, 4, P).transpose(0, 4, 3, 1, 2))

    arrays = {"xT": xT.reshape(P, -1), "cT": cT.reshape(P, -1), "weights": _weight_stream(a), "par": _parameters(a), "consts": _constants(),
              "w2": w2, "g2": a["rw_g2"], "a2g": a2g, "st_shift": st_shift, "st_rw": st_rw, "st_gla": st_gla,
              "st_c": st_c, "st_n": st_n, "st_m": st_m, "st_conv": st_conv}
    outs = {"yT": (P, DT * TOK), "o_rwp": (L, P, RP * HD), "o_rws": (L, P, RP * DB * HD), "o_shift": (L, P, NRW * (1 + DB)),
            "o_glap": (L, P, GP * DV), "o_glas": (L, P, GP * DB * DV), "o_cp": (L, P, MP * HD), "o_cs": (L, P, MP * DB * HD),
            "o_np": (L, P, MP * (1 + DB)), "o_m": (L, MH, 1 + DB), "o_conv": (L, P, 4 * (1 + DB) * (CONV - 1))}
    nc = bacc.Bacc("TRN2", target_bir_lowering=False, num_devices=1)
    args = {}
    feed = {}
    for name, v in arrays.items():
        v = np.ascontiguousarray(v)
        feed[name + "_dram"] = v
        args[name] = nc.dram_tensor(name + "_dram", v.shape, F32, kind="ExternalInput").ap()
    for name, shape in outs.items():
        args[name] = nc.dram_tensor(name + "_dram", shape, F32, kind="ExternalOutput").ap()
    hybrid_trunk(nc, **args)
    r = run_bass_kernel_spmd(nc, [feed], core_ids=[0]).results[0]
    o = {name: np.asarray(r[name + "_dram"]) for name in outs}

    y = o["yT"].reshape(P, DT, TOK).transpose(2, 1, 0).reshape(TOK, D)
    shift = o["o_shift"].reshape(L, P, NRW, 1 + DB).transpose(0, 3, 2, 1).reshape(L, 1 + DB, RW_PROJ)
    n = o["o_np"].reshape(L, 2, HD, MP, 1 + DB).transpose(0, 4, 3, 1, 2).reshape(L, 1 + DB, MH, HD)
    m = o["o_m"].transpose(0, 2, 1)
    conv = o["o_conv"].reshape(L, P, 4, 1 + DB, CONV - 1).transpose(0, 3, 4, 2, 1).reshape(L, 1 + DB, CONV - 1, 2 * MW)

    def heads(v, pairs, seqs, k, width, swap):
        v = v.reshape(L, 2, 64, pairs, seqs, width)[:, :, :k].transpose(0, 4, 3, 1, 2, 5).reshape(L, seqs, 2 * pairs, k, width)
        return np.ascontiguousarray(v.transpose(0, 1, 2, 4, 3) if swap else v)

    cc = np.ascontiguousarray
    return (cc(y[:SEQ].reshape(1, SEQ, D)), cc(y[SEQ:].reshape(DB, DS, D)),
            heads(o["o_rwp"], RP, 1, HD, HD, True), cc(shift[:, :1]), heads(o["o_glap"], GP, 1, DK, DV, False),
            heads(o["o_cp"], MP, 1, HD, HD, True), cc(n[:, :1]), cc(m[:, :1]), cc(conv[:, :1]),
            heads(o["o_rws"], RP, DB, HD, HD, True), cc(shift[:, 1:]), heads(o["o_glas"], GP, DB, DK, DV, False),
            heads(o["o_cs"], MP, DB, HD, HD, True), cc(n[:, 1:]), cc(m[:, 1:]), cc(conv[:, 1:]))
```

```python
from contextlib import ExitStack

import numpy as np

import concourse.bass as bass
from concourse import mybir

F32 = mybir.dt.float32
F32R = mybir.dt.float32r
ALU = mybir.AluOpType
ACT = mybir.ActivationFunctionType

P = 128
D = 1024
DT = D // P
SEQ, DB, DS = 256, 8, 8
NS = DB * DS
TOK = SEQ + NS
DEPTH = 2
FF = 2752
FT = -(-FF // P)
ALPHA = (2 * DEPTH) ** 0.25
LN_EPS, GN_EPS, NORM_EPS = 1e-5, 64e-5, 1e-6
CH = 64
NCH = SEQ // CH

RW_H, HD = 6, 64
RW_W = RW_H * HD
RP = RW_H // 2
RW_PROJ = 3 * RW_W + 64 + 64 + 128
GH, DK, DV = 4, 48, 96
GP = GH // 2
GQK, GW = GH * DK, GH * DV
GLA_PROJ = 2 * GQK + 2 * GW + 16
MH = 4
MP = MH // 2
MW = MH * HD
CONV = 4
CW = SEQ + CONV - 1
CS = DS + CONV - 1
CN = CW + DB * CS

T_R, T_K, T_V, T_WA, T_G = 0, 3, 6, 9, 10
T_GQ, T_GK, T_GV, T_LOW, T_GR = 11, 13, 15, 18, 19
T_MQK, T_MV, T_MO = 23, 27, 29
NPROJ = 31
NRW = 11
MIXT = RP + GH + MP

_cols, _n = {}, 0
for _name, _k in (("ln_g", 24), ("ln_b", 24), ("ada_b", 72), ("mu", 11), ("w0", 3), ("a0", 3), ("k_k", 3),
                  ("k_a", 3), ("r_k", 3), ("gn_g", 3), ("gn_b", 3), ("gla_b", 2), ("gla_g", 4),
                  ("conv_w", 16), ("conv_b", 4), ("ml_g", 2), ("i_b", 1), ("f_b", 1)):
    _cols[_name] = _n
    _n += _k
PARC = _cols
NPAR = _n

_cols, _n = {}, 0
for _name, _k in (("ident", 128), ("ones64", 128), ("mean1024", 128), ("ones96", 128),
                  ("ident64", 64), ("mask_p", 128), ("mask_s", 128), ("level", 6 * 64), ("level0t", 64), ("neg_p", 64),
                  ("neg_s", 64), ("seqmask", 8), ("reset", TOK), ("pairsel", 256), ("headsel", 256),
                  ("fold", 9), ("negreset", TOK)):
    _cols[_name] = _n
    _n += _k
CC = _cols
NCONST = _n

LEVELS = (6, 6, 3)
RW_PRE = (3, 2, 2, 4, 1)
RW_TAUS = []
for _levels in LEVELS:
    RW_TAUS += [1, 2, 2] + [2] * (2 * (_levels - 1)) + [1, 1] + ([1] * 4 + [1] if _levels == 6 else [1, 1, 1] + [1] * 3)
RW_TAUS += [1, 1, 0]
PRE_FILL = 9
GL_STEPS, ML_STEPS = 12, 14

def layer_items():
    def ada(i, groups):
        out = []
        for g in groups:
            for q in range(4):
                out.append(("ada", i, g, q))
                if q == 1 and g > groups[0]:
                    out.append(("fold", i, g - 1))
        return out + [("fold", i, groups[-1])]

    def spread(slots, fill):
        out, total, given, so_far = [], sum(w for _, w in slots), 0, 0
        for item, w in slots:
            out.append(item)
            so_far += w
            upto = round(len(fill) * so_far / total)
            out += fill[given:upto]
            given = upto
        return out

    items = ada(0, range(0, 4))
    items += spread([(("up", 0, f), 1) for f in range(FT)], ada(0, range(4, 6)) + ada(1, range(6)))
    items += [("down", 0, 0)]
    items += [("proj", t) for t in range(NRW)]
    rest = [("proj", t) for t in range(NRW, NPROJ)]
    first, later = rest[:PRE_FILL], rest[PRE_FILL:]
    items += spread([(("rw",), w) for w in RW_PRE], first)
    items += spread([(("rw",), w) for w in RW_TAUS], spread([(t, 1) for t in later], ada(2, range(6))))
    both = [(("ml",), 1)] + [(kind, 1) for _ in range(GL_STEPS) for kind in (("gl",), ("ml",))]
    both += [(("ml",), 1)] * (ML_STEPS - GL_STEPS - 1)
    items += [item for item, _ in both]
    items += [("mix",)]
    items += [("out",)]
    items += [("up", 1, f) for f in range(FT)]
    items += [("down", 1, 0)]
    return items


CHUNKS_OF = {"ada": 1, "fold": 0, "rw": 0, "gl": 0, "ml": 0, "up": 2, "down": DT * FT // 8, "proj": 1, "mix": 0, "out": DT * MIXT // 8}
ITEMS = layer_items()
NCHUNK = sum(CHUNKS_OF[i[0]] for i in ITEMS)

def chunk_starts():
    at, out = 0, []
    for item in ITEMS:
        out.append(at)
        at += CHUNKS_OF[item[0]]
    return out


RAW, SPL = 4, 3


class Arena:

    def __init__(self, nc, at):
        self.nc, self.at = nc, at

    def take(self, name, shape, dt=F32):
        size = 4 * int(np.prod(shape[1:]))
        t = self.nc.alloc_sbuf_tensor_at(name, shape, dt, offset=self.at)
        self.at += -(-size // 32) * 32
        assert self.at <= 229344, (name, self.at)
        return t


class Lane:

    def __init__(self, eng, steps):
        self.eng, self.steps, self.count, self.last = eng, steps, {}, None

    def do(self, ins, signal=None):
        s = self.steps if signal is None else signal
        self.count[s.num] = self.count.get(s.num, 0) + 1
        self.last = (s, self.count[s.num])
        ins.then_inc(s, 1)

    def settle(self):
        if self.last:
            self.eng.wait_ge(*self.last)
            self.last = None

    def mark(self, signal):
        self.settle()
        self.eng.sem_inc(signal, 1)
        self.count[signal.num] = self.count.get(signal.num, 0) + 1


class Banks:

    def __init__(self, pe, banks, full, free):
        self.pe, self.banks, self.full, self.free = pe, banks, full, free
        self.n, self.frees, self.freed = 0, 0, [None] * len(banks)

    def open(self):
        at = self.n % len(self.banks)
        if self.freed[at]:
            self.pe.wait_ge(*self.freed[at])
        return self.banks[at]

    def close(self, ins=None, freed=None):
        if ins is not None:
            ins.then_inc(self.full, 1)
        if freed is None:
            self.frees += 1
            freed = (self.free, self.frees)
        self.freed[self.n % len(self.banks)] = freed
        self.n += 1
        return freed


class RowTiles:

    def __init__(self, pe, order):
        self.pe, self.order, self.n = pe, order, 0

    def after(self, ins):
        ins.then_inc(self.order, 1)
        self.n += 1
        self.pe.wait_ge(self.order, self.n)


class Filled:

    def __init__(self, eng, banks, full):
        self.eng, self.banks, self.full, self.n, self.fulls = eng, banks, full, 0, 0

    def take(self, at=None):
        if at is None:
            self.fulls += 1
            at = (self.full, self.fulls)
        self.eng.wait_ge(*at)
        self.n += 1
        return self.banks[(self.n - 1) % len(self.banks)]


def hybrid_trunk(nc, xT, cT, weights, par, consts, w2, g2, a2g, st_shift, st_rw, st_gla, st_c, st_n, st_m, st_conv,
                 yT, o_rwp, o_rws, o_shift, o_glap, o_glas, o_cp, o_cs, o_np, o_m, o_conv):
    with ExitStack() as ctx:
        sems = {}

        def sem(name):
            if name not in sems:
                sems[name] = ctx.enter_context(nc.semaphore(name))
            return sems[name]

        keep = Arena(nc, 16512)
        XT = keep.take("XT", [P, DT, TOK])
        raw = keep.take("raw", [P, RAW, 8, P])
        whi = keep.take("whi", [P, SPL, 8, P], F32R)
        wlo = keep.take("wlo", [P, SPL, 8, P], F32R)
        CON = keep.take("CON", [P, NCONST])
        PAR = keep.take("PAR", [P, NPAR])
        MODS = keep.take("MODS", [P, 72, 1 + DB])
        CS_T = keep.take("CS_T", [P, 8, P], F32R)
        crow = keep.take("crow", [P, 8, 1 + DB])
        w2_at = keep.at
        W2 = keep.take("W2", [P, RW_W])
        G2 = keep.take("G2", [P, RW_W])
        OMK = keep.take("OMK", [P, RP])
        A2G = keep.take("A2G", [16, GP, P])
        MR = keep.take("MR", [64, 2, 512])
        XH = keep.take("XH", [P, 9, TOK], F32R)
        XL = keep.take("XL", [P, 9, TOK], F32R)
        base = keep.at
        xh_at, xl_at = base - 2 * 4 * MIXT * TOK, base - 4 * MIXT * TOK
        ffn = Arena(nc, base)
        ZT = ffn.take("ZT", [P, DT, TOK])
        HH = ffn.take("HH", [P, FT, TOK], F32R)
        HL = ffn.take("HL", [P, FT, TOK], F32R)
        SG = ffn.take("SG", [P, 2, TOK])
        HF = ffn.take("HF", [P, 2, TOK])
        SQ = ffn.take("SQ", [P, DT, TOK])
        XM = SQ
        ZSUM = ffn.take("ZSUM", [P, TOK])
        QSUM = ffn.take("QSUM", [P, TOK])
        MN = ffn.take("MN", [P, TOK])
        VR = ffn.take("VR", [P, TOK])
        gtmp = ffn.take("gtmp", [P, 2, NS])

        mix = Arena(nc, base)
        PJ = mix.take("PJ", [P, NPROJ, TOK])
        hold = mix.at
        rw = Arena(nc, hold)
        DF = rw.take("DF", [P, NRW, TOK])
        rw = Arena(nc, hold)
        AR = rw.take("AR", [P, 2, RP, TOK])
        BH = rw.take("BH", [P, RP, TOK])
        KH = rw.take("KH", [P, RP, TOK])
        BT = rw.take("BT", [P, RP, TOK])
        KT = rw.take("KT", [P, RP, TOK])
        SH = rw.take("SH", [P, NRW, DB])
        SHO = rw.take("SHO", [P, NRW, 1 + DB])
        GG2 = rw.take("GG2", [P, TOK])
        ZS = rw.take("ZS", [P, RP, DB, HD])
        tau0 = rw.at
        TK = rw.take("TK", [P, 4, RW_W])
        AM = rw.take("AM", [P, RW_H, 4, CH])
        Tn = rw.take("Tn", [P, RW_H, CH])
        Tt = rw.take("Tt", [P, RW_H, CH])
        Yb = rw.take("Yb", [P, RW_H, CH])
        RB = rw.take("RB", [P, RW_W])
        UX = rw.take("UX", [64, 2, 2, DB, HD])
        U0 = rw.take("U0", [P, RW_W])
        U = rw.take("U", [P, RW_W])
        WT = rw.take("WT", [P, RP, P])
        Z = rw.take("Z", [P, 2, RP, HD])
        ZP = rw.take("ZP", [P, RP, HD])
        PC = rw.take("PC", [P, RP, NCH + DB])
        GT = rw.take("GT", [P, RP, NS])
        pre = Arena(nc, tau0)
        TH = pre.take("TH", [64, TOK])
        SGD = pre.take("SGD", [P, TOK])
        SW = pre.take("SW", [P, RP, TOK])
        BB = pre.take("BB", [P, RP, TOK])
        BP = pre.take("BP", [P, RP, TOK])
        KKS = pre.take("KKS", [P, RP, TOK])
        EX = pre.take("EX", [P, 2, RP, TOK])
        AA = pre.take("AA", [P, RP, TOK])
        KK = pre.take("KK", [P, RP, TOK])
        post = Arena(nc, tau0)
        N2 = post.take("N2", [P, RP, TOK])
        N3 = post.take("N3", [P, RP, TOK])
        N4 = post.take("N4", [P, RP, TOK])
        BON, YT = PJ[:, T_R:T_R + RP], PJ[:, T_K:T_K + RP]
        gm = Arena(nc, hold)
        GZ = gm.take("GZ", [P, GP, TOK])
        GE = gm.take("GE", [P, GP, TOK])
        GB = gm.take("GB", [P, GP, TOK])
        GN = nc.alloc_sbuf_tensor_at("GN", [P, GH, TOK], F32, offset=hold)
        KX = nc.alloc_sbuf_tensor_at("KX", [64, DB, GP * P], F32, offset=hold)
        gm.at = hold + 4 * DB * GP * P
        OT = nc.alloc_sbuf_tensor_at("OT", [P, GH, TOK], F32, offset=gm.at)
        KI = gm.take("KI", [P, GP, TOK])
        KE = gm.take("KE", [P, GP, TOK])
        QD = gm.take("QD", [P, GP, TOK])
        VG = gm.take("VG", [P, 3, GW])
        KET = gm.take("KET", [P, 3, GP * P])
        ATG = gm.take("ATG", [P, 3, GH, CH])
        SP = gm.take("SP", [P, NCH + 1, GP, DV])
        S0 = gm.take("S0", [P, GP, DB, DV])
        GPC = gm.take("GPC", [P, GP, NCH + DB])
        at = gm.at
        XP = gm.take("XP", [P, 4, CN])
        QW = nc.alloc_sbuf_tensor_at("QW", [P, MP, TOK], F32, offset=at)
        EMB = nc.alloc_sbuf_tensor_at("EMB", [P, MP, TOK], F32, offset=at + 4 * MP * TOK)
        QK = gm.take("QK", [P, 4, TOK])
        M0 = gm.take("M0", [MH, DB])
        MO = gm.take("MO", [MH, 1 + DB])
        N0 = gm.take("N0", [P, MP, DB])
        NO = gm.take("NO", [P, MP, 1 + DB])
        SCV = gm.take("SCV", [P, 4, DB, CONV - 1])
        COV = gm.take("COV", [P, 4, 1 + DB, CONV - 1])
        COLS = gm.take("COLS", [P, 3, 8])
        MPC = gm.take("MPC", [P, MP, NCH + DB])
        ST = gm.take("ST", [P, 3, MH, CH])
        CP = gm.take("CP", [P, NCH + 1, MP, P])
        C0 = gm.take("C0", [P, MP, DB, P])
        VM = gm.take("VM", [P, 3, MH, P])
        KW = nc.alloc_sbuf_tensor_at("KW", [P, 3, MW], F32, offset=w2_at)
        dead = Arena(nc, base)
        VX = dead.take("VX", [64, MH, DB, HD])
        at = dead.at
        CV = dead.take("CV", [P, 4, CN])
        HT = nc.alloc_sbuf_tensor_at("HT", [P, MP, TOK], F32, offset=at)
        DD = nc.alloc_sbuf_tensor_at("DD", [P, MP, TOK], F32, offset=at + 4 * MP * TOK)
        assert dead.at <= base + 4 * NRW * TOK
        over = [a + 4 * TOK * i for a in (xh_at, xl_at) for i in range(RP, MIXT)]
        IG, FZ, LF, BM, MM, ER, CR, D0, D1, E2, WJ = (
            nc.alloc_sbuf_tensor_at(f"row{i}", [MH, TOK], F32, offset=over[i]) for i in range(11))
        DW = nc.alloc_sbuf_tensor_at("DW", [P, MH, CH], F32, offset=over[11])

        psV = [ctx.enter_context(nc.psum_tensor(f"psV{i}", [P, 512], F32)) for i in range(4)]
        psA = [ctx.enter_context(nc.psum_tensor(f"psA{i}", [P, 512], F32)) for i in range(2)]
        psY = ctx.enter_context(nc.psum_tensor("psY", [P, 512], F32))
        psC = ctx.enter_context(nc.psum_tensor("psC", [P, 512], F32))

        def con(name, k, rows=P, at=0):
            return CON[0:rows, CC[name] + at:CC[name] + at + k]

        def pcol(name, i=0, lo=0, hi=P):
            return PAR[lo:hi, PARC[name] + i:PARC[name] + i + 1]

        def s8(ap):
            return ap.rearrange("p (s t) -> p s t", t=DS)

        def t88(ap):
            return ap.rearrange("p a (s t) -> p a s t", t=DS)

        def whole(t):
            return t.rearrange("p a b -> p (a b)")

        loaded0 = sem("loaded0")
        with nc.Block() as block:
            @block.sync
            def _(sp):
                sp.dma_start(CON[:], consts).then_inc(loaded0, 16)
                sp.dma_start(crow[:], cT).then_inc(loaded0, 16)
                sp.dma_start(XT[:], xT).then_inc(loaded0, 16)
                sp.wait_ge(loaded0, 48)

            @block.gpsimd
            def _(pool):
                nc.gpsimd.memset(raw[:, 0], 0.0).then_inc(sem("zeroed"), 1)
                nc.gpsimd.memset(A2G[:], 0.0).then_inc(sem("zeroed"), 1)

            @block.scalar
            def _(act):
                act.wait_ge(loaded0, 48)
                nc.scalar.activation(crow[:], crow[:], ACT.Silu).then_inc(sem("c_silu"), 1)

            @block.vector
            def _(vec):
                vec.wait_ge(sem("c_silu"), 1)
                vec.wait_ge(sem("zeroed"), 2)
                nc.vector.tensor_copy(CS_T[:], raw[:, 0]).then_inc(sem("c_split"), 1)
                vec.wait_ge(sem("c_split"), 1)
                nc.vector.tensor_copy(CS_T[:, :, 0:9], crow[:]).then_inc(sem("c_split"), 1)
                vec.wait_ge(sem("c_split"), 2)
                nc.vector.tensor_tensor(CS_T[:, :, 32:41], crow[:], CS_T[:, :, 0:9].bitcast(F32),
                                        ALU.subtract).then_inc(sem("c_split"), 1)
                vec.wait_ge(sem("c_split"), 3)

        names = ["chunk_used", "row_tiles", "hi_done", "lo_done", "bankV_full", "bankV_free", "bankA_full", "bankA_free",
                 "steps_vec", "steps_act", "steps_pool", "x_split", "xm_sample", "gate_done", "hidden_done", "h_ready",
                 "z_ready", "sq_ready", "zsum_ready", "zn_ready", "x_ready", "mods_ready", "mrow_done",
                 "var_ready", "sd_ready", "proj_ready", "params", "stored"]
        for n in names:
            sem(n)
        loaded = [sem(f"loaded_{i}") for i in range(RAW)]
        chunk_used, hi_done, lo_done = sem("chunk_used"), sem("hi_done"), sem("lo_done")

        STARTS = chunk_starts()

        def product_end(d, kts):
            q = (d + 1) * kts
            return q % 8 == 0, q // 8

        def scol(i, j, dt, g=0, n=1):
            return MODS[:, i * 24 + j * 8 + dt, g:g + n]

        nc.all_engine_barrier()
        with nc.Fori(0, DEPTH) as layer:
            with nc.Block() as block:
                at_layer = bass.ds(layer, 1)

                def of_layer(ap):
                    return ap[at_layer].rearrange("l p a -> p (l a)")

                TAUS = ((0, 0, P), (1, P, P), (2, 2 * P, NS))

                PARTS = [[(slice(64 * i, 64 * i + 64), t0 + 64 * i) for i in range(w // 64)] for _, t0, w in TAUS]

                def hp(h):
                    return h // 2, slice(64 * (h % 2), 64 * (h % 2) + 64)

                def rsqrt(A, ap, signal):
                    A.do(nc.scalar.activation(ap, ap, ACT.Ln))
                    A.settle()
                    A.do(nc.scalar.activation(ap, ap, ACT.Exp, scale=-0.5), signal)

                def gg(j):
                    return PJ[:, T_WA + j] if j < 2 else GG2[:]

                SCORE_HEADS = ((0, 2), (1, 3), (4,), (5,))

                PAIRED = [(2 * j + i, s) for j in range(RP) for s in range(DB) for i in range(2)]

                def EVEN_ODD(n):
                    return [*range(0, n, 2), *range(1, n, 2)]

                def rw_pe(pe, bV, bA, rt):
                    mm, tr = nc.tensor.matmul, nc.tensor.transpose

                    yield
                    pe.wait_ge(sem("rw_tanh"), 1)
                    for j in range(RP):
                        bank = bA.open()
                        bA.close(mm(bank[:, 0:TOK], W2[0:64, j * P:(j + 1) * P], TH[:], start=True, stop=True),
                                 (sem("rw_low"), j + 1))
                    for j in range(RP):
                        bank = bA.open()
                        bA.close(mm(bank[:, 0:TOK], W2[64:128, j * P:(j + 1) * P], PJ[64:128, T_WA], start=True, stop=True),
                                 (sem("rw_low"), 3 + j + 1))
                    yield
                    pe.wait_ge(sem("rw_gd"), 1)
                    for j in range(RP):
                        bank = bA.open()
                        bA.close(mm(bank[:, 0:TOK], G2[:, j * P:(j + 1) * P], SGD[:], start=True, stop=True),
                                 (sem("rw_low"), 6 + j + 1))
                    pe.wait_ge(sem("rw_sq"), 1)
                    for j in range(RP):
                        bank = bV.open()
                        bV.close(mm(bank[:, 0:TOK], con("ones64", P), KKS[:, j], start=True, stop=True))
                    yield
                    yield
                    pe.wait_ge(sem("rw_rkk"), 1)
                    for j in range(RP):
                        bank = bV.open()
                        bV.close(mm(bank[:, 0:TOK], con("ones64", P), BB[:, j], start=True, stop=True))
                    yield
                    for tau, t0, w in TAUS:
                        if tau == 0:
                            pe.wait_ge(sem("rw_hats"), 1)
                        for q, src in enumerate((PJ[:, T_V:T_V + RP], BT[:], KT[:], AR[:, 0])):
                            bank = bA.open()
                            for j in range(RP):
                                ins = tr(bank[0:w, j * P:(j + 1) * P], src[:, j, t0:t0 + w], con("ident", P))
                            tok_freed = bA.close(ins)
                        for heads in SCORE_HEADS:
                            bank = bV.open()
                            for i, h in enumerate(heads):
                                j, p = hp(h)
                                for c, tc in PARTS[tau]:
                                    for q, lhs in enumerate((BH, KH)):
                                        o = 256 * i + 128 * q
                                        ins = mm(bank[c, o:o + 128].rearrange("p (x t) -> p x t", x=2), lhs[p, j, tc:tc + CH],
                                                 AR[p, :, j, tc:tc + CH], start=True, stop=True)
                            am_freed = bV.close(ins)
                            if heads[-1] in (3, 5):
                                yield
                        pe.wait_ge(*am_freed)
                        def six(f, last=None):
                            bank = bV.open()
                            for h in range(RW_H):
                                for c, _ in PARTS[tau]:
                                    lhs, rhs = f(c, h)
                                    ins = mm(bank[c, h * CH:(h + 1) * CH], lhs, rhs, start=True, stop=True)
                            return bV.close(ins, last)

                        f = six(lambda c, h: (AM[c, h, 0], CON[c, CC["ident"] + c.start:CC["ident"] + c.stop]),
                                (sem("rw_t0"), tau + 1))
                        yield
                        pe.wait_ge(*f)
                        pe.wait_ge(sem("rw_tt"), tau + 1)
                        levels = LEVELS[tau]
                        for lev in range(1, levels):
                            f = six(lambda c, h: (AM[c, h, 0], Tn[c, h]))
                            yield
                            pe.wait_ge(*f)
                            if lev < levels - 1:
                                six(lambda c, h: (Tt[c, h], Yb[c, h]))
                            f = six(lambda c, h: (Yb[c, h], Tt[c, h]))
                            yield
                            pe.wait_ge(*f)
                        pe.wait_ge(*tok_freed)
                        bank = bA.open()
                        for h in range(RW_H):
                            for c, _ in PARTS[tau]:
                                ins = mm(bank[c, h * HD:(h + 1) * HD], AM[c, h, 2], TK[c, 0, h * HD:(h + 1) * HD],
                                         start=True, stop=True)
                        f = bA.close(ins)
                        bank = bA.open()
                        for c, tc in PARTS[tau]:
                            if tc > t0:
                                rt.after(ins)
                            for h in range(RW_H):
                                j, p = hp(h)
                                o = j * P + tc - t0
                                ins = mm(bank[p, o:o + CH], TK[c, 3, h * HD:(h + 1) * HD], Tt[c, h], start=True, stop=True)
                        bA.close(ins)
                        yield
                        pe.wait_ge(*f)
                        bank = bA.open()
                        for h in range(RW_H):
                            for c, _ in PARTS[tau]:
                                ins = mm(bank[c, h * HD:(h + 1) * HD], Tt[c, h], RB[c, h * HD:(h + 1) * HD],
                                         start=True, stop=True)
                        f = bA.close(ins)
                        yield
                        pe.wait_ge(*f)
                        if tau:
                            pe.wait_ge(sem("rw_y"), tau)
                        if tau < 2:
                            for half in range(2):
                                c, s = 2 * tau + half, slice(64 * half, 64 * half + 64)
                                bank = bV.open()
                                pe.wait_ge(sem("rw_z"), c + 1)
                                for h in EVEN_ODD(RW_H):
                                    j, p = hp(h)
                                    ins = mm(bank[s, h * HD:(h + 1) * HD], WT[p, j, s], Z[p, c % 2, j], start=True, stop=True)
                                    if h == RW_H - 2:
                                        rt.after(ins)
                                f = bV.close(ins)
                                for h in range(RW_H):
                                    j, p = hp(h)
                                    ins = mm(psY[p, j * P + 64 * half:j * P + 64 * half + 64], Z[p, c % 2, j],
                                             AR[p, 1, j, t0 + 64 * half:t0 + 64 * half + 64],
                                             start=(half == 0 and j == 0), stop=False, skip_group_check=True)
                                if half:
                                    rt.after(ins)
                                yield
                                pe.wait_ge(*f)
                                bank = bV.open()
                                for h in range(RW_H):
                                    j, p = hp(h)
                                    mm(bank[p, j * HD:(j + 1) * HD], TK[s, 1, h * HD:(h + 1) * HD],
                                       U[s, h * HD:(h + 1) * HD], start=(j == 0), stop=False, skip_group_check=True)
                                for h in range(RW_H):
                                    j, p = hp(h)
                                    ins = mm(bank[p, j * HD:(j + 1) * HD], TK[s, 2, h * HD:(h + 1) * HD],
                                             TK[s, 0, h * HD:(h + 1) * HD], start=False, stop=True, skip_group_check=True)
                                bV.close(ins, (sem("rw_z"), c + 2))
                                yield
                        else:
                            pe.wait_ge(sem("rw_state"), 16)
                            bank = bA.open()
                            for h, s in PAIRED[:RW_H * DB]:
                                j, p = hp(h)
                                ins = mm(bank[p, j * NS + 8 * s:j * NS + 8 * s + 8], ZS[p, j, s],
                                         WT[p, j, 8 * s:8 * s + 8], start=True, stop=True)
                            f = bA.close(ins)
                            for h, s in PAIRED[:RW_H * DB]:
                                j, p = hp(h)
                                ins = mm(psY[p, j * P + 8 * s:j * P + 8 * s + 8], ZS[p, j, s],
                                         AR[p, 1, j, t0 + 8 * s:t0 + 8 * s + 8],
                                         start=(s == 0 and j == 0), stop=False, skip_group_check=True)
                            rt.after(ins)
                            yield
                            pe.wait_ge(*f)
                            bank = bV.open()
                            for j in range(RP):
                                ins = tr(bank[0:NS, j * P:(j + 1) * P], GT[:, j], con("ident", P))
                            f = bV.close(ins)
                            yield
                            pe.wait_ge(*f)
                        for c, tc in PARTS[tau]:
                            if tc > t0:
                                rt.after(ins)
                            for h in range(RW_H):
                                j, p = hp(h)
                                o = j * P + tc - t0
                                mm(psY[p, o:o + CH], U[c, h * HD:(h + 1) * HD], AM[c, h, 1],
                                   start=False, stop=False, skip_group_check=True)
                                ins = mm(psY[p, o:o + CH], TK[c, 0, h * HD:(h + 1) * HD], AM[c, h, 3],
                                         start=False, stop=True, skip_group_check=True)
                        ins.then_inc(sem("rw_y_full"), 1)
                        yield
                        if tau == 2:
                            for j in range(RP):
                                bank = bV.open()
                                pe.wait_ge(sem("rw_spread_u"), j + 1)
                                pe.wait_ge(sem("rw_spread_v"), j + 1)
                                for h in (2 * j, 2 * j + 1):
                                    _, p = hp(h)
                                    mm(bank[p, :], TK[0:NS, 1, h * HD:(h + 1) * HD], UX[0:NS, 0, h % 2].rearrange("p s v -> p (s v)"),
                                       start=True, stop=False, skip_group_check=True)
                                    ins = mm(bank[p, :], TK[0:NS, 2, h * HD:(h + 1) * HD], UX[0:NS, 1, h % 2].rearrange("p s v -> p (s v)"),
                                             start=False, stop=True, skip_group_check=True)
                                bV.close(ins)
                                yield
                    pe.wait_ge(sem("rw_y"), 3)
                    for j in range(RP):
                        bank = bV.open()
                        bV.close(mm(bank[:, 0:TOK], con("ones64", P), YT[:, j], start=True, stop=True))
                    yield
                    pe.wait_ge(sem("rw_gsq"), 1)
                    for j in range(RP):
                        bank = bV.open()
                        bV.close(mm(bank[:, 0:TOK], con("ones64", P), N3[:, j], start=True, stop=True))
                    yield

                def rw_act(act, A, fA):
                    activation = nc.scalar.activation

                    act.wait_ge(sem("rw_xs"), 1)
                    A.do(activation(TH[:], PJ[0:64, T_WA], ACT.Tanh), sem("rw_tanh"))
                    act.wait_ge(sem("rw_xs"), 2)
                    A.do(activation(SGD[:], PJ[:, T_G], ACT.Sigmoid), sem("rw_gd"))
                    yield
                    for j in range(RP):
                        bank = fA.take()
                        A.do(activation(SW[:, j], bank[:, 0:TOK], ACT.Sigmoid, bias=pcol("w0", j)), sem("rw_low"))
                    for j in range(RP):
                        bank = fA.take()
                        A.do(activation(AA[:, j], bank[:, 0:TOK], ACT.Sigmoid, bias=pcol("a0", j)), sem("rw_low"))
                    yield
                    act.wait_ge(sem("rw_kk0"), 1)
                    A.do(activation(KKS[:], KK[:], ACT.Square), sem("rw_sq"))
                    for j in range(RP):
                        bank = fA.take()
                        A.do(activation(gg(j), bank[:, 0:TOK], ACT.Copy), sem("rw_low"))
                    yield
                    act.wait_ge(sem("rw_n2"), 1)
                    rsqrt(A, KKS[:], sem("rw_root"))
                    act.wait_ge(sem("rw_b"), 1)
                    A.do(activation(EX[:, 0], BB[:], ACT.Exp), sem("rw_exp"))
                    A.do(activation(EX[:, 1], BB[:], ACT.Exp, scale=-1.0), sem("rw_exp"))
                    act.wait_ge(sem("rw_b"), 2)
                    A.do(activation(BP[:], BP[:], ACT.Exp), sem("rw_exp"))
                    act.wait_ge(sem("rw_be"), 1)
                    A.do(activation(SW[:], SW[:], ACT.Exp), sem("rw_exp"))
                    yield
                    yield
                    for tau, t0, w in TAUS:
                        for q in range(4):
                            bank = fA.take()
                            if q == 0:
                                act.wait_ge(sem("rw_hats"), 1)
                            A.do(activation(TK[0:w, q], bank[0:w, 0:RW_W], ACT.Copy), sem("bankA_free"))
                        for _ in range(3 + 2 * (LEVELS[tau] - 1)):
                            yield
                        bank = fA.take()
                        A.do(activation(RB[0:w], bank[0:w, 0:RW_W], ACT.Copy), sem("bankA_free"))
                        bank = fA.take()
                        A.do(activation(WT[:, :, 0:w], bank[:, 0:RW_W].rearrange("p (j t) -> p j t", t=P)[:, :, 0:w], ACT.Copy),
                             sem("bankA_free"))
                        yield
                        bank = fA.take()
                        A.do(activation(U0[0:w], bank[0:w, 0:RW_W], ACT.Copy), sem("bankA_free"))
                        yield
                        if tau == 2:
                            bank = fA.take()
                            A.do(activation(GT[:], bank[:, 0:RP * NS].rearrange("p (j t) -> p j t", t=NS), ACT.Copy), sem("bankA_free"))
                            yield
                            yield
                        else:
                            for _ in range(4):
                                yield
                        act.wait_ge(sem("rw_y_full"), tau + 1)
                        A.do(activation(YT[:, :, t0:t0 + w], psY[:, 0:RW_W].rearrange("p (j t) -> p j t", t=P)[:, :, 0:w], ACT.Copy),
                             sem("rw_y"))
                        yield
                    for _ in range(RP):
                        yield
                    act.wait_ge(sem("rw_yc"), 1)
                    A.do(activation(N3[:], N2[:], ACT.Square), sem("rw_gsq"))
                    yield
                    act.wait_ge(sem("rw_gvar"), 1)
                    rsqrt(A, N4[:], sem("rw_gsd"))
                    yield
                    act.wait_ge(sem("rw_m"), 1)
                    act.wait_ge(sem("proj_ready"), NPROJ)
                    A.do(activation(XH[:, 0:RP], N2[:], ACT.Copy), sem("rw_mh"))

                def rw_vec(vec, V, fV):
                    tt, ts, stt = nc.vector.tensor_tensor, nc.vector.tensor_scalar, nc.vector.scalar_tensor_tensor
                    copy = nc.vector.tensor_copy
                    pj = PJ[:, 0:NRW]

                    vec.wait_ge(sem("proj_ready"), NRW)
                    vec.wait_ge(sem("rw_shift"), 16)
                    V.do(tt(DF[:, :, 1:SEQ], pj[:, :, 0:SEQ - 1], pj[:, :, 1:SEQ], ALU.subtract))
                    V.do(ts(DF[:, :, 0:1], pj[:, :, 0:1], -1.0, None, ALU.mult))
                    df, pp = t88(DF[:, :, SEQ:TOK]), t88(pj[:, :, SEQ:TOK])
                    V.do(tt(df[:, :, :, 1:DS], pp[:, :, :, 0:DS - 1], pp[:, :, :, 1:DS], ALU.subtract))
                    V.do(tt(df[:, :, :, 0], SH[:], pp[:, :, :, 0], ALU.subtract))
                    vec.wait_ge(sem("rw_shift_kept"), 2)
                    V.settle()
                    for i in (T_WA, T_G, 0, 1, 2, 3, 4, 5, 6, 7, 8):
                        V.do(stt(PJ[:, i], DF[:, i], pcol("mu", i), PJ[:, i], ALU.mult, ALU.add), sem("rw_xs"))
                    V.settle()
                    r, k, v = PJ[:, T_R:T_R + RP], PJ[:, T_K:T_K + RP], PJ[:, T_V:T_V + RP]
                    for j in range(RP):
                        V.do(ts(KK[:, j], k[:, j], pcol("k_k", j), None, ALU.mult))
                    V.mark(sem("rw_kk0"))
                    yield
                    vec.wait_ge(sem("rw_low"), 3)
                    V.do(ts(SW[:], SW[:], -float(np.exp(-0.5)), None, ALU.mult))
                    V.settle()
                    for j in range(RP):
                        V.do(nc.vector.tensor_tensor_scan(BB[:, j], con("reset", TOK), SW[:, j], 0.0, ALU.mult, ALU.add))
                    V.mark(sem("rw_b"))
                    V.do(tt(BP[:], BB[:], SW[:], ALU.subtract), sem("rw_b"))
                    V.settle()
                    ends = BB[:, :, CH - 1:SEQ:CH]
                    V.do(tt(SW[:, :, 0:SEQ].rearrange("p a (c t) -> p a c t", t=CH), ends.unsqueeze(3).to_broadcast([P, RP, NCH, CH]),
                            BB[:, :, 0:SEQ].rearrange("p a (c t) -> p a c t", t=CH), ALU.subtract))
                    ends8 = BB[:, :, SEQ + DS - 1:TOK:DS]
                    V.do(tt(t88(SW[:, :, SEQ:TOK]), ends8.unsqueeze(3).to_broadcast([P, RP, DB, DS]), t88(BB[:, :, SEQ:TOK]), ALU.subtract))
                    V.mark(sem("rw_be"))
                    yield
                    vec.wait_ge(sem("rw_low"), 6)
                    for j in range(RP):
                        V.do(ts(OMK[:, j:j + 1], pcol("k_a", j), -1.0, 1.0, ALU.mult, ALU.add))
                    V.settle()
                    for j in range(RP):
                        V.do(ts(BT[:, j], AA[:, j], pcol("k_a", j), OMK[:, j:j + 1], ALU.mult, ALU.add))
                    V.settle()
                    V.do(tt(k, k, BT[:], ALU.mult))
                    V.settle()
                    for j in range(RP):
                        bank = fV.take()
                        if j == 0:
                            vec.wait_ge(sem("rw_sq"), 1)
                        V.do(ts(KKS[:, j], bank[:, 0:TOK], 64.0, 1e-24, ALU.mult, ALU.max), sem("bankV_free"))
                    V.mark(sem("rw_n2"))
                    yield
                    vec.wait_ge(sem("rw_root"), 1)
                    V.do(tt(KK[:], KK[:], KKS[:], ALU.mult))
                    V.settle()
                    V.do(tt(BT[:], KK[:], AA[:], ALU.mult))
                    vec.wait_ge(sem("rw_exp"), 4)
                    V.do(stt(AR[:, 0], KK[:], -1.0, BP[:], ALU.mult, ALU.mult))
                    V.settle()
                    V.do(tt(BH[:], BT[:], EX[:, 1], ALU.mult))
                    V.settle()
                    V.do(tt(BT[:], BT[:], SW[:], ALU.mult))
                    V.do(tt(KH[:], k, EX[:, 1], ALU.mult))
                    V.do(tt(AR[:, 1], r, EX[:, 0], ALU.mult))
                    V.do(tt(KT[:], k, SW[:], ALU.mult))
                    V.do(copy(PC[:, :, 0:NCH], EX[:, 0, :, CH - 1:SEQ:CH]))
                    V.do(copy(PC[:, :, NCH:NCH + DB], EX[:, 0, :, SEQ + DS - 1:TOK:DS]))
                    for j in range(RP):
                        V.do(stt(BB[:, j], r[:, j], pcol("r_k", j), k[:, j], ALU.mult, ALU.mult))
                    V.mark(sem("rw_rkk"))
                    V.do(nc.vector.memset(Z[:, 0], 0.0), sem("rw_z"))
                    yield
                    for j in range(RP):
                        bank = fV.take()
                        V.do(stt(BON[:, j], bank[:, 0:TOK], 64.0, v[:, j], ALU.mult, ALU.mult), sem("bankV_free"))
                    V.mark(sem("rw_hats"))
                    yield
                    for tau, t0, w in TAUS:
                        mask = con("mask_p" if tau < 2 else "mask_s", P, rows=w).unsqueeze(1)
                        for heads in SCORE_HEADS:
                            bank = fV.take()
                            n = len(heads)
                            V.do(tt(AM[0:w, heads[0]:heads[-1] + 1:2].rearrange("p h b t -> p h (b t)").rearrange("p h (q x) -> p h q x", q=2),
                                    bank[0:w, 0:256 * n].rearrange("p (h q x) -> p h q x", h=n, q=2),
                                    mask.unsqueeze(1).to_broadcast([w, n, 2, P]), ALU.mult), sem("bankV_free"))
                            if heads[-1] == 3:
                                yield
                        V.mark(sem("rw_am"))
                        yield

                        def six():
                            return fV.take()[0:w, 0:RW_H * CH].rearrange("p (h t) -> p h t", t=CH)

                        def level(i):
                            return con("level", CH, rows=w, at=i * CH).unsqueeze(1).to_broadcast([w, RW_H, CH])

                        V.do(tt(Tn[0:w], six(), level(0), ALU.mult))
                        V.settle()
                        V.do(tt(Tn[0:w], Tn[0:w], con("ident64", CH, rows=w).unsqueeze(1).to_broadcast([w, RW_H, CH]), ALU.add),
                             sem("rw_t0"))
                        yield
                        levels = LEVELS[tau]
                        for lev in range(1, levels):
                            V.do(tt(Yb[0:w], six(), level(lev), ALU.mult), sem("bankV_free"))
                            V.settle()
                            yield
                            for T in ((Tn, Tt) if lev < levels - 1 else (Tt,)):
                                if T is Tt and lev == 1:
                                    vec.wait_ge(sem("rw_tt"), tau + 1)
                                V.do(tt(T[0:w], six(), T[0:w], ALU.add), sem("bankV_free"))
                            V.settle()
                            yield
                        yield
                        yield
                        if tau < 2:
                            for half in range(2):
                                c, s = 2 * tau + half, slice(64 * half, 64 * half + 64)
                                V.do(tt(ZP[:], Z[:, c % 2], PC[:, :, c:c + 1].to_broadcast([P, RP, HD]), ALU.mult))
                                bank = fV.take()
                                V.do(tt(U[s], bank[s, 0:RW_W], U0[s], ALU.add), sem("bankV_free"))
                                yield
                                bank = fV.take()
                                V.settle()
                                V.do(tt(Z[:, (c + 1) % 2], bank[:, 0:RP * HD].rearrange("p (j v) -> p j v", v=HD), ZP[:], ALU.add),
                                     sem("rw_z"))
                                V.settle()
                                yield
                            yield
                        else:
                            yield
                            bank = fV.take()
                            V.do(tt(U[0:NS], bank[0:NS, 0:RW_W], U0[0:NS], ALU.add), sem("bankV_free"))
                            V.mark(sem("rw_u8"))
                            yield
                            yield
                            seqmask = con("seqmask", DB, rows=NS).unsqueeze(2).to_broadcast([NS, DB, HD])
                            for j in range(RP):
                                for h in (2 * j, 2 * j + 1):
                                    V.do(tt(UX[0:NS, 0, h % 2], U[0:NS, h * HD:(h + 1) * HD].unsqueeze(1).to_broadcast([NS, DB, HD]),
                                            seqmask, ALU.mult), sem("rw_spread_u") if h % 2 else None)
                                V.do(tt(ZS[:, j], ZS[:, j], PC[:, j, NCH:NCH + DB].unsqueeze(2).to_broadcast([P, DB, HD]), ALU.mult))
                                bank = fV.take()
                                V.settle()
                                V.do(tt(ZS[:, j], bank[:].rearrange("p (s v) -> p s v", v=HD), ZS[:, j], ALU.add), sem("bankV_free"))
                                V.mark(sem("rw_zs"))
                                yield
                    for j in range(RP):
                        bank = fV.take()
                        V.do(tt(N2[:, j], YT[:, j], bank[:, 0:TOK], ALU.subtract), sem("bankV_free"))
                    V.mark(sem("rw_yc"))
                    yield
                    for j in range(RP):
                        bank = fV.take()
                        V.do(ts(N4[:, j], bank[:, 0:TOK], GN_EPS, None, ALU.add), sem("bankV_free"))
                    V.mark(sem("rw_gvar"))
                    yield
                    vec.wait_ge(sem("rw_gsd"), 1)
                    V.do(tt(N2[:], N2[:], N4[:], ALU.mult))
                    V.settle()
                    for j in range(RP):
                        V.do(ts(N2[:, j], N2[:, j], pcol("gn_g", j), pcol("gn_b", j), ALU.mult, ALU.add))
                    V.settle()
                    V.do(tt(N2[:], N2[:], BON, ALU.add))
                    V.settle()
                    for j in range(RP):
                        V.do(tt(N2[:, j], N2[:, j], gg(j), ALU.mult))
                    V.mark(sem("rw_m"))
                    vec.wait_ge(sem("rw_mh"), 1)
                    V.do(tt(XL[:, 0:RP], N2[:], XH[:, 0:RP].bitcast(F32), ALU.subtract))
                    for j in range(RP):
                        V.mark(sem("mixed"))

                def rw_pool(pool, G):
                    pool.wait_ge(sem("proj_ready"), NRW)
                    G.do(nc.gpsimd.tensor_copy(SHO[:, :, 0:1], PJ[:, 0:NRW, SEQ - 1:SEQ]), sem("rw_shift_kept"))
                    G.do(nc.gpsimd.tensor_copy(SHO[:, :, 1:1 + DB], PJ[:, 0:NRW, SEQ + DS - 1:TOK:DS]), sem("rw_shift_kept"))
                    for tau, t0, w in TAUS:
                        pool.wait_ge(sem("rw_am"), tau + 1)
                        lev = con("level0t", CH, rows=w).unsqueeze(1).to_broadcast([w, RW_H, CH])
                        G.do(nc.gpsimd.tensor_tensor(Tt[0:w], AM[0:w, :, 0], lev, ALU.mult))
                        G.settle()
                        G.do(nc.gpsimd.tensor_tensor(Tt[0:w], Tt[0:w],
                                                     con("ident64", CH, rows=w).unsqueeze(1).to_broadcast([w, RW_H, CH]), ALU.add),
                             sem("rw_tt"))
                    seqmask = con("seqmask", DB, rows=NS).unsqueeze(2).to_broadcast([NS, DB, HD])
                    for j in range(RP):
                        pool.wait_ge(*((sem("rw_u8"), 1) if j == 0 else (sem("rw_zs"), j)))
                        for h in (2 * j, 2 * j + 1):
                            G.do(nc.gpsimd.tensor_tensor(UX[0:NS, 1, h % 2],
                                                         TK[0:NS, 0, h * HD:(h + 1) * HD].unsqueeze(1).to_broadcast([NS, DB, HD]),
                                                         seqmask, ALU.mult), sem("rw_spread_v") if h % 2 else None)

                def rw_stores(sp):
                    sp.wait_ge(sem("rw_shift_kept"), 2)
                    sp.dma_start(of_layer(o_shift), whole(SHO[:])).then_inc(sem("stored"), 16)
                    sp.wait_ge(sem("rw_z"), NCH + 1)
                    sp.dma_start(of_layer(o_rwp), Z[:, 0].rearrange("p j v -> p (j v)")).then_inc(sem("stored"), 16)
                    sp.wait_ge(sem("rw_zs"), RP)
                    sp.dma_start(of_layer(o_rws), ZS[:].rearrange("p j s v -> p (j s v)")).then_inc(sem("stored"), 16)

                def gl_pe(pe, bV, bA, rt):
                    mm, tr = nc.tensor.matmul, nc.tensor.transpose
                    pe.wait_ge(sem("gl_start"), 1)
                    for j in range(GP):
                        bank = bV.open()
                        bV.close(mm(bank[:, 0:TOK], A2G[:, j], PJ[0:16, T_LOW], start=True, stop=True))
                    yield
                    for tau, t0, w in TAUS:
                        bank = bA.open()
                        for j in range(3):
                            ins = tr(bank[0:w, j * P:(j + 1) * P], PJ[:, T_GV + j, t0:t0 + w], con("ident", P))
                        bA.close(ins)
                    yield
                    yield
                    pe.wait_ge(sem("gl_hats"), 1)
                    for tau, t0, w in TAUS:
                        bank = bA.open()
                        for j in range(GP):
                            ins = tr(bank[0:w, j * P:(j + 1) * P], KE[:, j, t0:t0 + w], con("ident", P))
                        tok_freed = bA.close(ins)
                        bank = bV.open()
                        for h in EVEN_ODD(GH):
                            j, p = hp(h)
                            for c, tc in PARTS[tau]:
                                ins = mm(bank[c, h * CH:(h + 1) * CH], KI[p, j, tc:tc + CH], QD[p, j, tc:tc + CH],
                                         start=True, stop=True)
                            if h == GH - 2:
                                rt.after(ins)
                        att_freed = bV.close(ins)
                        yield
                    pe.wait_ge(*tok_freed)
                    for c in range(NCH):
                        s = slice(64 * (c % 2), 64 * (c % 2) + 64)
                        bank = bV.open()
                        for h in range(GH):
                            j, p = hp(h)
                            ins = mm(bank[p, j * DV:(j + 1) * DV], KET[s, c // 2, h * 64:(h + 1) * 64],
                                     VG[s, c // 2, h * DV:(h + 1) * DV], start=True, stop=True)
                        bV.close(ins, (sem("gl_state"), c + 2))
                    yield
                    pe.wait_ge(sem("gl_state"), NCH + 1)
                    pe.wait_ge(*att_freed)
                    pe.wait_ge(sem("gl_state0"), 16)
                    for h in range(GH):
                        j, p = hp(h)
                        bank = bA.open()
                        for half in range(2):
                            if half:
                                rt.after(ins)
                            for tau in range(3 - half):
                                c, tc = PARTS[tau][half]
                                ins = mm(bank[0:DV, tc:tc + CH], VG[c, tau, h * DV:(h + 1) * DV], ATG[c, tau, h],
                                         start=(tau == 0 and half == 0), stop=False, skip_group_check=True)
                        if h % 2 == 0:
                            rt.after(ins)
                        for c in range(1, NCH):
                            mm(bank[0:DV, c * CH:(c + 1) * CH], SP[p, c, j], QD[p, j, c * CH:(c + 1) * CH],
                               start=False, stop=False, skip_group_check=True)
                        for s in range(DB):
                            ins = mm(bank[0:DV, SEQ + DS * s:SEQ + DS * (s + 1)], S0[p, j, s],
                                     QD[p, j, SEQ + DS * s:SEQ + DS * (s + 1)], start=False, stop=True, skip_group_check=True)
                        bA.close(ins)
                        if h % 2:
                            yield
                    pe.wait_ge(sem("gl_kx"), 1)
                    for b in range(DB // 2):
                        bank = bV.open()
                        for s in (2 * b, 2 * b + 1):
                            for h in range(GH):
                                j, p = hp(h)
                                o = (s % 2) * GP * DV + j * DV
                                ins = mm(bank[p, o:o + DV], KX[:, s, h * 64:(h + 1) * 64], VG[0:NS, 2, h * DV:(h + 1) * DV],
                                         start=True, stop=True)
                        bV.close(ins)
                    yield
                    pe.wait_ge(sem("gl_sq"), 1)
                    for h in range(GH):
                        bank = bV.open()
                        bV.close(mm(bank[0:DV, 0:TOK], CON[0:DV, CC["ones96"]:CC["ones96"] + DV], GN[0:DV, h], start=True, stop=True))
                    yield

                def gl_act(act, A, fA):
                    activation = nc.scalar.activation
                    act.wait_ge(sem("gl_start"), 1)
                    yield
                    act.wait_ge(sem("gl_abs"), 1)
                    A.do(activation(GE[:], GE[:], ACT.Exp, scale=-1.0))
                    A.settle()
                    A.do(activation(GE[:], GE[:], ACT.Ln, bias=1.0), sem("gl_log"))
                    for tau, t0, w in TAUS:
                        bank = fA.take()
                        A.do(activation(VG[0:w, tau], bank[0:w, 0:GW], ACT.Copy), sem("bankA_free"))
                    yield
                    act.wait_ge(sem("gl_b"), 1)
                    A.do(activation(QD[:], GB[:], ACT.Exp, scale=1.0 / 16), sem("gl_exp"))
                    A.do(activation(KI[:], GB[:], ACT.Exp, scale=-1.0 / 16), sem("gl_exp"))
                    act.wait_ge(sem("gl_b"), 2)
                    A.do(activation(KE[:], GE[:], ACT.Exp, scale=1.0 / 16), sem("gl_exp"))
                    yield
                    for tau, t0, w in TAUS:
                        bank = fA.take()
                        A.do(activation(KET[0:w, tau], bank[0:w, 0:GP * P], ACT.Copy), sem("bankA_free"))
                        yield
                    yield
                    for h in range(GH):
                        bank = fA.take()
                        A.do(activation(OT[0:DV, h], bank[0:DV, 0:TOK], ACT.Copy), sem("bankA_free"))
                        if h == 1:
                            yield
                    A.mark(sem("gl_ot"))
                    yield
                    act.wait_ge(sem("gl_out"), 1)
                    A.do(activation(GN[0:DV], OT[0:DV], ACT.Square), sem("gl_sq"))
                    A.do(activation(PJ[0:DV, T_GR:T_GR + GH], PJ[0:DV, T_GR:T_GR + GH], ACT.Silu), sem("gl_gate"))
                    yield
                    yield
                    act.wait_ge(sem("gl_var"), 1)
                    rsqrt(A, GN[0:DV], sem("gl_sd"))
                    yield

                def gl_vec(vec, V, fV):
                    tt, ts, stt = nc.vector.tensor_tensor, nc.vector.tensor_scalar, nc.vector.scalar_tensor_tensor
                    copy = nc.vector.tensor_copy
                    V.mark(sem("gl_start"))
                    for j in range(GP):
                        bank = fV.take()
                        V.do(ts(GZ[:, j], bank[:, 0:TOK], pcol("gla_b", j), None, ALU.add), sem("bankV_free"))
                    V.settle()
                    V.do(stt(GE[:], GZ[:], -1.0, GZ[:], ALU.mult, ALU.max), sem("gl_abs"))
                    yield
                    vec.wait_ge(sem("gl_log"), 1)
                    V.do(stt(GZ[:], GZ[:], 0.0, GE[:], ALU.min, ALU.subtract))
                    V.settle()
                    for j in range(GP):
                        V.do(nc.vector.tensor_tensor_scan(GB[:, j], con("reset", TOK), GZ[:, j], 0.0, ALU.mult, ALU.add))
                    V.mark(sem("gl_b"))
                    ends, ends8 = GB[:, :, CH - 1:SEQ:CH], GB[:, :, SEQ + DS - 1:TOK:DS]
                    V.do(tt(GE[:, :, 0:SEQ].rearrange("p a (c t) -> p a c t", t=CH), ends.unsqueeze(3).to_broadcast([P, GP, NCH, CH]),
                            GB[:, :, 0:SEQ].rearrange("p a (c t) -> p a c t", t=CH), ALU.subtract))
                    V.do(tt(t88(GE[:, :, SEQ:TOK]), ends8.unsqueeze(3).to_broadcast([P, GP, DB, DS]), t88(GB[:, :, SEQ:TOK]), ALU.subtract))
                    V.mark(sem("gl_b"))
                    yield
                    vec.wait_ge(sem("gl_exp"), 3)
                    V.do(copy(GPC[:, :, 0:NCH], QD[:, :, CH - 1:SEQ:CH]))
                    V.do(copy(GPC[:, :, NCH:NCH + DB], QD[:, :, SEQ + DS - 1:TOK:DS]))
                    V.do(tt(KI[:], PJ[:, T_GK:T_GK + GP], KI[:], ALU.mult))
                    V.do(tt(KE[:], PJ[:, T_GK:T_GK + GP], KE[:], ALU.mult))
                    V.settle()
                    V.do(stt(QD[:], PJ[:, T_GQ:T_GQ + GP], DK ** -0.5, QD[:], ALU.mult, ALU.mult))
                    V.do(nc.vector.memset(SP[:, 0], 0.0))
                    V.mark(sem("gl_hats"))
                    yield
                    for tau, t0, w in TAUS:
                        bank = fV.take()
                        m = con("mask_p" if tau < 2 else "mask_s", CH, rows=w, at=CH)
                        V.do(tt(ATG[0:w, tau], bank[0:w, 0:GH * CH].rearrange("p (h t) -> p h t", t=CH),
                                m.unsqueeze(1).to_broadcast([w, GH, CH]), ALU.mult), sem("bankV_free"))
                        yield
                    V.mark(sem("gl_state"))
                    for c in range(NCH):
                        bank = fV.take()
                        V.settle()
                        V.do(stt(SP[:, c + 1, 0], SP[:, c, 0], GPC[:, 0, c:c + 1], bank[:, 0:DV], ALU.mult, ALU.add))
                        V.do(stt(SP[:, c + 1, 1], SP[:, c, 1], GPC[:, 1, c:c + 1], bank[:, DV:2 * DV], ALU.mult, ALU.add),
                             sem("gl_state"))
                    yield
                    yield
                    yield
                    vec.wait_ge(sem("gl_ot"), 1)
                    V.do(tt(S0[:], S0[:], GPC[:, :, NCH:NCH + DB].unsqueeze(3).to_broadcast([P, GP, DB, DV]), ALU.mult))
                    V.settle()
                    for b in range(DB // 2):
                        bank = fV.take()
                        V.do(tt(S0[:, :, 2 * b:2 * b + 2], bank[:, 0:4 * DV].rearrange("p (s j v) -> p j s v", s=2, j=2),
                                S0[:, :, 2 * b:2 * b + 2], ALU.add), sem("bankV_free"))
                    V.mark(sem("gl_out"))
                    yield
                    for h in range(GH):
                        bank = fV.take()
                        V.do(ts(GN[0:DV, h], bank[0:DV, 0:TOK], NORM_EPS, None, ALU.add), sem("bankV_free"))
                    V.mark(sem("gl_var"))
                    yield
                    vec.wait_ge(sem("gl_sd"), 1)
                    V.do(tt(OT[0:DV], OT[0:DV], GN[0:DV], ALU.mult))
                    V.settle()
                    for h in range(GH):
                        V.do(stt(OT[0:DV, h], OT[0:DV, h], pcol("gla_g", h, 0, DV), PJ[0:DV, T_GR + h], ALU.mult, ALU.mult))
                    yield

                def gl_pool(pool, G):
                    pool.wait_ge(sem("gl_start"), 1)
                    pool.wait_ge(sem("proj_ready"), NPROJ)
                    for x in (XH, XL):
                        G.do(nc.gpsimd.tensor_scalar(x[64:P, RP:RP + GH], CON[64:P, 0:GH * TOK].rearrange("p (h t) -> p h t", t=TOK),
                                                     0.0, None, ALU.mult))
                    G.mark(sem("gl_zero"))
                    pool.wait_ge(sem("gl_state"), NCH + 1)
                    G.do(nc.gpsimd.tensor_tensor(KX[:], KET[0:NS, 2].unsqueeze(1).to_broadcast([NS, DB, GP * P]),
                                                 con("seqmask", DB, rows=NS).unsqueeze(2).to_broadcast([NS, DB, GP * P]), ALU.mult),
                         sem("gl_kx"))

                def mix_loads(sp):
                    sp.wait_ge(sem("ml_start"), 1)
                    sp.dma_start(SCV[:].rearrange("p a s t -> p (a s t)"), of_layer(st_conv)).then_inc(sem("ml_conv0"), 16)
                    sp.dma_start(M0[:], of_layer(st_m)).then_inc(sem("ml_m0"), 16)
                    sp.dma_start(S0[:].rearrange("p j s v -> p (j s v)"), of_layer(st_gla)).then_inc(sem("gl_state0"), 16)
                    sp.dma_start(C0[:, :, :, 0:HD].rearrange("p j s v -> p (j s) v"),
                                 st_c[at_layer].rearrange("l p (a v) -> p (l a) v", v=HD)).then_inc(sem("ml_c00"), 16)
                    sp.dma_start(N0[:].rearrange("p j s -> p (j s)"), of_layer(st_n)).then_inc(sem("ml_c00"), 16)

                def mix_stores(sp):
                    sp.wait_ge(sem("gl_state"), NCH + 1)
                    sp.dma_start(of_layer(o_glap), SP[:, NCH].rearrange("p j v -> p (j v)")).then_inc(sem("stored"), 16)
                    sp.wait_ge(sem("gl_out"), 1)
                    sp.dma_start(of_layer(o_glas), S0[:].rearrange("p j s v -> p (j s v)")).then_inc(sem("stored"), 16)
                    sp.wait_ge(sem("ml_m"), 1)
                    sp.dma_start(of_layer(o_m), MO[:]).then_inc(sem("stored"), 16)
                    sp.wait_ge(sem("ml_conv"), 1)
                    sp.dma_start(of_layer(o_conv), COV[:].rearrange("p a s t -> p (a s t)")).then_inc(sem("stored"), 16)
                    sp.wait_ge(sem("ml_prompt"), 1)
                    sp.dma_start(of_layer(o_cp).rearrange("p (j v) -> p j v", v=HD), CP[:, NCH, :, 0:HD]).then_inc(sem("stored"), 16)
                    sp.wait_ge(sem("ml_out"), 1)
                    sp.dma_start(of_layer(o_cs).rearrange("p (a v) -> p a v", v=HD),
                                 C0[:, :, :, 0:HD].rearrange("p j s v -> p (j s) v")).then_inc(sem("stored"), 16)
                    sp.dma_start(of_layer(o_np), NO[:].rearrange("p j s -> p (j s)")).then_inc(sem("stored"), 16)

                def ml_pe(pe, bV, bA, rt):
                    mm, tr = nc.tensor.matmul, nc.tensor.transpose
                    pe.wait_ge(sem("ml_start"), 1)
                    for tau, t0, w in TAUS:
                        bank = bA.open()
                        for j in range(MP):
                            ins = tr(bank[0:w, j * P:(j + 1) * P], PJ[:, T_MV + j, t0:t0 + w], con("ident", P))
                        vm_freed = bA.close(ins)
                    for _ in range(4):
                        yield
                    pe.wait_ge(sem("ml_rows"), 1)
                    bank = bV.open()
                    for tau, t0, w in TAUS:
                        for q, row in enumerate((CR, WJ)):
                            o = tau * 8 + 4 * q
                            ins = tr(bank[0:w, o:o + 4], row[:, t0:t0 + w], con("ident", 4, rows=4))
                    bV.close(ins)
                    for j in range(MP):
                        bank = bV.open()
                        bV.close(mm(bank[:, 0:TOK], con("pairsel", P, rows=4, at=j * P), E2[:], start=True, stop=True))
                    for j in range(MP):
                        bank = bA.open()
                        bA.close(mm(bank[:, 0:TOK], con("pairsel", P, rows=4, at=j * P), D1[:], start=True, stop=True))
                    yield
                    for tau, t0, w in TAUS:
                        bank = bV.open()
                        for h in range(MH):
                            for c, tc in PARTS[tau]:
                                ins = mm(bank[c, h * CH:(h + 1) * CH], con("headsel", CH, rows=4, at=h * CH), ER[:, tc:tc + CH],
                                         start=True, stop=True)
                        bV.close(ins)
                        bank = bV.open()
                        for h in EVEN_ODD(MH):
                            j, p = hp(h)
                            for c, tc in PARTS[tau]:
                                ins = mm(bank[c, h * CH:(h + 1) * CH], QK[p, 2 + j, tc:tc + CH], QK[p, j, tc:tc + CH],
                                         start=True, stop=True)
                            if h == MH - 2:
                                rt.after(ins)
                        bV.close(ins)
                        bank = bV.open()
                        for j in range(MP):
                            ins = tr(bank[0:w, j * P:(j + 1) * P], QK[:, 2 + j, t0:t0 + w], con("ident", P))
                        kw_freed = bV.close(ins)
                        yield
                    pe.wait_ge(*vm_freed)
                    pe.wait_ge(*kw_freed)
                    pe.wait_ge(sem("ml_ones"), 1)
                    for c in range(NCH):
                        s = slice(64 * (c % 2), 64 * (c % 2) + 64)
                        bank = bV.open()
                        for h in range(MH):
                            j, p = hp(h)
                            ins = mm(bank[p, j * P:(j + 1) * P], KW[s, c // 2, h * HD:(h + 1) * HD], VM[s, c // 2, h],
                                     start=True, stop=True)
                        bV.close(ins, (sem("ml_state"), c + 2))
                    yield
                    pe.wait_ge(sem("ml_state"), NCH + 1)
                    pe.wait_ge(sem("ml_c0"), 1)
                    for j in range(MP):
                        for part in (slice(64, 128), slice(0, 64)):
                            bank = bV.open()
                            for half in range(2):
                                if half:
                                    rt.after(ins)
                                for h in (2 * j, 2 * j + 1):
                                    _, p = hp(h)
                                    for tau in range(3 - half):
                                        c, tc = PARTS[tau][half]
                                        ins = mm(bank[p, tc:tc + CH], VM[c, tau, h, part], ST[c, tau, h],
                                                 start=(tau == 0 and half == 0), stop=False, skip_group_check=True)
                            rt.after(ins)
                            for c in range(1, NCH):
                                for h in (2 * j, 2 * j + 1):
                                    _, p = hp(h)
                                    mm(bank[p, c * CH:(c + 1) * CH], CP[p, c, j, part], QW[p, j, c * CH:(c + 1) * CH],
                                       start=False, stop=False, skip_group_check=True)
                            for s in range(DB):
                                for h in (2 * j, 2 * j + 1):
                                    _, p = hp(h)
                                    ins = mm(bank[p, SEQ + DS * s:SEQ + DS * (s + 1)], C0[p, j, s, part],
                                             QW[p, j, SEQ + DS * s:SEQ + DS * (s + 1)], start=False, stop=True, skip_group_check=True)
                            bV.close(ins)
                        yield
                    pe.wait_ge(sem("ml_vx"), 1)
                    for j in range(MP):
                        bank = bV.open()
                        for h in (2 * j, 2 * j + 1):
                            _, p = hp(h)
                            ins = mm(bank[p, :], KW[0:NS, 2, h * HD:(h + 1) * HD], VX[:, h].rearrange("p s v -> p (s v)"),
                                     start=True, stop=True)
                        bV.close(ins)
                        bank = bV.open()
                        for h in (2 * j, 2 * j + 1):
                            _, p = hp(h)
                            ins = mm(bank[p, 0:DB], KW[0:NS, 2, h * HD:(h + 1) * HD], con("seqmask", DB, rows=NS), start=True, stop=True)
                        bV.close(ins)
                    yield
                    pe.wait_ge(sem("ml_h"), 1)
                    for j in range(MP):
                        bank = bV.open()
                        bV.close(mm(bank[:, 0:TOK], con("ones64", P), HT[:, j], start=True, stop=True))
                    yield
                    pe.wait_ge(sem("ml_sq"), 1)
                    for j in range(MP):
                        bank = bV.open()
                        bV.close(mm(bank[:, 0:TOK], con("ones64", P), DD[:, j], start=True, stop=True))

                def ml_act(act, A, fA):
                    activation = nc.scalar.activation
                    act.wait_ge(sem("ml_start"), 1)
                    qk = PJ[:, T_MQK:T_MQK + 4]
                    A.do(activation(XP[:, :, CONV - 1:CW], qk[:, :, 0:SEQ], ACT.Copy))
                    xs = XP[:, :, CW:CN].rearrange("p a (s t) -> p a s t", t=CS)
                    for i in range(4):
                        A.do(activation(xs[:, i, :, CONV - 1:CS], s8(qk[:, i, SEQ:TOK]), ACT.Copy))
                    act.wait_ge(sem("ml_conv0"), 16)
                    for i in range(4):
                        A.do(activation(xs[:, i, :, 0:CONV - 1], SCV[:, i], ACT.Copy))
                    A.mark(sem("ml_xp"))
                    for tau, t0, w in TAUS:
                        bank = fA.take()
                        A.do(activation(VM[0:w, tau, :, 0:HD], bank[0:w, 0:MW].rearrange("p (h v) -> p h v", v=HD), ACT.Copy),
                             sem("bankA_free"))
                    yield
                    act.wait_ge(sem("ml_f"), 1)
                    A.do(activation(D0[:], D0[:], ACT.Exp, scale=-1.0))
                    A.settle()
                    A.do(activation(D0[:], D0[:], ACT.Ln, bias=1.0), sem("ml_log"))
                    act.wait_ge(sem("ml_m"), 1)
                    A.do(activation(E2[:], E2[:], ACT.Exp))
                    A.do(activation(WJ[:], WJ[:], ACT.Exp))
                    A.do(activation(D1[:], MM[:], ACT.Exp, scale=-1.0))
                    yield
                    yield
                    act.wait_ge(sem("ml_conv"), 1)
                    A.do(activation(QK[:, :, 0:SEQ], CV[:, :, 0:SEQ], ACT.Silu))
                    for i in range(4):
                        A.do(activation(s8(QK[:, i, SEQ:TOK]),
                                        CV[:, i, CW:CN].rearrange("p (s t) -> p s t", t=CS)[:, :, 0:DS], ACT.Silu))
                    A.mark(sem("ml_qk"))
                    yield
                    for j in range(MP):
                        bank = fA.take()
                        A.do(activation(EMB[:, j], bank[:, 0:TOK], ACT.Copy), sem("bankA_free"))
                    A.mark(sem("ml_emb"))
                    yield
                    for tau, t0, w in TAUS:
                        act.wait_ge(sem("ml_arg"), tau + 1)
                        A.do(activation(DW[0:w], DW[0:w], ACT.Exp), sem("ml_dw"))
                        yield
                    A.do(activation(PJ[:, T_MO:T_MO + MP], PJ[:, T_MO:T_MO + MP], ACT.Sigmoid), sem("ml_gate"))
                    for _ in range(4):
                        yield
                    act.wait_ge(sem("ml_hc"), 1)
                    A.do(activation(DD[:], HT[:], ACT.Square), sem("ml_sq"))
                    yield
                    act.wait_ge(sem("ml_var"), 1)
                    rsqrt(A, DD[:], sem("ml_sd"))

                def ml_vec(vec, V, fV):
                    tt, ts, stt = nc.vector.tensor_tensor, nc.vector.tensor_scalar, nc.vector.scalar_tensor_tensor
                    copy = nc.vector.tensor_copy
                    vec.wait_ge(sem("stored"), 48)
                    vec.wait_ge(sem("proj_ready"), NPROJ)
                    V.do(nc.vector.memset(XP[:, :, 0:CONV - 1], 0.0))
                    V.do(nc.vector.memset(CP[:, 0], 0.0))
                    V.mark(sem("ml_start"))
                    V.do(ts(IG[:], PJ[32:36, T_LOW], pcol("i_b", 0, 32, 36), None, ALU.add))
                    V.do(ts(FZ[:], PJ[64:68, T_LOW], pcol("f_b", 0, 64, 68), None, ALU.add))
                    V.settle()
                    V.do(stt(D0[:], FZ[:], -1.0, FZ[:], ALU.mult, ALU.max), sem("ml_f"))
                    yield
                    vec.wait_ge(sem("ml_log"), 1)
                    V.do(stt(LF[:], FZ[:], 0.0, D0[:], ALU.min, ALU.subtract))
                    V.do(copy(D1[:], IG[:]))
                    V.settle()
                    first = slice(SEQ, TOK, DS)
                    vec.wait_ge(sem("ml_m0"), 16)
                    V.do(tt(MO[:, 1:1 + DB], M0[:], LF[:, first], ALU.add))
                    V.do(tt(D0[:], LF[:], con("negreset", TOK, rows=4), ALU.add))
                    V.do(nc.vector.tensor_tensor_scan(BM[:], con("reset", TOK, rows=4), LF[:], 0.0, ALU.mult, ALU.add))
                    V.settle()
                    V.do(tt(D1[:, first], MO[:, 1:1 + DB], IG[:, first], ALU.max))
                    V.settle()
                    V.do(nc.vector.tensor_tensor_scan(MM[:], D0[:], D1[:], 0.0, ALU.add, ALU.max))
                    V.do(tt(CR[:], IG[:], BM[:], ALU.subtract))
                    V.settle()
                    V.do(tt(ER[:], BM[:], MM[:], ALU.subtract))
                    V.do(copy(MO[:, 0:1], MM[:, SEQ - 1:SEQ]))
                    V.do(copy(MO[:, 1:1 + DB], MM[:, SEQ + DS - 1:TOK:DS]))
                    V.settle()
                    def c64(ap, n):
                        return ap.rearrange("p (c t) -> p c t", t=CH if n != DB else DS)
                    V.do(copy(E2[:, 0:CH], ER[:, 0:CH]))
                    V.do(tt(c64(E2[:, CH:SEQ], 3), c64(ER[:, CH:SEQ], 3),
                            MM[:, CH - 1:SEQ - 1:CH].unsqueeze(2).to_broadcast([MH, NCH - 1, CH]), ALU.add))
                    V.do(tt(s8(E2[:, SEQ:TOK]), s8(ER[:, SEQ:TOK]), M0[:].unsqueeze(2).to_broadcast([MH, DB, DS]), ALU.add))
                    V.do(tt(c64(WJ[:, 0:SEQ], 4), c64(CR[:, 0:SEQ], 4),
                            ER[:, CH - 1:SEQ:CH].unsqueeze(2).to_broadcast([MH, NCH, CH]), ALU.add))
                    V.do(tt(s8(WJ[:, SEQ:TOK]), s8(CR[:, SEQ:TOK]), ER[:, SEQ + DS - 1:TOK:DS].unsqueeze(2).to_broadcast([MH, DB, DS]), ALU.add))
                    V.mark(sem("ml_m"))
                    yield
                    vec.wait_ge(sem("ml_xp"), 1)
                    n = CN - CONV + 1
                    for i in range(4):
                        V.do(ts(CV[:, i, 0:n], XP[:, i, 3:3 + n], pcol("conv_w", 12 + i), pcol("conv_b", i), ALU.mult, ALU.add))
                    for tap in (2, 1, 0):
                        V.settle()
                        for i in range(4):
                            V.do(stt(CV[:, i, 0:n], XP[:, i, tap:tap + n], pcol("conv_w", 4 * tap + i), CV[:, i, 0:n],
                                     ALU.mult, ALU.add))
                    V.do(copy(COV[:, :, 0], XP[:, :, SEQ:CW]))
                    for i in range(4):
                        V.do(copy(COV[:, i, 1:1 + DB], XP[:, i, CW:CN].rearrange("p (s t) -> p s t", t=CS)[:, :, DS:CS]))
                    V.mark(sem("ml_conv"))
                    yield
                    vec.wait_ge(sem("ml_qk"), 1)
                    V.do(ts(QK[:, 2:4], QK[:, 2:4], HD ** -0.5, None, ALU.mult))
                    V.mark(sem("ml_rows"))
                    yield
                    bank = fV.take()
                    V.do(copy(COLS[:, 0:2], bank[:, 0:16].rearrange("p (a b) -> p a b", b=8)))
                    V.do(copy(COLS[0:NS, 2], bank[0:NS, 16:24]), sem("bankV_free"))
                    for j in range(MP):
                        bank = fV.take()
                        V.do(copy(MPC[:, j, 0:NCH], bank[:, CH - 1:SEQ:CH]))
                        V.do(copy(MPC[:, j, NCH:NCH + DB], bank[:, SEQ + DS - 1:TOK:DS]))
                        V.do(tt(QW[:, j], bank[:, 0:TOK], QK[:, j], ALU.mult), sem("bankV_free"))
                    V.settle()
                    yield
                    for tau, t0, w in TAUS:
                        bank = fV.take()
                        neg = con("neg_p" if tau < 2 else "neg_s", CH, rows=w)
                        for h in range(MH):
                            V.do(stt(DW[0:w, h], bank[0:w, h * CH:(h + 1) * CH], COLS[0:w, tau, h:h + 1], neg, ALU.add, ALU.add),
                                 sem("bankV_free") if h == 3 else None)
                        V.mark(sem("ml_arg"))
                        bank = fV.take()
                        vec.wait_ge(sem("ml_dw"), tau + 1)
                        V.do(tt(ST[0:w, tau], bank[0:w, 0:MH * CH].rearrange("p (h t) -> p h t", t=CH), DW[0:w], ALU.mult),
                             sem("bankV_free"))
                        bank = fV.take()
                        V.settle()
                        V.do(tt(KW[0:w, tau].rearrange("p (h d) -> p h d", d=HD), bank[0:w, 0:MW].rearrange("p (h d) -> p h d", d=HD),
                                COLS[0:w, tau, 4:8].unsqueeze(2).to_broadcast([w, MH, HD]), ALU.mult), sem("bankV_free"))
                        yield
                    vec.wait_ge(sem("ml_c00"), 32)
                    V.do(copy(C0[:, :, :, HD:P].rearrange("p j s v -> p (j s) v"),
                              N0[:].rearrange("p j s -> p (j s)").unsqueeze(2).to_broadcast([P, MP * DB, HD])))
                    V.mark(sem("ml_c0"))
                    V.mark(sem("ml_state"))
                    for c in range(NCH):
                        bank = fV.take()
                        V.settle()
                        for j in range(MP):
                            V.do(stt(CP[:, c + 1, j], CP[:, c, j], MPC[:, j, c:c + 1], bank[:, j * P:(j + 1) * P], ALU.mult, ALU.add),
                                 sem("ml_state") if j == 1 else None)
                    V.settle()
                    V.do(copy(NO[:, :, 0:1], CP[:, NCH, :, HD:HD + 1]))
                    V.mark(sem("ml_prompt"))
                    yield
                    vec.wait_ge(sem("ml_emb"), 1)
                    for j in range(MP):
                        bank = fV.take()
                        V.do(stt(DD[:, j], bank[:, 0:TOK], -1.0, EMB[:, j], ALU.mult, ALU.max))
                        V.settle()
                        V.do(tt(DD[:, j], bank[:, 0:TOK], DD[:, j], ALU.max), sem("bankV_free"))
                        V.settle()
                        V.do(nc.vector.reciprocal(DD[:, j], DD[:, j]))
                        bank = fV.take()
                        V.settle()
                        V.do(tt(HT[:, j], bank[:, 0:TOK], DD[:, j], ALU.mult), sem("bankV_free"))
                        if j < MP - 1:
                            yield
                    V.mark(sem("ml_h"))
                    yield
                    for j in range(MP):
                        V.do(tt(C0[:, j, :, 0:HD + 1], C0[:, j, :, 0:HD + 1],
                                MPC[:, j, NCH:NCH + DB].unsqueeze(2).to_broadcast([P, DB, HD + 1]), ALU.mult))
                    V.settle()
                    for j in range(MP):
                        bank = fV.take()
                        V.do(tt(C0[:, j, :, 0:HD], bank[:].rearrange("p (s v) -> p s v", v=HD), C0[:, j, :, 0:HD], ALU.add), sem("bankV_free"))
                        bank = fV.take()
                        V.do(tt(NO[:, j, 1:1 + DB], bank[:, 0:DB], C0[:, j, :, HD], ALU.add), sem("bankV_free"))
                    V.mark(sem("ml_out"))
                    yield
                    for j in range(MP):
                        bank = fV.take()
                        V.do(tt(HT[:, j], HT[:, j], bank[:, 0:TOK], ALU.subtract), sem("bankV_free"))
                    V.mark(sem("ml_hc"))
                    yield
                    for j in range(MP):
                        bank = fV.take()
                        V.do(ts(DD[:, j], bank[:, 0:TOK], NORM_EPS, None, ALU.add), sem("bankV_free"))
                    V.mark(sem("ml_var"))
                    vec.wait_ge(sem("ml_sd"), 1)
                    V.do(tt(HT[:], HT[:], DD[:], ALU.mult))
                    vec.wait_ge(sem("ml_gate"), 1)
                    V.settle()
                    for j in range(MP):
                        V.do(stt(HT[:, j], HT[:, j], pcol("ml_g", j), PJ[:, T_MO + j], ALU.mult, ALU.mult))

                def ml_pool(pool, G):
                    pool.wait_ge(sem("ml_start"), 1)
                    G.do(nc.gpsimd.memset(VM[:, :, :, HD:P], 1.0), sem("ml_ones"))
                    pool.wait_ge(sem("ml_state"), 2)
                    for h in range(MH):
                        G.do(nc.gpsimd.tensor_tensor(VX[:, h], VM[0:NS, 2, h, 0:HD].unsqueeze(1).to_broadcast([NS, DB, HD]),
                                                     con("seqmask", DB, rows=NS).unsqueeze(2).to_broadcast([NS, DB, HD]), ALU.mult))
                    G.mark(sem("ml_vx"))

                def mix_act(act, A):
                    act.wait_ge(sem("heads_done"), 1)
                    act.wait_ge(sem("gl_zero"), 1)
                    A.do(nc.scalar.activation(XH[0:DV, RP:RP + GH], OT[0:DV], ACT.Copy), sem("mix_hi"))
                    A.do(nc.scalar.activation(XH[:, RP + GH:MIXT], HT[:], ACT.Copy), sem("mix_hi"))

                def mix_vec(vec, V):
                    V.mark(sem("heads_done"))
                    vec.wait_ge(sem("mix_hi"), 1)
                    V.do(nc.vector.tensor_tensor(XL[0:DV, RP:RP + GH], OT[0:DV], XH[0:DV, RP:RP + GH].bitcast(F32), ALU.subtract))
                    for h in range(GH):
                        V.mark(sem("mixed"))
                    vec.wait_ge(sem("mix_hi"), 2)
                    V.do(nc.vector.tensor_tensor(XL[:, RP + GH:MIXT], HT[:], XH[:, RP + GH:MIXT].bitcast(F32), ALU.subtract))
                    for j in range(MP):
                        V.mark(sem("mixed"))

                def mix_pool(pool, G):
                    rw_pool(pool, G)
                    gl_pool(pool, G)
                    ml_pool(pool, G)

                @block.sync
                def _(sp):
                    sp.dma_start(PAR[:], of_layer(par)).then_inc(sem("params"), 16)
                    sp.dma_start(W2[:], of_layer(w2)).then_inc(sem("params"), 16)
                    sp.dma_start(G2[:], of_layer(g2)).then_inc(sem("params"), 16)
                    sp.dma_start(whole(A2G[:]), of_layer(a2g)).then_inc(sem("params"), 16)
                    for n in range(NCHUNK):
                        if n == STARTS[ITEMS.index(("proj", RAW + 2))]:
                            sp.wait_ge(sem("proj_ready"), 1)
                            sp.dma_start(whole(SH[:]), of_layer(st_shift)).then_inc(sem("rw_shift"), 16)
                            sp.dma_start(ZS[:].rearrange("p j s v -> p (j s v)"), of_layer(st_rw)).then_inc(sem("rw_state"), 16)
                        if n == STARTS[ITEMS.index(("ml",))] + SPL:
                            rw_stores(sp)
                            mix_loads(sp)
                        if n == STARTS[ITEMS.index(("out",))] + SPL + RAW:
                            mix_stores(sp)
                        if n >= RAW:
                            sp.wait_ge(lo_done, n - RAW + 1)
                        sp.dma_start(whole(raw[:, n % RAW]),
                                     weights[at_layer, n].rearrange("l p a -> p (l a)")).then_inc(loaded[n % RAW], 16)

                @block.tensor
                def _(pe):
                    bV = Banks(pe, psV, sem("bankV_full"), sem("bankV_free"))
                    bA = Banks(pe, psA, sem("bankA_full"), sem("bankA_free"))
                    rt = RowTiles(pe, sem("row_tiles"))
                    mm = nc.tensor.matmul

                    def three(out, n, k, kt, first, last, hi, lo):
                        mm(out, whi[:, n % SPL, k], hi[:, kt], start=first, stop=False)
                        mm(out, whi[:, n % SPL, k], lo[:, kt], start=False, stop=False)
                        return mm(out, wlo[:, n % SPL, k], hi[:, kt], start=False, stop=last)

                    def ada(n, i, g, q):
                        if q == 0 and i + g:
                            pe.wait_ge(sem("mrow_done"), i * 6 + g)
                        pe.wait_ge(lo_done, n + 1)
                        h = whi[:, n % SPL].rearrange("p (k c) n -> p k (c n)", k=2)
                        l = wlo[:, n % SPL].rearrange("p (k c) n -> p k (c n)", k=2)
                        for k in range(2):
                            kt = 2 * q + k
                            mm(psC[:], CS_T[:, kt], h[:, k], start=(kt == 0), stop=False)
                            ins = mm(psC[:], CS_T[:, kt], l[:, k], start=False, stop=(kt == 7))
                        ins.then_inc(chunk_used, 1)

                    def fold(i, g):
                        pe.wait_ge(sem("mrow_done"), i * 6 + g + 1)
                        bank = bV.open()
                        for j in range(4):
                            ins = mm(bank[:, 9 * j:9 * j + 9], MR[:, g % 2, j * P:(j + 1) * P],
                                     con("fold", 9, rows=64), start=True, stop=True)
                        bV.close(ins)

                    def up(n0, s, f):
                        for q, ring, freed in ((0, bA, (sem("gate_done"), s * FT + f + 1)),
                                               (1, bV, (sem("hidden_done"), s * FT + f + 1))):
                            n = n0 + q
                            bank = ring.open()
                            pe.wait_ge(lo_done, n + 1)
                            for kt in range(DT):
                                if f == 0 and q == 0:
                                    pe.wait_ge(sem("x_split"), 2 * s * DT + kt + 1)
                                ins = three(bank[:, 0:TOK], n, kt, kt, kt == 0, kt == DT - 1, XH, XL)
                            ins.then_inc(chunk_used, 1)
                            ring.close(None, freed=freed)

                    def product(n0, kts, hi, lo, wait_for, z0):
                        for d in range(DT):
                            bank = bV.open()
                            for k in range(kts):
                                q = d * kts + k
                                if q % 8 == 0:
                                    pe.wait_ge(lo_done, n0 + q // 8 + 1)
                                if d == 0:
                                    wait_for(k)
                                ins = three(bank[:, 0:TOK], n0 + q // 8, q % 8, k, k == 0, k == kts - 1, hi, lo)
                                if q % 8 == 7:
                                    ins.then_inc(chunk_used, 1)
                            bV.close(None if product_end(d, kts)[0] else ins, freed=(sem("z_ready"), z0 + d + 1))

                    def norm(s):
                        bank = bV.open()
                        pe.wait_ge(sem("zsum_ready"), s + 1)
                        mm(bank[:, 0:TOK], con("mean1024", P), ZSUM[:], start=True, stop=False)
                        pe.wait_ge(sem("z_ready"), (s + 1) * DT)
                        ins = mm(bank[:, 0:TOK], con("mean1024", P), ZT[:, DT - 1], start=False, stop=True)
                        bV.close(ins)
                        bank = bV.open()
                        mm(bank[:, 0:TOK], con("mean1024", P), QSUM[:], start=True, stop=False)
                        pe.wait_ge(sem("sq_ready"), (s + 1) * DT)
                        ins = mm(bank[:, 0:TOK], con("mean1024", P), SQ[:, DT - 1], start=False, stop=True)
                        bV.close(ins)

                    pe.wait_ge(sem("params"), 64)
                    mixers = {"rw": rw_pe(pe, bV, bA, rt), "gl": gl_pe(pe, bV, bA, rt), "ml": ml_pe(pe, bV, bA, rt)}
                    for item, n0 in zip(ITEMS, STARTS):
                        kind = item[0]
                        if kind == "ada":
                            ada(n0, *item[1:])
                        elif kind == "fold":
                            fold(*item[1:])
                        elif kind in mixers:
                            next(mixers[kind], None)
                        elif kind == "up":
                            up(n0, item[1], item[2])
                        elif kind == "down":
                            s = 2 * item[1]
                            product(n0, FT, HH, HL, lambda k, s=s: pe.wait_ge(sem("h_ready"), (s // 2) * FT + k + 1), s * DT)
                            norm(s)
                        elif kind == "proj":
                            t = item[1]
                            bank = bA.open()
                            pe.wait_ge(lo_done, n0 + 1)
                            for kt in range(DT):
                                if t == 0:
                                    pe.wait_ge(sem("x_split"), DT + kt + 1)
                                ins = three(bank[:, 0:TOK], n0, kt, kt, kt == 0, kt == DT - 1, XH, XL)
                            ins.then_inc(chunk_used, 1)
                            bA.close(None, freed=(sem("proj_ready"), t + 1))
                        elif kind == "mix":
                            pass
                        elif kind == "out":
                            product(n0, MIXT, XH, XL, lambda k: pe.wait_ge(sem("mixed"), k + 1), DT)
                            norm(1)

                @block.scalar
                def _(act):
                    A = Lane(act, sem("steps_act"))
                    fA = Filled(act, psA, sem("bankA_full"))
                    nsplit = [0]
                    activation = nc.scalar.activation

                    def split_to(m):
                        while nsplit[0] < min(m + 1, NCHUNK):
                            n = nsplit[0]
                            act.wait_ge(loaded[n % RAW], 16 * (n // RAW + 1))
                            if n >= SPL:
                                act.wait_ge(chunk_used, n - SPL + 1)
                            activation(whi[:, n % SPL], raw[:, n % RAW], ACT.Copy).then_inc(hi_done, 1)
                            nsplit[0] += 1

                    def modulate(s, after):
                        if s is not None:
                            act.wait_ge(sem("mods_ready"), s + 1)
                        for t in range(DT + 1):
                            if t < DT:
                                if after is not None:
                                    act.wait_ge(sem("zn_ready"), after * DT + t + 1)
                                    A.do(activation(XT[:, t], ZT[:, t], ACT.Identity,
                                                    scale=pcol("ln_g", after * DT + t),
                                                    bias=pcol("ln_b", after * DT + t)), sem("x_ready"))
                                    A.settle()
                                if s is not None:
                                    A.do(activation(XM[:, t, 0:SEQ], XT[:, t, 0:SEQ], ACT.Identity,
                                                    scale=scol(s, 1, t), bias=scol(s, 0, t)), sem("xm_prompt"))
                            if s is not None and t >= 1:
                                act.wait_ge(sem("xm_prompt"), s * DT + t)
                                act.wait_ge(sem("xm_sample"), s * DT + t)
                                A.do(activation(XH[:, t - 1], XM[:, t - 1], ACT.Copy), sem("xh_ready"))

                    def norm(n0, kts, s):
                        for d in range(DT):
                            split_to(n0 + ((d + 1) * kts - 1) // 8 + 2)
                            act.wait_ge(sem("z_ready"), s * DT + d + 1)
                            A.do(activation(SQ[:, d], ZT[:, d], ACT.Square), sem("sq_ready"))
                        act.wait_ge(sem("var_ready"), s + 1)
                        rsqrt(A, VR[:], sem("sd_ready"))
                        modulate(s + 1 if s < 2 else None, s)

                    act.wait_ge(sem("params"), 64)
                    mixers = {"rw": rw_act(act, A, fA), "gl": gl_act(act, A, fA), "ml": ml_act(act, A, fA)}
                    for item, n0 in zip(ITEMS, STARTS):
                        kind = item[0]
                        if kind == "ada":
                            split_to(n0 + 2)
                            if item[3] == 3:
                                act.wait_ge(chunk_used, n0 + 1)
                                A.do(activation(MR[:, item[2] % 2], psC[0:64, :], ACT.Copy), sem("mrow_done"))
                        elif kind == "fold":
                            if item[1:] == (0, 3):
                                modulate(0, None)
                        elif kind in mixers:
                            next(mixers[kind], None)
                        elif kind == "up":
                            u = item[1] * FT + item[2]
                            split_to(n0 + 2)
                            bank = fA.take((chunk_used, n0 + 1))
                            if u >= 2:
                                act.wait_ge(sem("hidden_done"), u - 1)
                            A.do(activation(SG[:, u % 2], bank[:, 0:TOK], ACT.Silu), sem("gate_done"))
                            split_to(n0 + 3)
                        elif kind == "down":
                            norm(n0, FT, 2 * item[1])
                        elif kind == "proj":
                            split_to(n0 + 2)
                            bank = fA.take((chunk_used, n0 + 1))
                            A.do(activation(PJ[:, item[1]], bank[:, 0:TOK], ACT.Copy), sem("proj_ready"))
                        elif kind == "mix":
                            split_to(n0 + 2)
                            mix_act(act, A)
                        elif kind == "out":
                            norm(n0, MIXT, 1)

                @block.vector
                def _(vec):
                    V = Lane(vec, sem("steps_vec"))
                    fV = Filled(vec, psV, sem("bankV_full"))
                    nsplit = [0]
                    tt, ts, stt = nc.vector.tensor_tensor, nc.vector.tensor_scalar, nc.vector.scalar_tensor_tensor

                    def split_to(m):
                        while nsplit[0] < min(m + 1, NCHUNK):
                            n = nsplit[0]
                            vec.wait_ge(hi_done, n + 1)
                            tt(wlo[:, n % SPL], raw[:, n % RAW], whi[:, n % SPL].bitcast(F32),
                               ALU.subtract).then_inc(lo_done, 1)
                            nsplit[0] += 1

                    def unfold(i, g):
                        bank = fV.take()
                        m = i * 24 + 4 * g
                        V.do(tt(MODS[:, m:m + 4], bank[:, 0:36].rearrange("p (a b) -> p a b", b=9),
                                PAR[:, PARC["ada_b"] + m:PARC["ada_b"] + m + 4].unsqueeze(2).to_broadcast([P, 4, 9]),
                                ALU.add), sem("bankV_free"))
                        if g == 3:
                            V.settle()
                            V.do(ts(MODS[:, i * 24 + 8:i * 24 + 16], MODS[:, i * 24 + 8:i * 24 + 16], 1.0, None, ALU.add))
                            V.mark(sem("mods_ready"))
                        if g == 5:
                            V.settle()
                            V.do(ts(MODS[:, i * 24 + 16:i * 24 + 24], MODS[:, i * 24 + 16:i * 24 + 24], 1.0,
                                    (1.0 if i == 1 else 0.5) / ALPHA, ALU.add, ALU.mult))
                            V.settle()

                    def by_sample(ap):
                        return ap.unsqueeze(2).to_broadcast([P, DB, DS])

                    def modulate(s, after):
                        for t in range(DT + 2):
                            if t < DT and after is not None:
                                V.do(tt(ZT[:, t], ZT[:, t], MN[:], ALU.subtract))
                                V.settle()
                                V.do(tt(ZT[:, t], ZT[:, t], VR[:], ALU.mult), sem("zn_ready"))
                            if s is not None and 1 <= t <= DT:
                                u = t - 1
                                if after is not None:
                                    vec.wait_ge(sem("x_ready"), after * DT + u + 1)
                                V.do(tt(s8(gtmp[:, u % 2]), s8(XT[:, u, SEQ:TOK]), by_sample(scol(s, 1, u, 1, DB)), ALU.mult))
                                V.settle()
                                V.do(tt(s8(XM[:, u, SEQ:TOK]), s8(gtmp[:, u % 2]), by_sample(scol(s, 0, u, 1, DB)), ALU.add),
                                     sem("xm_sample"))
                            if s is not None and t >= 2:
                                u = t - 2
                                vec.wait_ge(sem("xh_ready"), s * DT + u + 1)
                                V.do(tt(XL[:, u], XM[:, u], XH[:, u].bitcast(F32), ALU.subtract), sem("x_split"))

                    def norm(n0, kts, s):
                        for d in range(DT):
                            m = n0 + ((d + 1) * kts - 1) // 8
                            split_to(m + 2)
                            at_end, c = product_end(d, kts)
                            bank = fV.take((chunk_used, n0 + c) if at_end else None)
                            V.do(tt(s8(gtmp[:, d % 2]), s8(bank[:, SEQ:TOK]), by_sample(scol(s, 2, d, 1, DB)), ALU.mult))
                            V.do(stt(ZT[:, d, 0:SEQ], bank[:, 0:SEQ], scol(s, 2, d), XT[:, d, 0:SEQ], ALU.mult, ALU.add))
                            V.settle()
                            V.do(tt(ZT[:, d, SEQ:TOK], gtmp[:, d % 2], XT[:, d, SEQ:TOK], ALU.add), sem("z_ready"))
                        bank = fV.take()
                        V.do(nc.vector.tensor_copy(MN[:], bank[:, 0:TOK]), sem("bankV_free"))
                        V.settle()
                        V.do(tt(VR[:], MN[:], MN[:], ALU.mult))
                        V.settle()
                        bank = fV.take()
                        V.do(tt(VR[:], bank[:, 0:TOK], VR[:], ALU.subtract), sem("bankV_free"))
                        V.settle()
                        V.do(ts(VR[:], VR[:], 0.0, LN_EPS / ALPHA ** 2, ALU.max, ALU.add), sem("var_ready"))
                        vec.wait_ge(sem("sd_ready"), s + 1)
                        modulate(s + 1 if s < 2 else None, s)

                    vec.wait_ge(sem("params"), 64)
                    mixers = {"rw": rw_vec(vec, V, fV), "gl": gl_vec(vec, V, fV), "ml": ml_vec(vec, V, fV)}
                    for item, n0 in zip(ITEMS, STARTS):
                        kind = item[0]
                        if kind == "ada":
                            split_to(n0 + 2)
                        elif kind == "fold":
                            unfold(*item[1:])
                            if item[1:] == (0, 3):
                                modulate(0, None)
                        elif kind in mixers:
                            next(mixers[kind], None)
                        elif kind == "up":
                            u = item[1] * FT + item[2]
                            split_to(n0 + 3)
                            bank = fV.take((chunk_used, n0 + 2))
                            vec.wait_ge(sem("gate_done"), u + 1)
                            V.do(tt(HF[:, u % 2], SG[:, u % 2], bank[:, 0:TOK], ALU.mult), sem("hidden_done"))
                            V.settle()
                            V.do(nc.vector.tensor_copy(HH[:, item[2]], HF[:, u % 2]))
                            V.settle()
                            V.do(tt(HL[:, item[2]], HF[:, u % 2], HH[:, item[2]].bitcast(F32), ALU.subtract), sem("h_ready"))
                        elif kind == "down":
                            norm(n0, FT, 2 * item[1])
                        elif kind == "proj":
                            split_to(n0 + 2)
                        elif kind == "mix":
                            split_to(n0 + 2)
                            mix_vec(vec, V)
                        elif kind == "out":
                            vec.wait_ge(sem("stored"), 160)
                            norm(n0, MIXT, 1)

                @block.gpsimd
                def _(pool):
                    G = Lane(pool, sem("steps_pool"))

                    def sums(s):
                        add = nc.gpsimd.tensor_tensor
                        for d in range(1, DT - 1):
                            pool.wait_ge(sem("z_ready"), s * DT + d + 1)
                            G.settle()
                            G.do(add(ZSUM[:], ZT[:, 0] if d == 1 else ZSUM[:], ZT[:, d], ALU.add))
                            pool.wait_ge(sem("sq_ready"), s * DT + d + 1)
                            G.do(add(QSUM[:], SQ[:, 0] if d == 1 else QSUM[:], SQ[:, d], ALU.add))
                        G.mark(sem("zsum_ready"))

                    sums(0)
                    mix_pool(pool, G)
                    sums(1)
                    sums(2)
            numbers = [s.num for s in sems.values()]
            nc.all_engine_barrier(sems_to_clear=range(min(numbers), max(numbers) + 1))

        with nc.Block() as block:
            @block.sync
            def _(sp):
                sp.dma_start(yT, whole(XT[:])).then_inc(sem("stored"), 16)
                sp.wait_ge(sem("stored"), 16)


def _columns(v, rows=P):
    return np.ascontiguousarray(v.reshape(-1, rows).T)


def _spaced(v, heads, width, pitch):
    out = np.zeros(v.shape[:-1] + (heads, pitch), v.dtype)
    out[..., :width] = v.reshape(v.shape[:-1] + (heads, width))
    return out.reshape(v.shape[:-1] + (heads * pitch,))


def _weight_stream(a):
    out = np.zeros((DEPTH, NCHUNK, P, 8, P), np.float32)
    for l in range(DEPTH):
        ada = a["ada_w"][l].reshape(8, P, 18, 512)
        w_in = a["w_in"][l]
        g0, m0 = RW_PROJ, RW_PROJ + GLA_PROJ
        win = np.zeros((D, NPROJ * P), np.float32)

        def put(tile, part):
            win[:, tile * P:tile * P + part.shape[1]] = part

        put(0, w_in[:, 0:RW_PROJ])
        put(T_GQ, _spaced(w_in[:, g0:g0 + GQK], GH, DK, 64))
        put(T_GK, _spaced(w_in[:, g0 + GQK:g0 + 2 * GQK], GH, DK, 64))
        put(T_GV, w_in[:, g0 + 2 * GQK:g0 + 2 * GQK + GW])
        low = g0 + 2 * GQK + GW
        put(T_LOW, w_in[:, low:low + 16])
        win[:, T_LOW * P + 32:T_LOW * P + 36] = w_in[:, m0 + 4 * MW:m0 + 4 * MW + 4]
        win[:, T_LOW * P + 64:T_LOW * P + 68] = w_in[:, m0 + 4 * MW + 4:m0 + 4 * MW + 8]
        put(T_GR, _spaced(w_in[:, low + 16:low + 16 + GW], GH, DV, P))
        put(T_MQK, w_in[:, m0:m0 + 4 * MW])
        w_out = a["w_out"][l]
        wout = np.zeros((MIXT * P, D), np.float32)
        wout[0:RW_W] = w_out[0:RW_W]
        wout[RW_W:RW_W + GH * P] = _spaced(w_out[RW_W:RW_W + GW].T, GH, DV, P).T
        wout[RW_W + GH * P:] = w_out[RW_W + GW:]
        ff = {}
        for s in range(2):
            for name in ("ffn_wg", "ffn_wu"):
                t = np.zeros((D, FT * P), np.float32)
                t[:, :FF] = a[name][l, s]
                ff[name, s] = t
            t = np.zeros((FT * P, D), np.float32)
            t[:FF] = a["ffn_wd"][l, s]
            ff["ffn_wd", s] = t

        def columns(w, tile):
            return w[:, tile * P:(tile + 1) * P].reshape(8, P, P).transpose(1, 0, 2)

        def by_output(w):
            k = w.shape[0] // P
            t = w.reshape(k, P, DT, P).transpose(2, 0, 1, 3).reshape(DT * k // 8, 8, P, P)
            return t.transpose(0, 2, 1, 3)

        for item, n in zip(ITEMS, chunk_starts()):
            if item[0] == "ada":
                _, i, g, q = item
                out[l, n] = ada[2 * q:2 * q + 2, :, i * 6 + g].transpose(1, 0, 2).reshape(P, 8, P)
            elif item[0] == "up":
                out[l, n] = columns(ff["ffn_wg", item[1]], item[2])
                out[l, n + 1] = columns(ff["ffn_wu", item[1]], item[2])
            elif item[0] == "down":
                out[l, n:n + DT * FT // 8] = by_output(ff["ffn_wd", item[1]])
            elif item[0] == "proj":
                out[l, n] = columns(win, item[1])
            elif item[0] == "out":
                out[l, n:n + DT * MIXT // 8] = by_output(wout)
    return out.reshape(DEPTH, NCHUNK, P, 8 * P)


def _parameters(a):
    out = np.zeros((DEPTH, P, NPAR), np.float32)
    for l in range(DEPTH):
        def put(name, cols, row=0):
            out[l, row:row + cols.shape[0], PARC[name]:PARC[name] + cols.shape[1]] = cols

        for name, src in (("ln_g", "ln_g"), ("ln_b", "ln_b"), ("ada_b", "ada_b"), ("mu", "rw_mu"), ("w0", "rw_w0"),
                          ("a0", "rw_a0"), ("k_k", "rw_k_k"), ("k_a", "rw_k_a"), ("r_k", "rw_r_k"),
                          ("gn_g", "rw_gn_g"), ("gn_b", "rw_gn_b"), ("conv_w", "ml_conv_w"), ("conv_b", "ml_conv_b"),
                          ("ml_g", "ml_gn_g")):
            put(name, _columns(a[src][l]))
        put("gla_b", _columns(_spaced(a["gla_a_b"][l], GH, DK, 64)))
        put("gla_g", _columns(a["gla_gn_g"][l], DV))
        put("i_b", a["ml_i_b"][l][:, None], 32)
        put("f_b", a["ml_f_b"][l][:, None], 64)
    return out


def _constants():
    c = np.zeros((P, NCONST), np.float32)

    def put(name, m, at=0):
        c[:m.shape[0], CC[name] + at:CC[name] + at + m.shape[1]] = m

    i = np.arange(P)
    a, b = i[:, None], i[None, :]
    put("ident", np.eye(P, dtype=np.float32))
    put("ones64", (a // 64 == b // 64) / 64.0)
    put("mean1024", np.full((P, P), 1.0 / D))
    put("ones96", np.full((DV, P), 1.0 / DV))
    a, b = i[:, None] % CH, i[None, :CH]
    put("ident64", a == b)
    put("mask_p", a < b)
    put("mask_p", a <= b, CH)
    u, v = a[:NS], b
    put("mask_s", (u // DS == v // DS) * (u < v))
    put("mask_s", (u // DS == v // DS) * (u <= v), NS)
    for n in range(6):
        m = (a >> (n + 1) == b >> (n + 1)) * ((a >> n) % 2 == 1) * ((b >> n) % 2 == 0)
        put("level", m, n * CH)
        if n == 0:
            put("level0t", (b >> 1 == a >> 1) * (b % 2 == 1) * (a % 2 == 0))
    put("neg_p", np.where(a <= b, 0.0, -1e30))
    put("neg_s", np.where((u // DS == v // DS) & (u <= v), 0.0, -1e30))
    put("seqmask", np.arange(NS)[:, None] // DS == np.arange(DB)[None])
    t = np.arange(TOK)
    first = np.where(t < SEQ, t % CH == 0, t % DS == 0)
    put("reset", np.tile(1.0 - first, (P, 1)))
    put("negreset", np.tile(np.where((t >= SEQ) & (t % DS == 0), -3e38, 0.0), (MH, 1)))
    f = np.arange(2 * P)
    put("pairsel", np.arange(MH)[:, None] == f[None] // 64)
    f = np.arange(MH * CH)
    put("headsel", np.arange(MH)[:, None] == f[None] // CH)
    fold = np.zeros((64, 9))
    fold[np.arange(9), np.arange(9)] = 1
    fold[32 + np.arange(9), np.arange(9)] = 1
    put("fold", fold)
    return c


def kernel(**inputs):
    import concourse.bacc as bacc
    from concourse.bass_utils import run_bass_kernel_spmd

    a = {k: np.asarray(v) for k, v in inputs.items()}
    L = DEPTH

    def flat(v):
        return np.ascontiguousarray(v).reshape(v.shape[0], v.shape[1], -1)

    tokens = np.concatenate([a["x_prompt"].reshape(SEQ, D), a["x_sample"].reshape(NS, D)])
    cond = np.concatenate([a["c_prompt"], a["c_sample"]])
    xT = np.ascontiguousarray(tokens.T.reshape(DT, P, TOK).transpose(1, 0, 2))
    cT = np.ascontiguousarray(cond.T.reshape(DT, P, 1 + DB).transpose(1, 0, 2))
    w2 = np.concatenate([a["rw_w2"], a["rw_a2"]], axis=1)
    a2g = _spaced(a["gla_a2"], GH, DK, 64)
    st_shift = flat(a["state_rwkv_shift"].reshape(L, DB, NRW, P).transpose(0, 3, 2, 1))
    st_rw = flat(a["state_rwkv"].reshape(L, DB, RP, 2, HD, HD).transpose(0, 3, 5, 2, 1, 4).reshape(L, P, -1))
    st_gla = np.zeros((L, 2, 64, GP, DB, DV), np.float32)
    st_gla[:, :, :DK] = a["state_gla"].reshape(L, DB, GP, 2, DK, DV).transpose(0, 3, 4, 2, 1, 5)
    st_gla = st_gla.reshape(L, P, -1)
    st_c = flat(a["state_mlstm_c"].reshape(L, DB, MP, 2, HD, HD).transpose(0, 3, 5, 2, 1, 4).reshape(L, P, -1))
    st_n = flat(a["state_mlstm_n"].reshape(L, DB, MP, 2, HD).transpose(0, 3, 4, 2, 1).reshape(L, P, -1))
    st_m = np.ascontiguousarray(a["state_mlstm_m"].transpose(0, 2, 1))
    st_conv = flat(a["state_mlstm_conv"].reshape(L, DB, CONV - 1, 4, P).transpose(0, 4, 3, 1, 2))

    arrays = {"xT": xT.reshape(P, -1), "cT": cT.reshape(P, -1), "weights": _weight_stream(a), "par": _parameters(a), "consts": _constants(),
              "w2": w2, "g2": a["rw_g2"], "a2g": a2g, "st_shift": st_shift, "st_rw": st_rw, "st_gla": st_gla,
              "st_c": st_c, "st_n": st_n, "st_m": st_m, "st_conv": st_conv}
    outs = {"yT": (P, DT * TOK), "o_rwp": (L, P, RP * HD), "o_rws": (L, P, RP * DB * HD), "o_shift": (L, P, NRW * (1 + DB)),
            "o_glap": (L, P, GP * DV), "o_glas": (L, P, GP * DB * DV), "o_cp": (L, P, MP * HD), "o_cs": (L, P, MP * DB * HD),
            "o_np": (L, P, MP * (1 + DB)), "o_m": (L, MH, 1 + DB), "o_conv": (L, P, 4 * (1 + DB) * (CONV - 1))}
    nc = bacc.Bacc("TRN2", target_bir_lowering=False, num_devices=1)
    args = {}
    feed = {}
    for name, v in arrays.items():
        v = np.ascontiguousarray(v)
        feed[name + "_dram"] = v
        args[name] = nc.dram_tensor(name + "_dram", v.shape, F32, kind="ExternalInput").ap()
    for name, shape in outs.items():
        args[name] = nc.dram_tensor(name + "_dram", shape, F32, kind="ExternalOutput").ap()
    hybrid_trunk(nc, **args)
    r = run_bass_kernel_spmd(nc, [feed], core_ids=[0]).results[0]
    o = {name: np.asarray(r[name + "_dram"]) for name in outs}

    y = o["yT"].reshape(P, DT, TOK).transpose(2, 1, 0).reshape(TOK, D)
    shift = o["o_shift"].reshape(L, P, NRW, 1 + DB).transpose(0, 3, 2, 1).reshape(L, 1 + DB, RW_PROJ)
    n = o["o_np"].reshape(L, 2, HD, MP, 1 + DB).transpose(0, 4, 3, 1, 2).reshape(L, 1 + DB, MH, HD)
    m = o["o_m"].transpose(0, 2, 1)
    conv = o["o_conv"].reshape(L, P, 4, 1 + DB, CONV - 1).transpose(0, 3, 4, 2, 1).reshape(L, 1 + DB, CONV - 1, 2 * MW)

    def heads(v, pairs, seqs, k, width, swap):
        v = v.reshape(L, 2, 64, pairs, seqs, width)[:, :, :k].transpose(0, 4, 3, 1, 2, 5).reshape(L, seqs, 2 * pairs, k, width)
        return np.ascontiguousarray(v.transpose(0, 1, 2, 4, 3) if swap else v)

    cc = np.ascontiguousarray
    return (cc(y[:SEQ].reshape(1, SEQ, D)), cc(y[SEQ:].reshape(DB, DS, D)),
            heads(o["o_rwp"], RP, 1, HD, HD, True), cc(shift[:, :1]), heads(o["o_glap"], GP, 1, DK, DV, False),
            heads(o["o_cp"], MP, 1, HD, HD, True), cc(n[:, :1]), cc(m[:, :1]), cc(conv[:, :1]),
            heads(o["o_rws"], RP, DB, HD, HD, True), cc(shift[:, 1:]), heads(o["o_glas"], GP, DB, DK, DV, False),
            heads(o["o_cs"], MP, DB, HD, HD, True), cc(n[:, 1:]), cc(m[:, 1:]), cc(conv[:, 1:]))
```
